# Optimizing a Trainium2 kernel written in Bass

```python
import jax, jax.numpy as jnp
from jax import lax
import numpy as np

D_MODEL = 1024
BATCH = 1
SEQ = 256
DEPTH = 1
DEC_BATCH = 1
DEC_SEQ = 32
PAST_LEN = 128

CHUNK = 64
D_MIX = D_MODEL
HGRN_WIDTH = D_MIX // 2
HGRN_KDIM = 128
HGRN_HEADS = HGRN_WIDTH // HGRN_KDIM
HGRN_VDIM = HGRN_WIDTH // HGRN_HEADS
CONV_CH = D_MIX - HGRN_WIDTH
CONV_WIDTH = 31
IN_COLS = 4 * HGRN_WIDTH + 2 * CONV_CH
N_EXPERTS = 32
TOP_K = 4
D_FF = D_MODEL
SWIGLU_LIMIT = 7.0
SWIGLU_ALPHA = 1.702
PLE_DIM = 256
MOE_BLOCK = 128
EPS = 1e-6

kernel_name = 'hybrid_hgrn2_conformer_moe_stream_step'

def _rmsnorm(x, g):
    x32 = x.astype(jnp.float32)
    y = x32 * lax.rsqrt(jnp.mean(x32 * x32, axis=-1, keepdims=True) + EPS)
    return y.astype(x.dtype) * g

def _layernorm(x, g, b):
    x32 = x.astype(jnp.float32)
    mu = jnp.mean(x32, axis=-1, keepdims=True)
    var = jnp.mean(jnp.square(x32 - mu), axis=-1, keepdims=True)
    return ((x32 - mu) * lax.rsqrt(var + EPS)).astype(x.dtype) * g + b

def _hgrn2_scan(q, logf, k, v, s0, chunk):
    bsz, t, h, _ = q.shape
    dv = v.shape[-1]
    n = t // chunk

    def to_chunks(a):
        return a.reshape(bsz, n, chunk, h, a.shape[-1]).transpose(1, 0, 3, 2, 4)

    causal = jnp.tril(jnp.ones((chunk, chunk), dtype=bool))[:, :, None]

    def step(s, xs):
        qc, gc, kc, vc = xs
        b = jnp.cumsum(gc, axis=2)
        decay = jnp.exp(jnp.where(causal, b[:, :, :, None, :] - b[:, :, None, :, :], -jnp.inf))
        scores = jnp.einsum('bhtk,bhsk,bhtsk->bhts', qc, kc, decay)
        o = jnp.einsum('bhts,bhsv->bhtv', scores, vc) + jnp.einsum('bhtk,bhkv->bhtv', qc * jnp.exp(b), s)
        b_last = b[:, :, -1:, :]
        s_new = jnp.exp(b_last[:, :, 0, :])[..., None] * s + jnp.einsum('bhsk,bhsv->bhkv', kc * jnp.exp(b_last - b), vc)
        return s_new, o

    s_fin, o = lax.scan(step, s0, (to_chunks(q), to_chunks(logf), to_chunks(k), to_chunks(v)))
    return o.transpose(1, 0, 3, 2, 4).reshape(bsz, t, h, dv), s_fin

def _moe(x2d, w_router, b_router, w_gate_up, b_gate_up, w_down, b_down):
    n_tok, d = x2d.shape
    logits = (x2d @ w_router + b_router).astype(jnp.float32)
    top_val, top_idx = lax.top_k(logits, TOP_K)
    gates = jax.nn.softmax(top_val, axis=-1).astype(x2d.dtype)
    n_assign = n_tok * TOP_K
    flat_e = top_idx.reshape(n_assign)
    order = jnp.argsort(flat_e)
    sorted_e = flat_e[order]
    tok = order // TOP_K
    counts = jnp.bincount(flat_e, length=N_EXPERTS)
    padded = ((counts + MOE_BLOCK - 1) // MOE_BLOCK) * MOE_BLOCK
    pad_end = jnp.cumsum(padded)
    pad_start = pad_end - padded
    grp_start = jnp.cumsum(counts) - counts
    dest = pad_start[sorted_e] + (jnp.arange(n_assign) - grp_start[sorted_e])
    n_blocks = -(-n_assign // MOE_BLOCK) + N_EXPERTS
    rows = n_blocks * MOE_BLOCK
    xs = jnp.zeros((rows, d), x2d.dtype).at[dest].set(x2d[tok])
    block_e = jnp.minimum(jnp.searchsorted(pad_end, jnp.arange(n_blocks) * MOE_BLOCK, side='right'), N_EXPERTS - 1)

    def expert_block(args):
        xb, e = args
        gu = xb @ w_gate_up[e] + b_gate_up[e]
        gate = jnp.minimum(gu[:, :D_FF], SWIGLU_LIMIT)
        up = jnp.clip(gu[:, D_FF:], -SWIGLU_LIMIT, SWIGLU_LIMIT)
        hid = (up + 1.0) * (gate * jax.nn.sigmoid(SWIGLU_ALPHA * gate))
        return hid @ w_down[e] + b_down[e]

    ys = lax.map(expert_block, (xs.reshape(n_blocks, MOE_BLOCK, d), block_e)).reshape(rows, d)
    w_sorted = gates.reshape(n_assign)[order]
    return jnp.zeros_like(x2d).at[tok].add(w_sorted[:, None] * ys[dest])

def _layer(x, pe, s0, conv_buf, chunk, lb, norm_mix, w_in, hgrn_norm, conv_w, conv_b, conv_ln_g, conv_ln_b,
           w_out, norm_ffn, w_router, b_router, w_gate_up, b_gate_up, w_down, b_down, w_ple, norm_ple, w_ple_gate):
    bsz, t, _ = x.shape
    h = _rmsnorm(x, norm_mix)
    proj = h @ w_in
    q, fz, inp, g, u_a, u_b = jnp.split(
        proj, [HGRN_WIDTH, 2 * HGRN_WIDTH, 3 * HGRN_WIDTH, 4 * HGRN_WIDTH, 4 * HGRN_WIDTH + CONV_CH], axis=-1)

    def heads(a):
        return a.astype(jnp.float32).reshape(bsz, t, HGRN_HEADS, -1)
    lb_h = lb.reshape(HGRN_HEADS, HGRN_KDIM)
    f = lb_h + (1.0 - lb_h) * jax.nn.sigmoid(heads(fz))
    o, s_new = _hgrn2_scan(heads(q), jnp.log(f), 1.0 - f, heads(inp), s0.astype(jnp.float32), chunk)
    o = _rmsnorm(o, hgrn_norm.reshape(HGRN_HEADS, HGRN_VDIM).astype(jnp.float32))
    o = o.reshape(bsz, t, HGRN_WIDTH).astype(x.dtype) * jax.nn.silu(g)

    u = u_a * jax.nn.sigmoid(u_b)
    upad = jnp.concatenate([conv_buf.astype(u.dtype), u], axis=1)
    c = lax.conv_general_dilated(upad, conv_w[:, None, :], window_strides=(1,), padding='VALID',
                                 dimension_numbers=('NWC', 'WIO', 'NWC'), feature_group_count=CONV_CH) + conv_b
    new_buf = upad[:, -(CONV_WIDTH - 1):]
    c = jax.nn.silu(_layernorm(c, conv_ln_g, conv_ln_b))

    x = x + jnp.concatenate([o, c], axis=-1) @ w_out
    x = x + _moe(_rmsnorm(x, norm_ffn).reshape(bsz * t, D_MODEL), w_router, b_router,
                 w_gate_up, b_gate_up, w_down, b_down).reshape(bsz, t, D_MODEL)
    x = x + jax.nn.sigmoid(_rmsnorm(x, norm_ple) @ w_ple_gate) * (pe @ w_ple)
    return x, s_new.astype(x.dtype), new_buf

def setup_inputs(seed: int = 0) -> dict:
    key = jax.random.key(seed)
    ks = jax.random.split(key, 32)
    f32 = jnp.float32

    def nrm(k, shape, scale):
        return jax.random.normal(k, shape, f32) * scale

    def gain(k, shape):
        return 1.0 + nrm(k, shape, 0.05)

    return {
        'x_prompt': nrm(ks[0], (BATCH, SEQ, D_MODEL), 1.0),
        'x_sample': nrm(ks[1], (DEC_BATCH, DEC_SEQ, D_MODEL), 1.0),
        'state_hgrn': nrm(ks[2], (DEPTH, DEC_BATCH, HGRN_HEADS, HGRN_KDIM, HGRN_VDIM), 0.5),
        'cache_conv': nrm(ks[3], (DEPTH, DEC_BATCH, CONV_WIDTH - 1, CONV_CH), 0.5),
        'p_prompt': nrm(ks[4], (DEPTH, BATCH, SEQ, PLE_DIM), 1.0),
        'p_sample': nrm(ks[5], (DEPTH, DEC_BATCH, DEC_SEQ, PLE_DIM), 1.0),
        'norm_mix': gain(ks[6], (DEPTH, D_MODEL)),
        'w_in': nrm(ks[7], (DEPTH, D_MODEL, IN_COLS), D_MODEL ** -0.5),
        'hgrn_lb_logits': nrm(ks[8], (DEPTH + 1, HGRN_WIDTH), 0.5),
        'hgrn_norm': gain(ks[9], (DEPTH, HGRN_WIDTH)),
        'conv_w': nrm(ks[10], (DEPTH, CONV_WIDTH, CONV_CH), CONV_WIDTH ** -0.5),
        'conv_b': nrm(ks[11], (DEPTH, CONV_CH), 0.01),
        'conv_ln_g': gain(ks[12], (DEPTH, CONV_CH)),
        'conv_ln_b': nrm(ks[13], (DEPTH, CONV_CH), 0.01),
        'w_out': nrm(ks[14], (DEPTH, D_MIX, D_MODEL), D_MIX ** -0.5),
        'norm_ffn': gain(ks[15], (DEPTH, D_MODEL)),
        'w_router': nrm(ks[16], (DEPTH, D_MODEL, N_EXPERTS), D_MODEL ** -0.5),
        'b_router': nrm(ks[17], (DEPTH, N_EXPERTS), 0.01),
        'w_gate_up': nrm(ks[18], (DEPTH, N_EXPERTS, D_MODEL, 2 * D_FF), D_MODEL ** -0.5),
        'b_gate_up': nrm(ks[19], (DEPTH, N_EXPERTS, 2 * D_FF), 0.01),
        'w_down': nrm(ks[20], (DEPTH, N_EXPERTS, D_FF, D_MODEL), D_FF ** -0.5),
        'b_down': nrm(ks[21], (DEPTH, N_EXPERTS, D_MODEL), 0.01),
        'w_ple': nrm(ks[22], (DEPTH, PLE_DIM, D_MODEL), PLE_DIM ** -0.5),
        'norm_ple': gain(ks[23], (DEPTH, D_MODEL)),
        'w_ple_gate': nrm(ks[24], (DEPTH, D_MODEL, D_MODEL), D_MODEL ** -0.5),
        'norm_final': gain(ks[25], (D_MODEL,)),
    }

def reference(x_prompt, x_sample, state_hgrn, cache_conv, p_prompt, p_sample, norm_mix, w_in, hgrn_lb_logits,
              hgrn_norm, conv_w, conv_b, conv_ln_g, conv_ln_b, w_out, norm_ffn, w_router, b_router, w_gate_up,
              b_gate_up, w_down, b_down, w_ple, norm_ple, w_ple_gate, norm_final):
    lb_all = jnp.cumsum(jax.nn.softmax(hgrn_lb_logits.astype(jnp.float32), axis=0), axis=0)
    bp = x_prompt.shape[0]
    s0_prompt = jnp.zeros((bp, HGRN_HEADS, HGRN_KDIM, HGRN_VDIM), jnp.float32)
    buf0_prompt = jnp.zeros((bp, CONV_WIDTH - 1, CONV_CH), x_prompt.dtype)
    sample_len = x_sample.shape[1]
    yp, ys = x_prompt, x_sample
    sp_list, cp_list, ss_list, cs_list = [], [], [], []
    for l in range(DEPTH):
        params = (norm_mix[l], w_in[l], hgrn_norm[l], conv_w[l], conv_b[l], conv_ln_g[l], conv_ln_b[l], w_out[l],
                  norm_ffn[l], w_router[l], b_router[l], w_gate_up[l], b_gate_up[l], w_down[l], b_down[l],
                  w_ple[l], norm_ple[l], w_ple_gate[l])
        yp, sp, cp = _layer(yp, p_prompt[l], s0_prompt, buf0_prompt, CHUNK, lb_all[l], *params)
        ys, ss, cs = _layer(ys, p_sample[l], state_hgrn[l], cache_conv[l], sample_len, lb_all[l], *params)
        sp_list.append(sp)
        cp_list.append(cp)
        ss_list.append(ss)
        cs_list.append(cs)
    y_prompt = _rmsnorm(yp, norm_final)
    y_sample = _rmsnorm(ys, norm_final)
    return (y_prompt, y_sample, jnp.stack(sp_list), jnp.stack(cp_list), jnp.stack(ss_list), jnp.stack(cs_list))


_drawn_inputs = setup_inputs


def setup_inputs(seed=0):
    import zlib

    import numpy as np

    out = dict(_drawn_inputs(seed))
    spreads = {}
    factors = {'b_gate_up': 8.0, 'b_down': 8.0, 'norm_ple': 7.537}
    for name, (base, spread) in spreads.items():
        noise = np.random.default_rng([zlib.crc32(name.encode()), seed]).standard_normal(out[name].shape)
        drawn = base * np.exp(spread * noise) if base else spread * noise
        out[name] = __import__('jax').numpy.asarray(drawn.astype(out[name].dtype))
    for name, factor in factors.items():
        out[name] = (out[name] * factor).astype(out[name].dtype)
    return out
```

```python
from contextlib import ExitStack

import numpy as np

import concourse.bass as bass
from concourse import mybir

ALU = mybir.AluOpType
ACT = mybir.ActivationFunctionType
F32 = mybir.dt.float32
BF16 = mybir.dt.bfloat16
I32 = mybir.dt.int32
U32 = mybir.dt.uint32
AX = mybir.AxisListType.X

P = 128
D = 1024
DC = D // P
NB = 3
SEQ, DEC = 256, 32
T = SEQ + DEC
ROWS = [P, P, DEC]
H, KD = 4, 128
W = H * KD
CW = 31
PAD = CW - 1
UP = PAD + SEQ + PAD + DEC
CV = UP - PAD
CH = 32
NCH = T // CH
HALVES = [16, 8, 4, 2, 1]
NLEV = len(HALVES) + 1
E = 32
TOPK = 4
SLOTS = 64
PAIRS = E // 2
OVER = 4
LIST = 24
MORE = SEQ * TOPK // SLOTS + DEC * TOPK // SLOTS
RING = 6
UNIT = 4096
LEAD = 9
PER = 12
EPS = 1e-6
LIMIT, ALPHA = 7.0, 1.702
TINY = 2.0 ** -64

C_ID, C_TRI, C_ONE, C_IOTA, C_MASK, C_EYE, C_OVER = 0, 128, 256, 384, 448, 640, 674
C_END = C_OVER + OVER * PAIRS
R_MIX, R_FFN, R_PLE, R_LB, R_CB, R_LG, R_LBI, R_END = 0, 8, 16, 24, 32, 36, 40, 44


def constants():
    c = np.zeros((P, C_END), np.float32)
    c[:, C_ID:C_ID + P] = np.eye(P)
    c[:, C_TRI:C_TRI + P] = np.triu(np.ones((P, P)), 1)
    c[:, C_ONE:C_ONE + P] = 1.0
    c[:, C_IOTA:C_IOTA + SLOTS] = np.arange(SLOTS)
    s = np.arange(P)[:, None] % CH
    t = np.arange(CH)[None, :]
    masks = [(s == t)]
    for m in HALVES:
        masks.append((s // (2 * m) == t // (2 * m)) & (s % (2 * m) < m) & (t % (2 * m) >= m))
    c[:, C_MASK:C_MASK + NLEV * CH] = np.concatenate(masks, 1)
    c[:96, C_EYE:C_EYE + E] = np.arange(96)[:, None] % E == np.arange(E)[None, :]
    c[:, C_OVER:] = OVER * PAIRS - np.arange(OVER * PAIRS)
    return c


class Own:

    def __init__(self, engine, semaphore):
        self.engine, self.semaphore, self.count = engine, semaphore, 0

    def inc(self, ins):
        ins.then_inc(self.semaphore, 1)
        self.count += 1
        return self.count

    def link(self, ins):
        self.engine.wait_ge(self.semaphore, self.inc(ins))


def convolve(eng, own, chunks, U, out, par):
    done = {}
    for w in range(CW):
        for cc in chunks:
            tap = par[:, R_END + w * H + cc:R_END + w * H + cc + 1]
            if w:
                own.engine.wait_ge(own.semaphore, done[cc])
            if w == 0:
                ins = eng.tensor_scalar(out[:, cc, :], U[:, cc, 0:CV], tap, par[:, R_CB + cc:R_CB + cc + 1],
                                        ALU.mult, ALU.add)
            elif w < CW - 1:
                ins = eng.scalar_tensor_tensor(out=out[:, cc, :], in0=U[:, cc, w:w + CV], scalar=tap,
                                               in1=out[:, cc, :], op0=ALU.mult, op1=ALU.add)
            else:
                eng.scalar_tensor_tensor(out=out[:, cc, 0:SEQ], in0=U[:, cc, w:w + SEQ], scalar=tap,
                                         in1=out[:, cc, 0:SEQ], op0=ALU.mult, op1=ALU.add)
                ins = eng.scalar_tensor_tensor(out=out[:, cc, SEQ:T], in0=U[:, cc, w + CV - DEC:w + CV],
                                               scalar=tap, in1=out[:, cc, CV - DEC:CV], op0=ALU.mult, op1=ALU.add)
            done[cc] = own.inc(ins)


def program(nc, a, o):
    with ExitStack() as ctx:
        def sb(name, cols, dt=F32):
            return ctx.enter_context(nc.sbuf_tensor(name, [P, cols], dt))

        def sem(name):
            return ctx.enter_context(nc.semaphore(name))

        ps = ctx.enter_context(nc.psum_tensor("ps", [P, 8, 512], F32))

        ring = sb("ring", RING * UNIT)
        cst = sb("cst", C_END)
        par = sb("par", R_END + CW * H)
        acc = sb("acc", NB * D)
        ple = sb("ple", NB * D)
        xs = sb("xs", 2 * 3 * D // 2)
        xs_s = sb("xs_s", D // 2)
        bias = sb("bias", D)
        small = sb("small", 960)
        tbl = sb("tbl", 32, I32)
        pT = sb("pT", 2 * T)
        row = sb("row", E)

        def cs(at, n, rows=P):
            return cst[0:rows, at:at + n]

        ident, tri, ones = cs(C_ID, P), cs(C_TRI, P), cs(C_ONE, P)
        used = [0]

        def sm(n):
            used[0] += n
            assert used[0] <= 960, used[0]
            return small[:, used[0] - n:used[0]]

        def blocks(x, b=NB):
            return x.rearrange("p (b n) -> p b n", b=b)

        lbt, oml, lb_m, lb_e = sm(H), sm(H), sm(H), sm(2 * H)
        dec = blocks(sm(H * NCH), H)
        ss, rstd, eps = sm(NB), sm(NB), sm(1)
        hss, hrs = sm(NB * H), sm(NB * H)
        lg, top, topf = blocks(sm(NB * E)), blocks(sm(NB * 8)), blocks(sm(NB * 8))
        topi = blocks(sm(NB * 8).bitcast(U32))
        wts, wsum, ntop = blocks(sm(NB * TOPK)), sm(NB), sm(NB)
        msk, gat, htmp = blocks(sm(NB * E)), blocks(sm(NB * E)), blocks(sm(NB * E))
        posm = blocks(sm(NB * (E + 2)))
        cnt, pmax, over = sm(E), sm(PAIRS), sm(OVER * PAIRS)
        lst, lblk, lcode = sm(LIST), sm(LIST), sm(LIST)
        cur, curg, curw = blocks(sm(NB * 2)), blocks(sm(NB * 2)), blocks(sm(NB * 2))

        ARENA = 15248
        arena = sb("arena", ARENA)
        at = [0]

        def ar(n):
            at[0] += n
            assert at[0] <= ARENA, at[0]
            return arena[:, at[0] - n:at[0]]

        hT = ar(DC * T).rearrange("p (c t) -> p c t", c=DC)
        mixT = hT
        qf, kf, cf = ar(H * T), ar(H * T), ar(H * T)
        U_flat = ar(H * UP)
        U = blocks(U_flat, H)
        cacc = blocks(ar(H * CV), H)
        Qd, Kd = ar(H * T), ar(H * T)
        KdT_flat = ar(NB * W)
        KdT = blocks(KdT_flat)
        og = KdT
        St = [ar(W), ar(W)]
        So = ar(W)
        lev = ar(H * T)
        tails = Kd[0:PAD, 0:2 * W]
        par_rows = cacc[:, 0, 0:2 * P]
        crow = Kd[0:PAD, 0:W]
        junk1 = arena[:, 8424:8424 + D]
        reset = KdT_flat[:, 0:H * T]
        csq = blocks(U_flat[:, 0:H * T], H)
        hgn, Ss = bias[:, 0:W], bias[:, W:2 * W]
        xn = blocks(ple[:, :])
        v, g = blocks(ple[:, 0:NB * W]), blocks(ple[:, NB * W:2 * NB * W])
        ple3, X2 = blocks(ple[:, :]), blocks(acc[:, :])
        lq, lk = xs[:, 0:H * T], xs[:, H * T:2 * H * T]
        osq = blocks(xs[:, 0:NB * W])
        pr = blocks(xs[:, 2 * H * T:2 * H * T + NB * 256])
        score = xs[:, 2 * H * T:2 * H * T + NB * H * CH].rearrange("p (b h t) -> p b h t", b=NB, h=H)
        stmp = xs[:, 2 * H * T + NB * H * CH:3072].rearrange("p (b h t) -> p b h t", b=NB, h=H)
        cmean, croot = xs[:, 1728:1728 + T], xs[:, 2016:2016 + T]
        xn2 = blocks(arena[:, DC * T:DC * T + NB * D])
        gatT = arena[:, DC * T + NB * D:DC * T + NB * D + T]
        bd = U_flat[0:E, 0:D]
        wr = U_flat[:, 1136:1136 + DC * E]
        braw, bres = lev[0:96, 0:D], cf[0:96, 0:D]
        mtmp = arena[0:DEC, 7152:7152 + D // 2].bitcast(BF16)
        h4 = lambda x: blocks(x, H)

        at2 = [DC * T + 3 * H * T + H * UP]

        def ex(n):
            at2[0] += n
            assert at2[0] <= ARENA, at2[0]
            return arena[:, at2[0] - n:at2[0]]

        gath = ex(D)
        xT = blocks(ex(D), DC)
        gbuf, sgm, ubuf = ex(D), ex(D), ex(D)
        hidT = blocks(ex(D), DC)
        ybuf = ex(D)
        gw = ex(T)
        selg = blocks(ex(NB * P))
        selb = blocks(ex(NB * P // 2).bitcast(BF16))
        oneh = ex(P // 2).bitcast(BF16)
        eye = cst[:, C_EYE:C_EYE + E + 2]
        xn3 = blocks(arena[:, 0:NB * D])
        h3T = blocks(arena[:, 7152:7152 + DC * T], DC)
        sg = xn3
        nfin = arena[:, 5664:5664 + D]
        junk3 = ubuf
        xsb = xs[:, :].bitcast(BF16).rearrange("p (b k n) -> p b k n", b=2, k=3)
        xssb = xs_s[:, :].bitcast(BF16)
        biasb = bias[:, :].bitcast(BF16)

        def pcol(at, n):
            return par[:, at:at + n]

        def by_token(at, n, t):
            return par[:, at:at + n].unsqueeze(2).broadcast_to([P, n, t])

        S = {n: sem(n) for n in (
            "cst_in", "x_in", "aux_in", "p_in", "raw_in", "bd_in", "nfin_in",
            "dve", "pool", "act",
            "par_mm", "par_ready", "sq", "nvar", "nsqrt", "xn_ready", "xt_mm", "ht_ready", "pt_mm", "pt_ready",
            "proj_mm", "ubsig_ready", "u_ready", "f_sig", "q_ready", "v_ready", "gsig_ready", "g_ready",
            "f_ready", "lnf_ready", "c_ready", "ec_ready", "ed_ready", "edx_ready", "qd_ready", "kd_ready",
            "lev_neg", "lev_exp", "lev_q", "lev_k", "lev_mm", "lev_done", "kdt_mm", "kdt_ready",
            "um_mm", "st_ready", "o_mm", "o_copied", "hvar", "hsqrt", "mixa_ready", "mixa_mm", "mixa_copied",
            "conv_ready", "mean_mm", "csq_ready", "var_mm", "cvar", "csqrt", "cn_ready",
            "csig_ready", "mixc_ready", "tail_mm", "tail_ready",
            "out_mm", "x2_ready", "pl_mm", "pl_ready", "xn2_ready", "xt2_mm", "h2_ready", "lg_mm", "top_ready",
            "wexp", "msk_ready", "pos_mm", "table_ready", "xs_h", "xs_r", "xs_m", "xs_l", "gT_mm", "gT_ready",
            "bd_mm", "bd_added", "bias_ready", "zero_ready",
            "unit_done", "oneh_ready", "sel_cur", "sel_ready", "selg_cur", "selg_ready", "gath_mm", "gath_ev",
            "xt3_mm", "xt_ev", "gate_ready", "sig_ready", "up_ready", "gs_ready", "hid_ready", "hidt_mm",
            "hidt_ev", "y_ev", "gw_mm", "gw_ev", "comb_mm", "comb_add",
            "xn3_ready", "x3t_mm", "h3_ready", "pg_mm", "pg_sig", "x4_ready", "y_ready", "out_done")}
        full = [sem(f"ring_full{i}") for i in range(RING)]

        def slot(u):
            return ring[:, (u % RING) * UNIT:(u % RING + 1) * UNIT]

        block = ctx.enter_context(nc.Block())
        outs = {n: o[i] for i, n in enumerate(("yp", "ys", "sp", "cp", "ss", "cs"))}
        GROUPS = [5, 4, 1, 0, 2, 3]
        PROJ_DONE = [4, 8, 12, 16, 19, 22]
        ROW_OF = [(a["x_prompt"], 0), (a["x_prompt"], P), (a["x_sample"], 0)]

        @block.sync
        def _(sp):
            sp.dma_start(cst[:, :], a["consts"]).then_inc(S["cst_in"], 16)
            at_row = 0
            rows = par_rows[:, 0:P]
            for name, n in (("norm_mix", 8), ("norm_ffn", 8), ("norm_ple", 8), ("hgrn_lb_logits", 8),
                            ("conv_b", 4), ("conv_ln_g", 4), ("conv_ln_b", 4)):
                sp.dma_start(rows[at_row:at_row + n, :],
                             a[name].rearrange("l (c p) -> (l c) p", p=P)).then_inc(S["cst_in"], 16)
                at_row += n
            sp.dma_start(par_rows[0:CW * H, P:2 * P],
                         a["conv_w"].rearrange("l w (c p) -> (l w c) p", p=P)).then_inc(S["cst_in"], 16)
            for b in range(NB):
                src, r = ROW_OF[b]
                sp.dma_start(X2[0:ROWS[b], b, :], src[0, r:r + ROWS[b], :]).then_inc(S["x_in"], 16)

            def w_in(u):
                sp.dma_start(slot(u).rearrange("p (c n) -> p c n", c=DC),
                             a["w_in"][0, :, GROUPS[u] * W:(GROUPS[u] + 1) * W].rearrange(
                                 "(c p) n -> p c n", p=P)).then_inc(full[u % RING], 16)

            for u in range(6):
                w_in(u)
            for n in range(2):
                u = 6 + n
                sp.wait_ge(S["proj_mm"], PROJ_DONE[u - RING])
                sp.dma_start(slot(u).rearrange("p (c n) -> p c n", c=DC),
                             a["w_out"][0, :, n * W:(n + 1) * W].rearrange("(c p) n -> p c n", p=P)
                             ).then_inc(full[u % RING], 16)
            sp.wait_ge(S["proj_mm"], PROJ_DONE[2])
            sp.dma_start(slot(8)[:, 0:2 * D].rearrange("p (c n) -> p c n", c=2),
                         a["w_ple"][0].rearrange("(c p) n -> p c n", p=P)).then_inc(full[8 % RING], 16)

            def expert_unit(j, pair2, k):
                dst = slot(LEAD + k).rearrange("p (e n) -> p e n", e=2)
                if k < 8:
                    src = a["w_gate_up"][0, bass.ds(pair2, 2), k * P:(k + 1) * P, :].rearrange("e p n -> p e n")
                else:
                    r = (k - 8) * 2 * P
                    src = a["w_down"][0, bass.ds(pair2, 2), r:r + 2 * P, :].rearrange(
                        "e (p c) n -> p e (c n)", c=2)
                sp.dma_start(dst, src).then_inc(full[(LEAD + k) % RING], 16)

            before = {0: ("proj_mm", PROJ_DONE[3]), 1: ("proj_mm", PROJ_DONE[4]), 2: ("proj_mm", PROJ_DONE[5]),
                      3: ("out_mm", 3), 4: ("out_mm", 6), 5: ("pl_mm", 6)}
            for k in range(PER):
                if k in before:
                    sp.wait_ge(S[before[k][0]], before[k][1])
                else:
                    sp.wait_ge(S["unit_done"], k - RING + 1)
                expert_unit(0, 0, k)
            with sp.Fori(1, PAIRS) as j:
                for k in range(PER):
                    sp.wait_ge(S["unit_done"], j * PER + (k - RING + 1))
                    expert_unit(j, j * 2, k)
            sp.wait_ge(S["table_ready"], 1)
            n_more = sp.value_load(tbl[0:1, 0:1], min_val=0, max_val=MORE)
            with sp.If(n_more > 0):
                with sp.Fori(0, n_more) as i:
                    pair2 = sp.value_load(tbl[0:1, bass.ds(i + 1, 1)], min_val=0, max_val=E - 2)
                    for k in range(PER):
                        sp.wait_ge(S["unit_done"], i * PER + (PAIRS * PER + k - RING + 1))
                        expert_unit(i + PAIRS, pair2, k)
            steps = n_more + PAIRS
            for n in range(2):
                sp.wait_ge(S["unit_done"], steps * PER + (n - RING + 1))
                sp.dma_start(slot(LEAD + n).rearrange("p (c n) -> p c n", c=DC),
                             a["w_ple_gate"][0, :, n * W:(n + 1) * W].rearrange("(c p) n -> p c n", p=P)
                             ).then_inc(full[(LEAD + n) % RING], 16)
            for b in range(NB):
                sp.wait_ge(S["y_ready"], b + 1)
                dst = outs["yp"][0, b * P:(b + 1) * P, :] if b < 2 else outs["ys"][0]
                sp.dma_start(dst, sg[0:ROWS[b], b, :]).then_inc(S["out_done"], 16)
            sp.wait_ge(S["out_done"], 16 * 7)

        @block.tensor
        def _(pe):
            mm, tr = nc.tensor.matmul, nc.tensor.transpose
            pe.wait_ge(S["cst_in"], 16 * 9)
            tr(ps[:, 0, 0:R_END], par_rows[0:R_END, 0:P], cs(C_ID, R_END, R_END))
            tr(ps[:, 0, 64:64 + CW * H], par_rows[0:CW * H, P:2 * P],
               cs(C_ID, CW * H, CW * H)).then_inc(S["par_mm"], 1)

            def to_columns(src, ready, done, first_bank):
                for b in range(NB):
                    n = ROWS[b]
                    pe.wait_ge(ready, b + 1)
                    for c in range(DC):
                        t = tr(ps[:, first_bank + 2 * b + c // 4, (c % 4) * n:(c % 4 + 1) * n],
                               src[0:n, b, c * P:(c + 1) * P], cs(C_ID, n, n))
                        if c % 4 == 3:
                            t.then_inc(done, 1)

            to_columns(xn, S["xn_ready"], S["xt_mm"], 2)
            pe.wait_ge(S["p_in"], 16 * NB)
            for c in range(2):
                for b in range(NB):
                    t = tr(ps[:, 1 - c, 192 * c + b * P:192 * c + b * P + ROWS[b]],
                           pr[0:ROWS[b], b, c * P:(c + 1) * P], cs(C_ID, ROWS[b], ROWS[b]))
            pe.wait_ge(S["aux_in"], 16 * 4)
            for cc in range(H):
                t = tr(ps[:, 1, T + cc * PAD:T + (cc + 1) * PAD], crow[:, cc * P:(cc + 1) * P], cs(C_ID, PAD, PAD))
            t.then_inc(S["pt_mm"], 1)

            def columns(u, bank0):
                w = slot(u).rearrange("p (c n) -> p c n", c=DC)
                pe.wait_ge(full[u], 16)
                for cc in range(4):
                    for k in range(DC):
                        t = mm(ps[:, bank0 + cc, 0:T], w[:, k, cc * P:(cc + 1) * P], hT[:, k, :],
                               start=(k == 0), stop=(k == DC - 1))
                    t.then_inc(S["proj_mm"], 1)

            def token_rows(src, w, banks, done):
                for b in range(NB):
                    for k in range(DC):
                        t = mm(ps[0:ROWS[b], banks[b], :], src[:, k, b * P:b * P + ROWS[b]], w[:, k, :],
                               start=(k == 0), stop=(k == DC - 1))
                    t.then_inc(done, 1)

            pe.wait_ge(S["ht_ready"], 6)
            pe.wait_ge(S["pt_ready"], 1)
            columns(0, 0)
            columns(1, 4)
            pe.wait_ge(S["ubsig_ready"], 4)
            columns(2, 0)
            pe.wait_ge(S["u_ready"], 4)
            columns(3, 4)
            pe.wait_ge(S["f_sig"], 4)
            pe.wait_ge(full[4], 16)
            token_rows(hT, slot(4).rearrange("p (c n) -> p c n", c=DC), (0, 1, 2), S["proj_mm"])
            pe.wait_ge(S["q_ready"], 4)
            pe.wait_ge(S["kd_ready"], 1)
            pe.wait_ge(S["v_ready"], NB)
            for b, bank in enumerate((3, 7, 0)):
                for h in range(H):
                    t = tr(ps[0:ROWS[b], bank, h * KD:(h + 1) * KD],
                           h4(Kd)[:, h, b * P:b * P + ROWS[b]], ident)
                t.then_inc(S["kdt_mm"], 1)
            pe.wait_ge(full[5], 16)
            token_rows(hT, slot(5).rearrange("p (c n) -> p c n", c=DC), (4, 5, 6), S["proj_mm"])

            def level(l):
                lqs, lks = (qf, kf) if l == 0 else (lq, lk)
                if l:
                    pe.wait_ge(S["lev_q"], l)
                    pe.wait_ge(S["lev_k"], l)
                if l >= 2:
                    pe.wait_ge(S["lev_done"], l - 1)
                out = ps[:, 1 + l % 2, 0:NB * H * CH].rearrange("p (b h t) -> p b h t", b=NB, h=H)
                for i in range(NCH):
                    b, j = divmod(i, 4)
                    for h in range(H):
                        t = mm(out[j * CH:(j + 1) * CH, b, h, :], h4(lks)[:, h, i * CH:(i + 1) * CH],
                               h4(lqs)[:, h, i * CH:(i + 1) * CH], start=True, stop=True,
                               tile_position=(0, j * CH))
                t.then_inc(S["lev_mm"], 1)

            for l in range(NLEV):
                level(l)

            pe.wait_ge(S["kdt_ready"], NB)
            pe.wait_ge(S["g_ready"], NB)
            pe.wait_ge(S["lev_done"], NLEV)
            pe.wait_ge(S["qd_ready"], 1)

            def update(i):
                b, j = divmod(i, 4)
                if i >= 2:
                    pe.wait_ge(S["st_ready"], i - 1)
                for h in range(H):
                    t = mm(ps[:, (3, 7)[i % 2], h * KD:(h + 1) * KD],
                           KdT[j * CH:(j + 1) * CH, b, h * KD:(h + 1) * KD],
                           v[j * CH:(j + 1) * CH, b, h * KD:(h + 1) * KD], start=True, stop=True)
                t.then_inc(S["um_mm"], 1)

            update(0)
            for i in range(NCH):
                b, j = divmod(i, 4)
                if i + 1 < NCH:
                    update(i + 1)
                oo = ps[:, 4 + b, :]
                if i > 0:
                    if i < NCH - 1:
                        pe.wait_ge(S["st_ready"], i)
                    state = St[i % 2] if i < NCH - 1 else Ss
                    for h in range(H):
                        mm(oo[j * CH:(j + 1) * CH, h * KD:(h + 1) * KD], h4(Qd)[:, h, i * CH:(i + 1) * CH],
                           state[:, h * KD:(h + 1) * KD], start=(h == 0), stop=False,
                           tile_position=(0, j * CH), skip_group_check=True)
                for h in range(H):
                    pm = score[j * CH:(j + 1) * CH, b, h, :]
                    t = mm(oo[j * CH:(j + 1) * CH, h * KD:(h + 1) * KD], pm,
                           v[j * CH:(j + 1) * CH, b, h * KD:(h + 1) * KD],
                           start=(i == 0 and h == 0), stop=True,
                           tile_position=(j * CH, j * CH), skip_group_check=True)
                t.then_inc(S["o_mm"], 1)

            pe.wait_ge(S["conv_ready"], 1)
            pe.wait_ge(S["st_ready"], NCH)
            for cc in range(H):
                t = mm(ps[:, 3, 0:T], ones, cacc[:, cc, 0:T], start=(cc == 0), stop=(cc == H - 1))
            t.then_inc(S["mean_mm"], 1)
            for s_, lo in enumerate((PAD + SEQ - PAD, UP - PAD)):
                for cc in range(H):
                    t = tr(ps[0:PAD, 1 + s_, cc * P:(cc + 1) * P], U[:, cc, lo:lo + PAD], ident)
            t.then_inc(S["tail_mm"], 1)
            pe.wait_ge(S["csq_ready"], 1)
            for cc in range(H):
                t = mm(ps[:, 7, 0:T], ones, csq[:, cc, :], start=(cc == 0), stop=(cc == H - 1))
            t.then_inc(S["var_mm"], 1)
            pe.wait_ge(S["tail_ready"], 2)
            for b in range(NB):
                n = ROWS[b]
                pe.wait_ge(S["mixa_ready"], 1)
                for c in range(4):
                    t = tr(ps[:, b, c * n:(c + 1) * n], og[0:n, b, c * P:(c + 1) * P], cs(C_ID, n, n))
                t.then_inc(S["mixa_mm"], 1)

            pe.wait_ge(S["mixa_copied"], NB)
            pe.wait_ge(S["mixc_ready"], H)
            pe.wait_ge(full[0], 32)
            token_rows(mixT, slot(6).rearrange("p (c n) -> p c n", c=DC), (4, 5, 6), S["out_mm"])
            pe.wait_ge(full[1], 32)
            token_rows(mixT, slot(7).rearrange("p (c n) -> p c n", c=DC), (0, 1, 2), S["out_mm"])
            pe.wait_ge(full[2], 32)
            wple = slot(8)[:, 0:2 * D].rearrange("p (c n) -> p c n", c=2)
            for i in range(6):
                b, n = i // 2, i % 2
                if i >= 2:
                    pe.wait_ge(S["pl_ready"], i - 1)
                for c in range(2):
                    t = mm(ps[0:ROWS[b], (3, 7)[n], :], pT[:, c * T + b * P:c * T + b * P + ROWS[b]],
                           wple[:, c, n * W:(n + 1) * W], start=(c == 0), stop=(c == 1))
                t.then_inc(S["pl_mm"], 1)

            pe.wait_ge(S["x2_ready"], 6)
            for b in range(NB):
                n = ROWS[b]
                pe.wait_ge(S["xn2_ready"], b + 1)
                for c in range(DC):
                    t = tr(ps[:, (0, 1, 2, 4, 5, 6)[2 * b + c // 4], (c % 4) * n:(c % 4 + 1) * n],
                           xn2[0:n, b, c * P:(c + 1) * P], cs(C_ID, n, n))
                    if c % 4 == 3:
                        t.then_inc(S["xt2_mm"], 1)
            pe.wait_ge(S["h2_ready"], 6)
            pe.wait_ge(S["bd_in"], 32)
            pe.wait_ge(S["pl_ready"], 6)
            for b in range(NB):
                n = ROWS[b]
                for k in range(DC):
                    mm(ps[0:n, 7, b * E:(b + 1) * E], hT[:, k, b * P:b * P + n], wr[:, k * E:(k + 1) * E],
                       start=(k == 0), stop=False)
                t = mm(ps[0:n, 7, b * E:(b + 1) * E], ones[0:1, 0:n], row[0:1, 0:E], start=False, stop=True)
            t.then_inc(S["lg_mm"], 1)
            pe.wait_ge(S["msk_ready"], 1)
            for b in range(NB):
                for b2 in range(b + 1):
                    mm(ps[:, 3, b * E:(b + 1) * E], tri if b2 == b else ones, msk[:, b2, :],
                       start=(b2 == 0), stop=(b2 == b))
            for b in range(NB):
                t = mm(ps[:, 3, NB * E:NB * E + E], ones, msk[:, b, :], start=(b == 0), stop=(b == NB - 1))
            t.then_inc(S["pos_mm"], 1)

            G, PP, QQ = 0, 4, 6

            def gather(j):
                pe.wait_ge(S["sel_ready"], j + 1)
                for n in range(2):
                    cols = slice(n * 512, (n + 1) * 512)
                    for b in range(2):
                        for k in range(3):
                            mm(ps[:, PP + n, :], selb[:, b, :], xsb[:, b, k, cols],
                               start=(b == 0 and k == 0), stop=False)
                    mm(ps[:, PP + n, :], selb[0:96, 2, :], xssb[0:96, cols],
                       start=False, stop=True).then_inc(S["gath_mm"], 1)

            def turn_tokens(j):
                for n in range(2):
                    pe.wait_ge(S["gath_ev"], j * 2 + (n + 1))
                    for c in range(4 * n, 4 * n + 4):
                        t = tr(ps[:, PP + n, (c % 4) * P:(c % 4 + 1) * P], gath[:, c * P:(c + 1) * P], ident)
                    t.then_inc(S["xt3_mm"], 1)

            pe.wait_ge(S["xs_l"], NB)
            gather(0)
            turn_tokens(0)
            for b in range(NB):
                t = tr(ps[0:E, 0, b * P:b * P + ROWS[b]], gat[0:ROWS[b], b, :], cs(C_ID, ROWS[b], ROWS[b]))
            t.then_inc(S["gT_mm"], 1)
            pe.wait_ge(S["gT_ready"], 1)
            for i in range(6):
                b, n = i // 2, i % 2
                if i >= 2:
                    pe.wait_ge(S["bd_added"], i - 1)
                mm(ps[0:ROWS[b], 1 + n, :], gatT[0:E, b * P:b * P + ROWS[b]],
                   bd[0:E, n * 512:(n + 1) * 512], start=True, stop=True).then_inc(S["bd_mm"], 1)
            pe.wait_ge(S["bd_added"], 6)
            pe.wait_ge(S["bias_ready"], 1)

            def combine(j):
                pe.wait_ge(S["gw_ev"], j + 1)
                pe.wait_ge(S["y_ev"], j * 2 + 2)
                for i in range(6):
                    b, n = i // 2, i % 2
                    if i >= 2:
                        pe.wait_ge(S["comb_add"], j * 6 + (i - 1))
                    mm(ps[0:ROWS[b], QQ + n, :], gw[:, b * P:b * P + ROWS[b]],
                       ybuf[:, n * 512:(n + 1) * 512], start=True, stop=True).then_inc(S["comb_mm"], 1)

            def step(j):
                pe.wait_ge(S["oneh_ready"], j + 1)
                pe.wait_ge(S["xt_ev"], j * 2 + 2)
                for n in range(4):
                    mm(ps[:, G + n, :], oneh[0:96, :], biasb[0:96, n * 512:(n + 1) * 512],
                       start=True, stop=False, skip_group_check=True)
                for k in range(8):
                    u = LEAD + k
                    pe.wait_ge(full[u % RING], j * (16 * PER // RING) + 16 * (u // RING + 1))
                    w = slot(u).rearrange("p (e n) -> p e n", e=2)
                    for n in range(4):
                        for e in range(2):
                            t = mm(ps[e * 64:e * 64 + 64, G + n, :], xT[:, k, e * 64:e * 64 + 64],
                                   w[:, e, n * 512:(n + 1) * 512], start=False, stop=(k == 7),
                                   tile_position=(0, e * 64), skip_group_check=True)
                    t.then_inc(S["unit_done"], 1)
                pe.wait_ge(S["y_ev"], j * 2 + 2)
                gather(j + 1)
                combine(j)
                turn_tokens(j + 1)
                pe.wait_ge(S["comb_add"], j * 6 + 6)
                for n in range(2):
                    pe.wait_ge(S["hid_ready"], j * 2 + (n + 1))
                    for c in range(4 * n, 4 * n + 4):
                        k, r = c // 2, c % 2
                        t = tr(ps[:, QQ + n, (c % 4) * P:(c % 4 + 1) * P],
                               ubuf[:, 256 * k + r:256 * k + r + 255:2], ident)
                    t.then_inc(S["hidt_mm"], 1)
                pe.wait_ge(S["xt_ev"], j * 2 + 4)
                pe.wait_ge(S["hidt_ev"], j * 2 + 2)
                for k in range(4):
                    u = LEAD + 8 + k
                    pe.wait_ge(full[u % RING], j * (16 * PER // RING) + 16 * (u // RING + 1))
                    w = slot(u).rearrange("p (e c n) -> p e c n", e=2, c=2)
                    for c in range(2):
                        for n in range(2):
                            for e in range(2):
                                t = mm(ps[e * 64:e * 64 + 64, PP + n, :], hidT[:, 2 * k + c, e * 64:e * 64 + 64],
                                       w[:, e, c, n * 512:(n + 1) * 512],
                                       start=(k == 0 and c == 0), stop=(k == 3 and c == 1),
                                       tile_position=(0, e * 64))
                    t.then_inc(S["unit_done"], 1)
                    if k == 1:
                        pe.wait_ge(S["selg_ready"], j + 1)
                        for b in range(NB):
                            t = tr(ps[:, QQ, b * P:b * P + ROWS[b]], selg[0:ROWS[b], b, :],
                                   cs(C_ID, ROWS[b], ROWS[b]))
                        t.then_inc(S["gw_mm"], 1)

            with pe.Fori(0, PAIRS) as j:
                step(j)
            pe.wait_ge(S["table_ready"], 1)
            n_more = pe.value_load(tbl[0:1, 0:1], min_val=0, max_val=MORE)
            with pe.If(n_more > 0):
                with pe.Fori(0, n_more) as i:
                    step(i + PAIRS)
            steps = n_more + PAIRS
            combine(steps)
            to_columns(xn3, S["xn3_ready"], S["x3t_mm"], 0)
            pe.wait_ge(S["h3_ready"], 6)
            for n in range(2):
                u = LEAD + n
                pe.wait_ge(full[u % RING], steps * (16 * PER // RING) + 16 * (u // RING + 1))
                pe.wait_ge(S["comb_add"], steps * 6 + 6)
                token_rows(h3T, slot(u).rearrange("p (c n) -> p c n", c=DC), ((5, 6, 7), (0, 1, 2))[n], S["pg_mm"])


        @block.scalar
        def _(act):
            fn, copy = nc.scalar.activation, nc.scalar.copy
            act.dma_start(crow, a["cache_conv"][0, 0]).then_inc(S["aux_in"], 16)
            act.dma_start(Ss.rearrange("p (h v) -> p h v", h=H),
                          a["state_hgrn"][0, 0].rearrange("h k v -> k h v")).then_inc(S["aux_in"], 16)
            act.dma_start(hgn, a["hgrn_norm"].broadcast_to([P, W])).then_inc(S["aux_in"], 16)
            act.dma_start(row[0:1, :], a["b_router"]).then_inc(S["aux_in"], 16)
            for b in range(NB):
                src = a["p_prompt"][0, 0, b * P:(b + 1) * P, :] if b < 2 else a["p_sample"][0, 0]
                act.dma_start(pr[0:ROWS[b], b, :], src).then_inc(S["p_in"], 16)

            def squares(n, junk, ready, at):
                act.wait_ge(ready, at)
                for b in range(NB):
                    if b or n:
                        act.wait_ge(S["sq"], NB * n + b)
                    fn(junk, X2[:, b, :], ACT.Square, accum_out=ss[:, b:b + 1]).then_inc(S["sq"], 1)
                act.wait_ge(S["nvar"], n + 1)
                fn(rstd, rstd, ACT.Sqrt).then_inc(S["nsqrt"], 1)

            act.wait_ge(S["x_in"], 16 * NB)
            act.wait_ge(S["cst_in"], 16 * 9)
            squares(0, junk1, S["zero_ready"], 1)
            act.wait_ge(S["dve"], 3)
            fn(lb_e, lb_e, ACT.Exp).then_inc(S["act"], 1)
            act.wait_ge(S["pt_mm"], 1)
            copy(pT[:, 0:T], ps[:, 1, 0:T])
            copy(pT[:, T:2 * T], ps[:, 0, 192:192 + T])
            copy(U[:, :, PAD + SEQ:PAD + SEQ + PAD],
                 ps[:, 1, T:T + H * PAD].rearrange("p (c t) -> p c t", c=H)).then_inc(S["pt_ready"], 1)
            for cc in range(H):
                act.wait_ge(S["proj_mm"], cc + 1)
                fn(h4(Qd)[:, cc, :], ps[:, cc, 0:T], ACT.Sigmoid).then_inc(S["ubsig_ready"], 1)
            for cc in range(H):
                act.wait_ge(S["proj_mm"], 8 + cc + 1)
                fn(h4(kf)[:, cc, :], ps[:, cc, 0:T], ACT.Sigmoid).then_inc(S["f_sig"], 1)
            act.wait_ge(S["f_ready"], 1)
            fn(lev, cf, ACT.Ln).then_inc(S["lnf_ready"], 1)
            act.wait_ge(S["c_ready"], 1)
            fn(Qd, cf, ACT.Exp).then_inc(S["ec_ready"], 1)
            act.wait_ge(S["ed_ready"], 1)
            fn(Kd, lev, ACT.Exp).then_inc(S["edx_ready"], 1)
            for cc in range(H):
                act.wait_ge(S["proj_mm"], 12 + cc + 1)
                copy(h4(qf)[:, cc, :], ps[:, 4 + cc, 0:T]).then_inc(S["q_ready"], 1)
            for b in range(NB):
                act.wait_ge(S["proj_mm"], 16 + b + 1)
                copy(v[0:ROWS[b], b, :], ps[0:ROWS[b], b, :]).then_inc(S["v_ready"], 1)
            for b, bank in enumerate((3, 7, 0)):
                act.wait_ge(S["kdt_mm"], b + 1)
                copy(KdT[0:ROWS[b], b, :], ps[0:ROWS[b], bank, :]).then_inc(S["kdt_ready"], 1)
            for b in range(NB):
                act.wait_ge(S["proj_mm"], 19 + b + 1)
                fn(g[0:ROWS[b], b, :], ps[0:ROWS[b], 4 + b, :], ACT.Sigmoid).then_inc(S["gsig_ready"], 1)
            for l in range(1, NLEV):
                act.wait_ge(S["lev_neg"], l)
                fn(lev, lev, ACT.Exp).then_inc(S["lev_exp"], 1)
            act.wait_ge(S["um_mm"], NCH)
            for b in range(NB):
                act.wait_ge(S["o_mm"], min(4 * b + 4, NCH))
                copy(og[0:ROWS[b], b, :], ps[0:ROWS[b], 4 + b, :]).then_inc(S["o_copied"], 1)
            act.wait_ge(S["tail_mm"], 1)
            for s_ in range(2):
                copy(tails[:, s_ * W:(s_ + 1) * W], ps[0:PAD, 1 + s_, :]).then_inc(S["tail_ready"], 1)
            act.wait_ge(S["tail_ready"], 2)
            act.dma_start(outs["cp"][0, 0], tails[:, 0:W]).then_inc(S["out_done"], 16)
            act.dma_start(outs["cs"][0, 0], tails[:, W:2 * W]).then_inc(S["out_done"], 16)
            act.wait_ge(S["st_ready"], NCH)
            act.dma_start(outs["sp"][0, 0].rearrange("h k v -> k h v"),
                          St[0].rearrange("p (h v) -> p h v", h=H)).then_inc(S["out_done"], 16)
            act.dma_start(outs["ss"][0, 0].rearrange("h k v -> k h v"),
                          So.rearrange("p (h v) -> p h v", h=H)).then_inc(S["out_done"], 16)
            act.wait_ge(S["cvar"], 1)
            fn(croot, croot, ACT.Sqrt).then_inc(S["csqrt"], 1)
            act.wait_ge(S["hvar"], 1)
            fn(hrs, hrs, ACT.Sqrt).then_inc(S["hsqrt"], 1)
            for cc in range(H):
                act.wait_ge(S["cn_ready"], cc + 1)
                fn(csq[:, cc, :], cacc[:, cc, 0:T], ACT.Sigmoid).then_inc(S["csig_ready"], 1)
            for b in range(NB):
                act.wait_ge(S["mixa_mm"], b + 1)
                n = ROWS[b]
                copy(mixT[:, 0:4, b * P:b * P + n],
                     ps[:, b, 0:4 * n].rearrange("p (c t) -> p c t", c=4)).then_inc(S["mixa_copied"], 1)
            act.wait_ge(S["mixc_ready"], H)
            act.dma_start(bd, a["b_down"][0]).then_inc(S["bd_in"], 16)
            act.dma_start(wr.rearrange("p (c e) -> p c e", c=DC),
                          a["w_router"][0].rearrange("(c p) e -> p c e", p=P)).then_inc(S["bd_in"], 16)
            for i in range(6):
                b, n = i // 2, i % 2
                act.wait_ge(S["pl_mm"], i + 1)
                copy(ple3[0:ROWS[b], b, n * 512:(n + 1) * 512],
                     ps[0:ROWS[b], (3, 7)[n], :]).then_inc(S["pl_ready"], 1)
            squares(1, KdT_flat[:, 0:D], S["x2_ready"], 6)
            for b in range(NB):
                act.wait_ge(S["xn2_ready"], b + 1)
                if b < 2:
                    copy(xsb[:, b, 0, :], xn2[:, b, :]).then_inc(S["xs_h"], 1)
                else:
                    copy(xssb[0:DEC, :], xn2[0:DEC, b, :]).then_inc(S["xs_h"], 1)
            act.wait_ge(S["top_ready"], 1)
            for b in range(NB):
                fn(wts[:, b, :], top[:, b, 0:TOPK], ACT.Exp, bias=ntop[:, b:b + 1],
                   accum_out=wsum[:, b:b + 1]).then_inc(S["wexp"], 1)
            for b in range(NB):
                act.wait_ge(S["xs_r"], b + 1)
                if b < 2:
                    copy(xsb[:, b, 1, :], xn2[:, b, :]).then_inc(S["xs_m"], 1)
                else:
                    copy(mtmp, xn2[0:DEC, b, :]).then_inc(S["xs_m"], 1)
            act.wait_ge(S["xs_m"], NB)
            copy(xssb[DEC:2 * DEC, :], mtmp)
            for b in range(NB):
                act.wait_ge(S["xs_r"], NB + b + 1)
                if b < 2:
                    copy(xsb[:, b, 2, :], xn2[:, b, :]).then_inc(S["xs_l"], 1)
                else:
                    copy(xssb[2 * DEC:3 * DEC, :], xn2[0:DEC, b, :]).then_inc(S["xs_l"], 1)
            def copy_gathered(j):
                for n in range(2):
                    act.wait_ge(S["gath_mm"], j * 2 + (n + 1))
                    copy(gath[:, n * 512:(n + 1) * 512], ps[:, 4 + n, :]).then_inc(S["gath_ev"], 1)

            copy_gathered(0)
            act.wait_ge(S["gT_mm"], 1)
            copy(gatT[0:E, :], ps[0:E, 0, 0:T]).then_inc(S["gT_ready"], 1)
            act.wait_ge(S["bd_added"], 6)
            act.dma_start(nfin, a["norm_final"].rearrange("(o n) -> o n", o=1).broadcast_to([P, D])
                          ).then_inc(S["nfin_in"], 16)

            def step(j):
                for n in range(2):
                    act.wait_ge(S["gate_ready"], j * 2 + (n + 1))
                    cols = slice(n * 512, (n + 1) * 512)
                    fn(sgm[:, cols], gbuf[:, cols], ACT.Sigmoid, scale=ALPHA).then_inc(S["sig_ready"], 1)
                copy_gathered(j + 1)
                for n in range(2):
                    act.wait_ge(S["hidt_mm"], j * 2 + (n + 1))
                    copy(hidT[:, 4 * n:4 * n + 4, :],
                         ps[:, 6 + n, :].rearrange("p (c s) -> p c s", c=4)).then_inc(S["hidt_ev"], 1)
                act.wait_ge(S["unit_done"], j * PER + PER)
                for n in range(2):
                    copy(ybuf[:, n * 512:(n + 1) * 512], ps[:, 4 + n, :]).then_inc(S["y_ev"], 1)

            with act.Fori(0, PAIRS) as j:
                step(j)
            act.wait_ge(S["table_ready"], 1)
            n_more = act.value_load(tbl[0:1, 0:1], min_val=0, max_val=MORE)
            with act.If(n_more > 0):
                with act.Fori(0, n_more) as i:
                    step(i + PAIRS)
            steps = n_more + PAIRS
            squares(2, junk3, S["comb_add"], steps * 6 + 6)
            for i in range(6):
                n, b = divmod(i, NB)
                act.wait_ge(S["pg_mm"], i + 1)
                if i == 0:
                    act.wait_ge(S["x3t_mm"], 6)
                fn(sg[0:ROWS[b], b, n * 512:(n + 1) * 512], ps[0:ROWS[b], ((5, 6, 7), (0, 1, 2))[n][b], :],
                   ACT.Sigmoid).then_inc(S["pg_sig"], 1)
            squares(3, junk3, S["x4_ready"], 6)

        @block.gpsimd
        def _(pool):
            own = Own(pool, S["pool"])
            link = own.link
            for l in range(1, NLEV):
                pool.wait_ge(S["lev_exp"], l)
                if l >= 2:
                    pool.wait_ge(S["lev_mm"], l)
                nc.gpsimd.tensor_tensor(lk, kf, lev, ALU.mult).then_inc(S["lev_k"], 1)
            pool.wait_ge(S["mixa_ready"], 1)
            pool.wait_ge(S["st_ready"], NCH)
            pool.wait_ge(S["lev_done"], NLEV)
            pool.wait_ge(S["o_mm"], NCH)
            for n in range(2):
                cols = slice(n * D, (n + 1) * D)
                for r in range(3):
                    pool.dma_start(braw[r * E:(r + 1) * E, :], a["b_gate_up"][0, :, cols]).then_inc(S["raw_in"], 16)
                pool.wait_ge(S["raw_in"], 48 * (n + 1))
                link(nc.gpsimd.tensor_copy(biasb[0:96, cols], braw))
                link(nc.gpsimd.tensor_tensor(bres, braw, biasb[0:96, cols], ALU.subtract))
                link(nc.gpsimd.tensor_copy(biasb[E:2 * E, cols], bres[E:2 * E, :]))
                link(nc.gpsimd.tensor_copy(biasb[2 * E:3 * E, cols], bres[2 * E:3 * E, :]))
                link(nc.gpsimd.tensor_tensor(bres[2 * E:3 * E, :], bres[2 * E:3 * E, :], biasb[2 * E:3 * E, cols],
                                             ALU.subtract))
                last = nc.gpsimd.tensor_copy(biasb[2 * E:3 * E, cols], bres[2 * E:3 * E, :])
                if n == 0:
                    link(last)
                else:
                    last.then_inc(S["bias_ready"], 1)

        @block.vector
        def _(dve):
            V = nc.vector
            own = Own(dve, S["dve"])
            link = own.link

            def zero_rest(x):
                V.memset(x[DEC:64], 0.0)
                return V.memset(x[64:P], 0.0)

            V.memset(msk, 0.0)
            V.memset(gat, 0.0)
            zero_rest(X2[:, 2, :]).then_inc(S["zero_ready"], 1)
            dve.wait_ge(S["par_mm"], 1)
            V.tensor_copy(par[:, 0:R_END], ps[:, 0, 0:R_END])
            link(V.tensor_copy(par[:, R_END:R_END + CW * H], ps[:, 0, 64:64 + CW * H]))
            link(V.tensor_tensor(lb_m, pcol(R_LB, H), pcol(R_LB + H, H), ALU.max))
            link(V.tensor_tensor(blocks(lb_e, 2), blocks(pcol(R_LB, 2 * H), 2),
                                 lb_m.unsqueeze(1).broadcast_to([P, 2, H]), ALU.subtract))

            def root_of_mean(n):
                dve.wait_ge(S["sq"], NB * (n + 1))
                V.tensor_scalar(rstd, ss, 1.0 / D, EPS, ALU.mult, ALU.add).then_inc(S["nvar"], 1)
                dve.wait_ge(S["nsqrt"], n + 1)
                link(V.reciprocal(rstd, rstd))

            root_of_mean(0)
            for b in range(NB):
                V.tensor_scalar(xn[:, b, :], X2[:, b, :], rstd[:, b:b + 1], None, ALU.mult
                                ).then_inc(S["xn_ready"], 1)
            dve.wait_ge(S["act"], 1)
            link(V.tensor_tensor(lb_m, lb_e[:, 0:H], lb_e[:, H:2 * H], ALU.add))
            link(V.reciprocal(lb_m, lb_m))
            link(V.tensor_tensor(lbt, lb_e[:, 0:H], lb_m, ALU.mult))
            V.tensor_scalar(oml, lbt, -1.0, 1.0, ALU.mult, ALU.add).then_inc(S["par_ready"], 1)

            def columns_with_gain(dst, done, ready, banks, gain):
                for b in range(NB):
                    for n in range(2):
                        t = ROWS[b]
                        dve.wait_ge(S[done], 2 * b + n + 1)
                        V.tensor_tensor(dst[:, 4 * n:4 * n + 4, b * P:b * P + t],
                                        ps[:, banks[2 * b + n], 0:4 * t].rearrange("p (c t) -> p c t", c=4),
                                        by_token(gain + 4 * n, 4, t), ALU.mult).then_inc(S[ready], 1)

            columns_with_gain(hT, "xt_mm", "ht_ready", (2, 3, 4, 5, 6, 7), R_MIX)
            V.memset(U[:, :, 0:PAD], 0.0)
            link(V.memset(reset, 1.0))
            link(V.memset(reset[:, 0:H * T:CH], 0.0))
            for cc in range(H):
                dve.wait_ge(S["ubsig_ready"], cc + 1)
                dve.wait_ge(S["proj_mm"], 4 + cc + 1)
                V.tensor_tensor(U[:, cc, PAD:PAD + SEQ], ps[:, 4 + cc, 0:SEQ], h4(Qd)[:, cc, 0:SEQ], ALU.mult)
                V.tensor_tensor(U[:, cc, UP - DEC:UP], ps[:, 4 + cc, SEQ:T], h4(Qd)[:, cc, SEQ:T], ALU.mult
                                ).then_inc(S["u_ready"], 1)
            dve.wait_ge(S["pt_ready"], 1)
            dve.wait_ge(S["u_ready"], H)
            convolve(V, own, range(H), U, cacc, par)
            dve.wait_ge(S["dve"], own.count)
            V.memset(eps, 0.0).then_inc(S["conv_ready"], 1)
            for cc in range(H):
                dve.wait_ge(S["f_sig"], cc + 1)
                ins = V.tensor_scalar(h4(kf)[:, cc, :], h4(kf)[:, cc, :], oml[:, cc:cc + 1], lbt[:, cc:cc + 1],
                                      ALU.mult, ALU.add)
            link(ins)
            V.tensor_scalar(cf, kf, TINY, None, ALU.max).then_inc(S["f_ready"], 1)
            V.tensor_scalar(kf, kf, -1.0, 1.0, ALU.mult, ALU.add)
            dve.wait_ge(S["lnf_ready"], 1)
            V.tensor_tensor_scan(cf, reset, lev, 0.0, ALU.mult, ALU.add).then_inc(S["c_ready"], 1)
            dve.wait_ge(S["c_ready"], 1)
            by_chunk = cf.rearrange("p (i t) -> p i t", t=CH)
            V.tensor_tensor(lev.rearrange("p (i t) -> p i t", t=CH),
                            by_chunk[:, :, CH - 1:CH].broadcast_to([P, H * NCH, CH]), by_chunk, ALU.subtract
                            ).then_inc(S["ed_ready"], 1)
            dve.wait_ge(S["edx_ready"], 1)
            V.tensor_tensor(Kd, Kd, kf, ALU.mult).then_inc(S["kd_ready"], 1)
            dve.wait_ge(S["ec_ready"], 1)
            link(V.tensor_copy(dec, h4(Qd)[:, :, CH - 1:T:CH]))
            dve.wait_ge(S["q_ready"], H)
            V.tensor_tensor(Qd, Qd, qf, ALU.mult).then_inc(S["qd_ready"], 1)

            def masked(l):
                dve.wait_ge(S["lev_mm"], l + 1)
                if l:
                    dve.wait_ge(S["lev_done"], l)
                raw = ps[:, 1 + l % 2, 0:NB * H * CH].rearrange("p (b h t) -> p b h t", b=NB, h=H)
                mask = cs(C_MASK + l * CH, CH)
                for lo, n, rows in ((0, 2, P), (2, 1, DEC)):
                    dst = (score if l == 0 else stmp)[0:rows, lo:lo + n]
                    ins = V.tensor_tensor(dst, raw[0:rows, lo:lo + n],
                                          mask[0:rows].unsqueeze(1).unsqueeze(1).broadcast_to([rows, n, H, CH]),
                                          ALU.mult)
                if l == 0:
                    ins.then_inc(S["lev_done"], 1)
                    return
                link(ins)
                V.tensor_tensor(score[:, 0:2], score[:, 0:2], stmp[:, 0:2], ALU.add)
                V.tensor_tensor(score[0:DEC, 2], score[0:DEC, 2], stmp[0:DEC, 2], ALU.add
                                ).then_inc(S["lev_done"], 1)

            for l in range(1, NLEV):
                m = HALVES[l - 1]
                if l >= 2:
                    dve.wait_ge(S["lev_k"], l - 1)
                    dve.wait_ge(S["lev_q"], l - 1)
                view = cf.rearrange("p (i t) -> p i t", t=2 * m)
                link(V.tensor_tensor(lev.rearrange("p (i t) -> p i t", t=2 * m), view,
                                     view[:, :, m - 1:m].broadcast_to([P, H * T // (2 * m), 2 * m]),
                                     ALU.subtract))
                V.scalar_tensor_tensor(out=lev, in0=lev, scalar=-1.0, in1=lev, op0=ALU.mult, op1=ALU.min
                                       ).then_inc(S["lev_neg"], 1)
                if l == 3:
                    for b in range(NB):
                        n = ROWS[b]
                        dve.wait_ge(S["gsig_ready"], b + 1)
                        V.tensor_tensor(g[0:n, b, :], ps[0:n, 4 + b, :], g[0:n, b, :], ALU.mult
                                        ).then_inc(S["g_ready"], 1)
                dve.wait_ge(S["lev_exp"], l)
                if l >= 2:
                    dve.wait_ge(S["lev_mm"], l)
                V.tensor_tensor(lq, qf, lev, ALU.mult).then_inc(S["lev_q"], 1)
                masked(l - 1)
            masked(NLEV - 1)

            for i in range(NCH):
                last = i == NCH - 1
                old, new = (Ss, So) if last else (St[i % 2], St[(i + 1) % 2])
                up = ps[:, (3, 7)[i % 2], :]
                dve.wait_ge(S["um_mm"], i + 1)
                if i == 0:
                    V.tensor_copy(new, up).then_inc(S["st_ready"], 1)
                    continue
                if i >= 2:
                    dve.wait_ge(S["o_mm"], i)
                dve.wait_ge(S["st_ready"], i)
                for h in range(H):
                    hs = slice(h * KD, (h + 1) * KD)
                    ins = V.scalar_tensor_tensor(out=new[:, hs], in0=old[:, hs], scalar=dec[:, h, i:i + 1],
                                                 in1=up[:, hs], op0=ALU.mult, op1=ALU.add)
                ins.then_inc(S["st_ready"], 1)

            cv = cacc[:, :, 0:T]
            dve.wait_ge(S["mean_mm"], 1)
            link(V.tensor_scalar(cmean, ps[:, 3, 0:T], 1.0 / W, None, ALU.mult))
            link(V.tensor_tensor(cv, cv, cmean.unsqueeze(1).broadcast_to([P, H, T]), ALU.subtract))
            dve.wait_ge(S["tail_mm"], 1)
            V.tensor_tensor(csq, cv, cv, ALU.mult).then_inc(S["csq_ready"], 1)
            dve.wait_ge(S["o_copied"], NB)
            zero_rest(g[:, 2, :])
            link(zero_rest(og[:, 2, :]))
            link(V.tensor_tensor(osq, og, og, ALU.mult))
            heads = "p b (h n) -> p (b h) n"
            link(V.tensor_reduce(hss, osq.rearrange(heads, h=H), AX, ALU.add))
            V.tensor_scalar(hrs, hss, 1.0 / KD, EPS, ALU.mult, ALU.add).then_inc(S["hvar"], 1)
            dve.wait_ge(S["var_mm"], 1)
            V.tensor_scalar(croot, ps[:, 7, 0:T], 1.0 / W, EPS, ALU.mult, ALU.add).then_inc(S["cvar"], 1)
            dve.wait_ge(S["hsqrt"], 1)
            link(V.reciprocal(hrs, hrs))
            link(V.tensor_tensor(og.rearrange(heads, h=H), og.rearrange(heads, h=H),
                                 hrs.unsqueeze(2).broadcast_to([P, NB * H, KD]), ALU.mult))
            link(V.tensor_tensor(og, og, hgn.unsqueeze(1).broadcast_to([P, NB, W]), ALU.mult))
            V.tensor_tensor(og, og, g, ALU.mult).then_inc(S["mixa_ready"], 1)
            dve.wait_ge(S["csqrt"], 1)
            link(V.reciprocal(croot, croot))
            link(V.tensor_tensor(cv, cv, croot.unsqueeze(1).broadcast_to([P, H, T]), ALU.mult))
            for cc in range(H):
                V.tensor_scalar(cv[:, cc, :], cv[:, cc, :], pcol(R_LG + cc, 1), pcol(R_LBI + cc, 1),
                                ALU.mult, ALU.add).then_inc(S["cn_ready"], 1)
            for cc in range(H):
                dve.wait_ge(S["csig_ready"], cc + 1)
                V.tensor_tensor(mixT[:, 4 + cc, :], cv[:, cc, :], csq[:, cc, :], ALU.mult
                                ).then_inc(S["mixc_ready"], 1)

            for i in range(6):
                n, b = divmod(i, NB)
                x = X2[0:ROWS[b], b, n * 512:(n + 1) * 512]
                dve.wait_ge(S["out_mm"], i + 1)
                V.tensor_tensor(x, ps[0:ROWS[b], (4 + b, b)[n], :], x, ALU.add).then_inc(S["x2_ready"], 1)
            root_of_mean(1)
            dve.wait_ge(S["bias_ready"], 1)
            for b in range(NB):
                V.tensor_scalar(xn2[:, b, :], X2[:, b, :], rstd[:, b:b + 1], None, ALU.mult
                                ).then_inc(S["xn2_ready"], 1)
            columns_with_gain(hT, "xt2_mm", "h2_ready", (0, 1, 2, 4, 5, 6), R_FFN)

            zero_rest(lg[:, 2, :])
            dve.wait_ge(S["lg_mm"], 1)
            V.tensor_copy(lg[:, 0:2, :], ps[:, 7, 0:2 * E].rearrange("p (b e) -> p b e", b=2))
            link(V.tensor_copy(lg[0:DEC, 2, :], ps[0:DEC, 7, 2 * E:3 * E]))
            for b in range(NB):
                ins = V.max(top[:, b, :], lg[:, b, :])
            link(ins)
            V.tensor_scalar(ntop, top[:, :, 0], -1.0, None, ALU.mult).then_inc(S["top_ready"], 1)
            for b in range(NB):
                ins = V.max_index(topi[:, b, :], top[:, b, :], lg[:, b, :])
            link(ins)
            link(V.tensor_copy(topf, topi))
            dve.wait_ge(S["wexp"], NB)
            link(V.reciprocal(wsum, wsum))
            link(V.tensor_tensor(wts, wts, wsum.unsqueeze(2).broadcast_to([P, NB, TOPK]), ALU.mult))
            iota_e = cs(C_IOTA, E).unsqueeze(1).broadcast_to([P, NB, E])
            for k in range(TOPK):
                link(V.tensor_tensor(htmp, iota_e, topf[:, :, k:k + 1].broadcast_to([P, NB, E]), ALU.is_equal))
                link(V.tensor_tensor(msk, msk, htmp, ALU.add))
                link(V.tensor_tensor(htmp, htmp, wts[:, :, k:k + 1].broadcast_to([P, NB, E]), ALU.mult))
                link(V.tensor_tensor(gat, gat, htmp, ALU.add))
            zero_rest(gat[:, 2, :])
            zero_rest(msk[:, 2, :]).then_inc(S["msk_ready"], 1)

            def part(b, k):
                if b < 2:
                    return xn2[:, b, :], xsb[:, b, k, :]
                return xn2[0:DEC, b, :], (xssb[0:DEC, :], mtmp)[k]

            for k, had in enumerate(("xs_h", "xs_m")):
                for b in range(NB):
                    dve.wait_ge(S[had], b + 1)
                    r, p_ = part(b, k)
                    V.tensor_tensor(r, r, p_, ALU.subtract).then_inc(S["xs_r"], 1)
            dve.wait_ge(S["pos_mm"], 1)
            link(V.scalar_tensor_tensor(out=htmp, in0=ps[:, 3, 0:NB * E].rearrange("p (b e) -> p b e", b=NB),
                                        scalar=1.0, in1=msk, op0=ALU.add, op1=ALU.mult))
            link(V.tensor_scalar(posm[:, :, 0:E], htmp, -1.0, None, ALU.add))
            V.tensor_copy(posm[DEC:2 * DEC, 2, 0:E], posm[0:DEC, 2, 0:E])
            link(V.tensor_copy(posm[2 * DEC:3 * DEC, 2, 0:E], posm[0:DEC, 2, 0:E]))
            link(V.tensor_copy(cnt, ps[:, 3, NB * E:NB * E + E]))

            iota_s = cs(C_IOTA, SLOTS).unsqueeze(1).broadcast_to([P, NB * 2, SLOTS])

            def per_slot(x):
                return x.rearrange("p b e -> p (b e)").unsqueeze(2).broadcast_to([P, NB * 2, SLOTS])

            def columns_of(pair2, x):
                return x[:, :, bass.ds(pair2, 2)]

            def place(out, pair2, offset):
                if offset is None:
                    return V.tensor_copy(out, columns_of(pair2, posm))
                return V.tensor_scalar(out, columns_of(pair2, posm), offset, None, ALU.subtract)

            def select(j, pair2, offset):
                dve.wait_ge(S["gath_mm"], j * 2)
                place(cur, pair2, offset).then_inc(S["sel_cur"], 1)
                dve.wait_ge(S["sel_cur"], j + 1)
                V.tensor_tensor(selb.rearrange("p b (e s) -> p (b e) s", e=2), iota_s, per_slot(cur),
                                ALU.is_equal).then_inc(S["sel_ready"], 1)

            def select_bias(j, pair2):
                V.tensor_copy(oneh[0:96, :].rearrange("p (e s) -> p e s", e=2),
                              eye[0:96, bass.ds(pair2, 2)].unsqueeze(2).broadcast_to([96, 2, SLOTS])
                              ).then_inc(S["oneh_ready"], 1)

            def weigh(j, pair2, offset):
                place(curg, pair2, offset)
                V.tensor_copy(curw, columns_of(pair2, gat)).then_inc(S["selg_cur"], 1)
                dve.wait_ge(S["selg_cur"], j * 2 + 1)
                sel = selg.rearrange("p b (e s) -> p (b e) s", e=2)
                V.tensor_tensor(sel, iota_s, per_slot(curg), ALU.is_equal).then_inc(S["selg_cur"], 1)
                dve.wait_ge(S["selg_cur"], j * 2 + 2)
                V.tensor_tensor(sel, sel, per_slot(curw), ALU.mult).then_inc(S["selg_ready"], 1)

            def tokens_out(j):
                for n in range(2):
                    dve.wait_ge(S["xt3_mm"], j * 2 + (n + 1))
                    V.tensor_tensor(xT[:, 4 * n:4 * n + 4, :],
                                    ps[:, 4 + n, :].rearrange("p (c s) -> p c s", c=4),
                                    by_token(R_FFN + 4 * n, 4, P), ALU.mult).then_inc(S["xt_ev"], 1)

            dve.wait_ge(S["out_done"], 64)
            select(0, 0, None)
            select_bias(0, 0)
            tokens_out(0)
            V.memset(gw, 0.0).then_inc(S["gw_ev"], 1)
            V.memset(ybuf[:, 0:512], 0.0).then_inc(S["y_ev"], 1)
            V.memset(ybuf[:, 512:D], 0.0).then_inc(S["y_ev"], 1)
            for i in range(6):
                b, n = i // 2, i % 2
                x = X2[0:ROWS[b], b, n * 512:(n + 1) * 512]
                dve.wait_ge(S["bd_mm"], i + 1)
                V.tensor_tensor(x, ps[0:ROWS[b], 1 + n, :], x, ALU.add).then_inc(S["bd_added"], 1)

            link(V.tensor_tensor(pmax, cnt[:, 0:E:2], cnt[:, 1:E:2], ALU.max))
            for b in range(OVER):
                ins = V.tensor_scalar(over[:, b * PAIRS:(b + 1) * PAIRS], pmax, float(SLOTS * (b + 1)), None,
                                      ALU.is_gt)
            link(ins)
            link(V.tensor_reduce(lst[:, 0:1], over, AX, ALU.add))
            V.tensor_copy(tbl[:, 0:1], lst[:, 0:1])
            link(V.tensor_tensor(over, over, cs(C_OVER, OVER * PAIRS), ALU.mult))
            for r in range(LIST // 8):
                link(V.max(lst[:, 8 * r:8 * r + 8], over))
                if r < LIST // 8 - 1:
                    link(V.match_replace(over, lst[:, 8 * r:8 * r + 8], over, 0.0))
            link(V.tensor_scalar(lcode, lst, -1.0, float(OVER * PAIRS), ALU.mult, ALU.add))
            link(V.tensor_scalar(lblk, lcode, float(PAIRS), None, ALU.is_ge))
            for q in range(2, OVER + 1):
                link(V.scalar_tensor_tensor(out=lblk, in0=lcode, scalar=float(PAIRS * q), in1=lblk,
                                            op0=ALU.is_ge, op1=ALU.add))
            link(V.scalar_tensor_tensor(out=lcode, in0=lblk, scalar=-float(PAIRS), in1=lcode,
                                        op0=ALU.mult, op1=ALU.add))
            link(V.tensor_scalar(lblk, lblk, float(SLOTS), float(SLOTS), ALU.mult, ALU.add))
            V.tensor_scalar(tbl[:, 1:1 + LIST], lcode, 2.0, None, ALU.mult).then_inc(S["table_ready"], 1)
            dve.wait_ge(S["table_ready"], 1)
            first = dve.value_load(tbl[0:1, 1:2], min_val=0, max_val=E - 2)
            place(posm[:, :, E:E + 2], first, lblk[:, 0:1])
            link(V.tensor_copy(eye[0:96, E:E + 2], eye[0:96, bass.ds(first, 2)]))

            def step(j, this, following):
                select(j + 1, *following)
                dve.wait_ge(S["unit_done"], j * PER + 1)
                select_bias(j + 1, following[0])
                weigh(j, *this)
                dve.wait_ge(S["unit_done"], j * PER + 8)
                for n in range(2):
                    cols = slice(n * 512, (n + 1) * 512)
                    V.tensor_scalar(gbuf[:, cols], ps[:, n, :], LIMIT, None, ALU.min).then_inc(S["gate_ready"], 1)
                for n in range(2):
                    cols = slice(n * 512, (n + 1) * 512)
                    V.tensor_scalar(ubuf[:, cols], ps[:, 2 + n, :], LIMIT, -LIMIT, ALU.min, ALU.max
                                    ).then_inc(S["up_ready"], 1)
                for n in range(2):
                    cols = slice(n * 512, (n + 1) * 512)
                    dve.wait_ge(S["sig_ready"], j * 2 + (n + 1))
                    V.tensor_tensor(gbuf[:, cols], gbuf[:, cols], sgm[:, cols], ALU.mult).then_inc(S["gs_ready"], 1)
                for n in range(2):
                    cols = slice(n * 512, (n + 1) * 512)
                    dve.wait_ge(S["gs_ready"], j * 2 + (n + 1))
                    dve.wait_ge(S["up_ready"], j * 2 + (n + 1))
                    V.scalar_tensor_tensor(out=ubuf[:, cols], in0=ubuf[:, cols], scalar=1.0, in1=gbuf[:, cols],
                                           op0=ALU.add, op1=ALU.mult).then_inc(S["hid_ready"], 1)
                add_outputs(j)
                tokens_out(j + 1)
                dve.wait_ge(S["gw_mm"], j + 1)
                V.tensor_copy(gw, ps[:, 6, 0:T]).then_inc(S["gw_ev"], 1)

            def add_outputs(j):
                for i in range(6):
                    b, n = i // 2, i % 2
                    x = X2[0:ROWS[b], b, n * 512:(n + 1) * 512]
                    dve.wait_ge(S["comb_mm"], j * 6 + (i + 1))
                    V.tensor_tensor(x, ps[0:ROWS[b], 6 + n, :], x, ALU.add).then_inc(S["comb_add"], 1)

            with dve.Fori(0, PAIRS) as j:
                step(j, (j * 2, None), (j * 2 + 2, None))
            n_more = dve.value_load(tbl[0:1, 0:1], min_val=0, max_val=MORE)
            with dve.If(n_more > 0):
                with dve.Fori(0, n_more) as i:
                    now = dve.value_load(tbl[0:1, bass.ds(i + 1, 1)], min_val=0, max_val=E - 2)
                    then = dve.value_load(tbl[0:1, bass.ds(i + 2, 1)], min_val=0, max_val=E - 2)
                    step(i + PAIRS, (now, lblk[:, bass.ds(i, 1)]), (then, lblk[:, bass.ds(i + 1, 1)]))
            steps = n_more + PAIRS
            add_outputs(steps)

            root_of_mean(2)
            for b in range(NB):
                V.tensor_scalar(xn3[:, b, :], X2[:, b, :], rstd[:, b:b + 1], None, ALU.mult
                                ).then_inc(S["xn3_ready"], 1)
            columns_with_gain(h3T, "x3t_mm", "h3_ready", (0, 1, 2, 3, 4, 5), R_PLE)
            for i in range(6):
                n, b = divmod(i, NB)
                cols, rows = slice(n * 512, (n + 1) * 512), slice(0, ROWS[b])
                dve.wait_ge(S["pg_sig"], i + 1)
                link(V.tensor_tensor(sg[rows, b, cols], sg[rows, b, cols], ple3[rows, b, cols], ALU.mult))
                V.tensor_tensor(X2[rows, b, cols], X2[rows, b, cols], sg[rows, b, cols], ALU.add
                                ).then_inc(S["x4_ready"], 1)
            root_of_mean(3)
            dve.wait_ge(S["nfin_in"], 16)
            for b in range(NB):
                rows = slice(0, ROWS[b])
                V.scalar_tensor_tensor(out=sg[rows, b, :], in0=X2[rows, b, :], scalar=rstd[rows, b:b + 1],
                                       in1=nfin[rows, :], op0=ALU.mult, op1=ALU.mult).then_inc(S["y_ready"], 1)


INS = ["x_prompt", "x_sample", "state_hgrn", "cache_conv", "p_prompt", "p_sample", "norm_mix", "w_in",
       "hgrn_lb_logits", "hgrn_norm", "conv_w", "conv_b", "conv_ln_g", "conv_ln_b", "w_out", "norm_ffn",
       "w_router", "b_router", "w_gate_up", "b_gate_up", "w_down", "b_down", "w_ple", "norm_ple",
       "w_ple_gate", "norm_final"]
OUTS = [(1, SEQ, D), (1, DEC, D), (1, 1, H, KD, KD), (1, 1, PAD, W), (1, 1, H, KD, KD), (1, 1, PAD, W)]


def kernel(**inputs):
    import concourse.bacc as bacc
    from concourse.bass_utils import run_bass_kernel_spmd

    nc = bacc.Bacc("TRN2", target_bir_lowering=False, num_devices=1)
    arrays, aps, outs = {}, {}, []
    given = {n: np.ascontiguousarray(inputs[n]) for n in INS}
    given["consts"] = constants()
    for name, x in given.items():
        arrays[f"in_{name}"] = x
        aps[name] = nc.dram_tensor(f"in_{name}", x.shape, mybir.dt.from_np(x.dtype), kind="ExternalInput").ap()
    for i, shape in enumerate(OUTS):
        outs.append(nc.dram_tensor(f"out_{i}", shape, F32, kind="ExternalOutput").ap())
    program(nc, aps, outs)
    r = run_bass_kernel_spmd(nc, [arrays], core_ids=[0])
    return tuple(r.results[0][f"out_{i}"] for i in range(len(OUTS)))
```

```python
from contextlib import ExitStack

import numpy as np

import concourse.bass as bass
from concourse import mybir

ALU = mybir.AluOpType
ACT = mybir.ActivationFunctionType
F32 = mybir.dt.float32
BF16 = mybir.dt.bfloat16
I32 = mybir.dt.int32
U32 = mybir.dt.uint32
AX = mybir.AxisListType.X

P = 128
D = 1024
DC = D // P
NB = 3
SEQ, DEC = 256, 32
T = SEQ + DEC
ROWS = [P, P, DEC]
H, KD = 4, 128
W = H * KD
CW = 31
PAD = CW - 1
UP = PAD + SEQ + PAD + DEC
CV = UP - PAD
CH = 32
NCH = T // CH
HALVES = [16, 8, 4, 2, 1]
NLEV = len(HALVES) + 1
E = 32
TOPK = 4
SLOTS = 64
PAIRS = E // 2
OVER = 4
LIST = 24
MORE = SEQ * TOPK // SLOTS + DEC * TOPK // SLOTS
RING = 6
UNIT = 4096
LEAD = 9
PER = 12
EPS = 1e-6
LIMIT, ALPHA = 7.0, 1.702
TINY = 2.0 ** -64

C_ID, C_TRI, C_ONE, C_IOTA, C_MASK, C_EYE, C_OVER = 0, 128, 256, 384, 448, 640, 674
C_END = C_OVER + OVER * PAIRS
R_MIX, R_FFN, R_PLE, R_LB, R_CB, R_LG, R_LBI, R_HN, R_END = 0, 8, 16, 24, 32, 36, 40, 44, 48


def constants():
    c = np.zeros((P, C_END), np.float32)
    c[:, C_ID:C_ID + P] = np.eye(P)
    c[:, C_TRI:C_TRI + P] = np.triu(np.ones((P, P)), 1)
    c[:, C_ONE:C_ONE + P] = 1.0
    c[:, C_IOTA:C_IOTA + SLOTS] = np.arange(SLOTS)
    s = np.arange(P)[:, None] % CH
    t = np.arange(CH)[None, :]
    masks = [(s == t)]
    for m in HALVES:
        masks.append((s // (2 * m) == t // (2 * m)) & (s % (2 * m) < m) & (t % (2 * m) >= m))
    c[:, C_MASK:C_MASK + NLEV * CH] = np.concatenate(masks, 1)
    c[:96, C_EYE:C_EYE + E] = np.arange(96)[:, None] % E == np.arange(E)[None, :]
    c[:, C_OVER:] = OVER * PAIRS - np.arange(OVER * PAIRS)
    return c


class Own:

    def __init__(self, engine, semaphore):
        self.engine, self.semaphore, self.count = engine, semaphore, 0

    def inc(self, ins):
        ins.then_inc(self.semaphore, 1)
        self.count += 1
        return self.count

    def link(self, ins):
        self.engine.wait_ge(self.semaphore, self.inc(ins))


def convolve(V, own, chunks, taps, U, out, par, done):
    for w in taps:
        for cc in chunks:
            tap = par[:, R_END + w * H + cc:R_END + w * H + cc + 1]
            if w:
                own.engine.wait_ge(own.semaphore, done[cc])
            if w == 0:
                ins = V.tensor_scalar(out[:, cc, :], U[:, cc, 0:CV], tap, par[:, R_CB + cc:R_CB + cc + 1],
                                      ALU.mult, ALU.add)
            elif w < CW - 1:
                ins = V.scalar_tensor_tensor(out=out[:, cc, :], in0=U[:, cc, w:w + CV], scalar=tap,
                                             in1=out[:, cc, :], op0=ALU.mult, op1=ALU.add)
            else:
                V.scalar_tensor_tensor(out=out[:, cc, 0:SEQ], in0=U[:, cc, w:w + SEQ], scalar=tap,
                                       in1=out[:, cc, 0:SEQ], op0=ALU.mult, op1=ALU.add)
                ins = V.scalar_tensor_tensor(out=out[:, cc, SEQ:T], in0=U[:, cc, w + CV - DEC:w + CV],
                                             scalar=tap, in1=out[:, cc, CV - DEC:CV], op0=ALU.mult, op1=ALU.add)
            done[cc] = own.inc(ins)


def program(nc, a, o):
    with ExitStack() as ctx:
        def sb(name, cols, dt=F32):
            return ctx.enter_context(nc.sbuf_tensor(name, [P, cols], dt))

        def sem(name):
            return ctx.enter_context(nc.semaphore(name))

        ps = ctx.enter_context(nc.psum_tensor("ps", [P, 8, 512], F32))

        ring = sb("ring", RING * UNIT)
        cst = sb("cst", C_END)
        par = sb("par", R_END + CW * H)
        acc = sb("acc", NB * D)
        ple = sb("ple", NB * D)
        xs = sb("xs", 2 * 3 * D // 2)
        xs_s = sb("xs_s", D // 2)
        bias = sb("bias", D)
        small = sb("small", 1050)
        tbl = sb("tbl", 32, I32)
        pT = sb("pT", 2 * T)

        def cs(at, n, rows=P):
            return cst[0:rows, at:at + n]

        ident, tri, ones = cs(C_ID, P), cs(C_TRI, P), cs(C_ONE, P)
        used = [0]

        def sm(n):
            used[0] += n
            assert used[0] <= 1050, used[0]
            return small[:, used[0] - n:used[0]]

        def blocks(x, b=NB):
            return x.rearrange("p (b n) -> p b n", b=b)

        lbt, oml, lb_m, lb_e = sm(H), sm(H), sm(H), sm(2 * H)
        dec = blocks(sm(H * NCH), H)
        ss, rstd, eps, rs4, brow = sm(NB), sm(NB), sm(1), sm(1), sm(E)
        hss, hrs = sm(NB * H), sm(NB * H)
        lg, top, topf = blocks(sm(NB * E)), blocks(sm(NB * 8)), blocks(sm(NB * 8))
        topi = blocks(sm(NB * 8).bitcast(U32))
        wts, wsum, ntop = blocks(sm(NB * TOPK)), sm(NB), sm(NB)
        msk, gat, htmp = blocks(sm(NB * E)), blocks(sm(NB * E)), blocks(sm(NB * E))
        posm = blocks(sm(NB * (E + 2)))
        cnt, pmax, over = sm(E), sm(PAIRS), sm(OVER * PAIRS)
        lst, lblk, lcode = sm(LIST), sm(LIST), sm(LIST)
        cur, curg, curw = blocks(sm(NB * 2)), blocks(sm(NB * 2)), blocks(sm(NB * 2))

        ARENA = 15248
        arena = sb("arena", ARENA)
        at = [0]

        def ar(n):
            at[0] += n
            assert at[0] <= ARENA, at[0]
            return arena[:, at[0] - n:at[0]]

        hT = ar(DC * T).rearrange("p (c t) -> p c t", c=DC)
        mixT = hT
        qf, kf, cf = ar(H * T), ar(H * T), ar(H * T)
        U_flat = ar(H * UP)
        U = blocks(U_flat, H)
        cacc = blocks(ar(H * CV), H)
        Qd, Kd = ar(H * T), ar(H * T)
        KdT_flat = ar(NB * W)
        KdT = blocks(KdT_flat)
        og = KdT
        St = [ar(W), ar(W)]
        So = ar(W)
        lev = ar(H * T)
        tails = Kd[0:PAD, 0:2 * W]
        par_rows = cacc[:, 0, 0:2 * P]
        crow = Kd[0:PAD, 0:W]
        junk1 = arena[:, 8424:8424 + D]
        reset = KdT_flat[:, 0:H * T]
        csq = blocks(U_flat[:, 0:H * T], H)
        Ss = xs_s[:, 0:W]
        prod = So[:, 0:CV]
        ubs = KdT_flat[:, 0:H * T]
        xn = blocks(ple[:, :])
        v, g = blocks(ple[:, 0:NB * W]), blocks(ple[:, NB * W:2 * NB * W])
        ple3, X2 = blocks(ple[:, :]), blocks(acc[:, :])
        lq, lk = xs[:, 0:H * T], xs[:, H * T:2 * H * T]
        osq = blocks(xs[:, 0:NB * W])
        pr = blocks(xs[:, 2 * H * T:2 * H * T + NB * 256])
        score = xs[:, 2 * H * T:2 * H * T + NB * H * CH].rearrange("p (b h t) -> p b h t", b=NB, h=H)
        stmp = xs[:, 2 * H * T + NB * H * CH:3072].rearrange("p (b h t) -> p b h t", b=NB, h=H)
        cmean, croot = xs[:, 1728:1728 + T], xs[:, 2016:2016 + T]
        xn2 = blocks(arena[:, DC * T:DC * T + NB * D])
        gatT = arena[:, DC * T + NB * D:DC * T + NB * D + T]
        bd = U_flat[0:E, 0:D]
        wr = U_flat[:, 1136:1136 + DC * E]
        braw, bres = St[0][0:96, :], St[1][0:96, :]
        mtmp = arena[0:DEC, 7152:7152 + D // 2].bitcast(BF16)
        h4 = lambda x: blocks(x, H)

        at2 = [DC * T + 3 * H * T + H * UP]

        def ex(n):
            at2[0] += n
            assert at2[0] <= ARENA, at2[0]
            return arena[:, at2[0] - n:at2[0]]

        gath = ex(D)
        xT = blocks(ex(D), DC)
        gbuf, sgm, ubuf = ex(D), ex(D), ex(D)
        hidT = blocks(ex(D), DC)
        ybuf = ex(D)
        gw = ex(T)
        selg = blocks(ex(NB * P))
        selb = blocks(ex(NB * P // 2).bitcast(BF16))
        oneh = ex(P // 2).bitcast(BF16)
        eye = cst[:, C_EYE:C_EYE + E + 2]
        gate0 = blocks(arena[:, 0:DC * W], DC)
        h3T = blocks(arena[:, 7152:7152 + DC * T], DC)
        sg = blocks(arena[:, 9456:9456 + NB * D])
        nfin = arena[:, 5664:5664 + D]
        junk3 = arena[:, 12528:12528 + D]
        xsb = xs[:, :].bitcast(BF16).rearrange("p (b k n) -> p b k n", b=2, k=3)
        xssb = xs_s[:, :].bitcast(BF16)
        biasb = bias[:, :].bitcast(BF16)

        def pcol(at, n):
            return par[:, at:at + n]

        def by_token(at, n, t):
            return par[:, at:at + n].unsqueeze(2).broadcast_to([P, n, t])

        S = {n: sem(n) for n in (
            "cst_in", "x_in", "aux_in", "p_in", "raw_in", "gate_in", "bd_in", "nfin_in",
            "dve", "pool", "act",
            "par_mm", "par_ready", "sq", "nvar", "nsqrt", "xn_ready", "xt_mm", "ht_ready", "pt_mm", "pt_ready",
            "proj_mm", "ubsig_ready", "u_ready", "f_sig", "q_ready", "v_ready", "gsig_ready", "g_ready",
            "f_ready", "lnf_ready", "c_ready", "ec_ready", "ed_ready", "edx_ready", "qd_ready", "kd_ready",
            "lev_neg", "lev_exp", "lev_q", "lev_k", "lev_mm", "lev_done", "kdt_mm", "kdt_ready",
            "um_mm", "st_ready", "o_mm", "o_copied", "hvar", "hsqrt", "mixa_ready", "mixa_mm", "mixa_copied",
            "conv_ready", "conv_pool", "mean_mm", "csq_ready", "var_mm", "cvar", "csqrt", "cn_ready",
            "csig_ready", "mixc_ready", "tail_mm", "tail_ready",
            "out_mm", "x2_ready", "pl_mm", "pl_ready", "xn2_ready", "xt2_mm", "h2_ready", "lg_mm", "top_ready",
            "wexp", "msk_ready", "gat_ready", "pos_mm", "table_ready", "xs_h", "xs_r", "xs_m", "xs_l", "gT_mm", "gT_ready", "wr_ready", "x2_lo", "x2_hi",
            "bd_mm", "bd_added", "bias_ready", "zero_ready",
            "unit_done", "oneh_ready", "sel_cur", "sel_ready", "selg_cur", "selg_ready", "gath_mm", "gath_ev",
            "xt3_mm", "xt_ev", "gate_ready", "sig_ready", "up_ready", "gs_ready", "hid_ready", "hidt_mm",
            "hidt_ev", "y_ev", "gw_mm", "gw_ev", "comb_mm", "comb_add",
            "rs4_ready", "x3t_mm", "h3_ready", "pg_mm", "pg_sig", "x4_ready", "y_ready", "out_done")}
        full = [sem(f"ring_full{i}") for i in range(RING)]

        def slot(u):
            return ring[:, (u % RING) * UNIT:(u % RING + 1) * UNIT]

        block = ctx.enter_context(nc.Block())
        outs = {n: o[i] for i, n in enumerate(("yp", "ys", "sp", "cp", "ss", "cs"))}
        GROUPS = [1, 0, 5, 4, 2, 3]
        PROJ_DONE = [4, 8, 12, 16, 19, 22]
        X_BANK = ((0, 1), (2, 5), (6, 7))
        ROW_OF = [(a["x_prompt"], 0), (a["x_prompt"], P), (a["x_sample"], 0)]

        @block.sync
        def _(sp):
            for b in range(NB):
                src, r = ROW_OF[b]
                sp.dma_start(X2[0:ROWS[b], b, :], src[0, r:r + ROWS[b], :]).then_inc(S["x_in"], 16)
            sp.dma_start(cst[:, :], a["consts"]).then_inc(S["cst_in"], 16)
            at_row = 0
            rows = par_rows[:, 0:P]
            for name, n in (("norm_mix", 8), ("norm_ffn", 8), ("norm_ple", 8), ("hgrn_lb_logits", 8),
                            ("conv_b", 4), ("conv_ln_g", 4), ("conv_ln_b", 4), ("hgrn_norm", 4)):
                sp.dma_start(rows[at_row:at_row + n, :],
                             a[name].rearrange("l (c p) -> (l c) p", p=P)).then_inc(S["cst_in"], 16)
                at_row += n
            sp.dma_start(par_rows[0:CW * H, P:2 * P],
                         a["conv_w"].rearrange("l w (c p) -> (l w c) p", p=P)).then_inc(S["cst_in"], 16)
            def w_in(u):
                sp.dma_start(slot(u).rearrange("p (c n) -> p c n", c=DC),
                             a["w_in"][0, :, GROUPS[u] * W:(GROUPS[u] + 1) * W].rearrange(
                                 "(c p) n -> p c n", p=P)).then_inc(full[u % RING], 16)

            for u in range(6):
                w_in(u)
            for n in range(2):
                u = 6 + n
                sp.wait_ge(S["proj_mm"], PROJ_DONE[u - RING])
                sp.dma_start(slot(u).rearrange("p (c n) -> p c n", c=DC),
                             a["w_out"][0, :, n * W:(n + 1) * W].rearrange("(c p) n -> p c n", p=P)
                             ).then_inc(full[u % RING], 16)
            sp.wait_ge(S["proj_mm"], PROJ_DONE[2])
            sp.dma_start(slot(8)[:, 0:2 * D].rearrange("p (c n) -> p c n", c=2),
                         a["w_ple"][0].rearrange("(c p) n -> p c n", p=P)).then_inc(full[8 % RING], 16)

            def expert_unit(j, pair2, k):
                dst = slot(LEAD + k).rearrange("p (e n) -> p e n", e=2)
                if k < 8:
                    src = a["w_gate_up"][0, bass.ds(pair2, 2), k * P:(k + 1) * P, :].rearrange("e p n -> p e n")
                else:
                    r = (k - 8) * 2 * P
                    src = a["w_down"][0, bass.ds(pair2, 2), r:r + 2 * P, :].rearrange(
                        "e (p c) n -> p e (c n)", c=2)
                sp.dma_start(dst, src).then_inc(full[(LEAD + k) % RING], 16)

            before = {0: ("proj_mm", PROJ_DONE[3]), 1: ("proj_mm", PROJ_DONE[4]), 2: ("proj_mm", PROJ_DONE[5]),
                      3: ("out_mm", 6), 4: ("out_mm", 6), 5: ("pl_mm", 6)}
            for k in range(PER):
                if k in before:
                    sp.wait_ge(S[before[k][0]], before[k][1])
                else:
                    sp.wait_ge(S["unit_done"], k - RING + 1)
                expert_unit(0, 0, k)
            with sp.Fori(1, PAIRS) as j:
                for k in range(PER):
                    sp.wait_ge(S["unit_done"], j * PER + (k - RING + 1))
                    expert_unit(j, j * 2, k)
            sp.wait_ge(S["table_ready"], 1)
            n_more = sp.value_load(tbl[0:1, 0:1], min_val=0, max_val=MORE)
            with sp.If(n_more > 0):
                with sp.Fori(0, n_more) as i:
                    pair2 = sp.value_load(tbl[0:1, bass.ds(i + 1, 1)], min_val=0, max_val=E - 2)
                    for k in range(PER):
                        sp.wait_ge(S["unit_done"], i * PER + (PAIRS * PER + k - RING + 1))
                        expert_unit(i + PAIRS, pair2, k)
            steps = n_more + PAIRS
            sp.wait_ge(S["unit_done"], steps * PER + (1 - RING))
            sp.dma_start(slot(LEAD).rearrange("p (c n) -> p c n", c=DC),
                         a["w_ple_gate"][0, :, W:2 * W].rearrange("(c p) n -> p c n", p=P)
                         ).then_inc(full[LEAD % RING], 16)
            for b in range(NB):
                sp.wait_ge(S["y_ready"], b + 1)
                dst = outs["yp"][0, b * P:(b + 1) * P, :] if b < 2 else outs["ys"][0]
                sp.dma_start(dst, sg[0:ROWS[b], b, :]).then_inc(S["out_done"], 16)
            sp.wait_ge(S["out_done"], 16 * 7)

        @block.tensor
        def _(pe):
            mm, tr = nc.tensor.matmul, nc.tensor.transpose
            pe.wait_ge(S["cst_in"], 16 * 10)
            tr(ps[:, 0, 0:R_END], par_rows[0:R_END, 0:P], cs(C_ID, R_END, R_END))
            tr(ps[:, 0, 64:64 + CW * H], par_rows[0:CW * H, P:2 * P],
               cs(C_ID, CW * H, CW * H)).then_inc(S["par_mm"], 1)

            def to_columns(src, ready, done, first_bank):
                for b in range(NB):
                    n = ROWS[b]
                    pe.wait_ge(ready, b + 1)
                    for c in range(DC):
                        t = tr(ps[:, first_bank + 2 * b + c // 4, (c % 4) * n:(c % 4 + 1) * n],
                               src[0:n, b, c * P:(c + 1) * P], cs(C_ID, n, n))
                        if c % 4 == 3:
                            t.then_inc(done, 1)

            to_columns(xn, S["xn_ready"], S["xt_mm"], 2)
            pe.wait_ge(S["p_in"], 16 * NB)
            for c in range(2):
                for b in range(NB):
                    t = tr(ps[:, 1 - c, 192 * c + b * P:192 * c + b * P + ROWS[b]],
                           pr[0:ROWS[b], b, c * P:(c + 1) * P], cs(C_ID, ROWS[b], ROWS[b]))
            pe.wait_ge(S["aux_in"], 16 * 3)
            for cc in range(H):
                t = tr(ps[:, 1, T + cc * PAD:T + (cc + 1) * PAD], crow[:, cc * P:(cc + 1) * P], cs(C_ID, PAD, PAD))
            t.then_inc(S["pt_mm"], 1)

            ROUND = (0, 3, 4, 5, 6, 7)
            reader = [(S["f_sig"], n + 1) for n in range(4)] + [(S["q_ready"], n + 1) for n in range(4)] + \
                     [(S["ubsig_ready"], n + 1) for n in range(4)] + [(S["u_ready"], n + 1) for n in range(4)]

            def free_bank(t):
                if t >= 6:
                    pe.wait_ge(*reader[t - 6])
                return ROUND[t % 6]

            def columns(u):
                w = slot(u).rearrange("p (c n) -> p c n", c=DC)
                pe.wait_ge(full[u], 16)
                for cc in range(4):
                    bank = free_bank(4 * u + cc)
                    for k in range(DC):
                        t = mm(ps[:, bank, 0:T], w[:, k, cc * P:(cc + 1) * P], hT[:, k, :],
                               start=(k == 0), stop=(k == DC - 1))
                    t.then_inc(S["proj_mm"], 1)

            def row_block(src, w, b, bank, ks, last):
                for k in ks:
                    if b < 2:
                        t = mm(ps[:, bank, :], src[:, k, b * P:(b + 1) * P], w[:, k, :],
                               start=(k == 0), stop=(k == last), skip_group_check=True)
                    else:
                        for q in range(4):
                            t = mm(ps[q * DEC:(q + 1) * DEC, bank, 0:P], src[:, k, SEQ:T],
                                   w[:, k, q * P:(q + 1) * P], start=(k == 0), stop=(k == last),
                                   tile_position=(0, q * DEC), skip_group_check=True)
                return t

            def token_rows(src, w, banks, done):
                for b in range(NB):
                    row_block(src, w, b, banks[b], range(DC), DC - 1).then_inc(done, 1)

            def level(l):
                lqs, lks = (qf, kf) if l == 0 else (lq, lk)
                if l:
                    pe.wait_ge(S["lev_q"], l)
                    pe.wait_ge(S["lev_k"], l)
                else:
                    pe.wait_ge(S["kd_ready"], 1)
                    pe.wait_ge(S["q_ready"], 4)
                if l >= 2:
                    pe.wait_ge(S["lev_done"], l - 1)
                out = ps[:, 1 + l % 2, 0:NB * H * CH].rearrange("p (b h t) -> p b h t", b=NB, h=H)
                for i in range(NCH):
                    b, j = divmod(i, 4)
                    for h in range(H):
                        t = mm(out[j * CH:(j + 1) * CH, b, h, :], h4(lks)[:, h, i * CH:(i + 1) * CH],
                               h4(lqs)[:, h, i * CH:(i + 1) * CH], start=True, stop=True,
                               tile_position=(0, j * CH))
                t.then_inc(S["lev_mm"], 1)

            pe.wait_ge(S["ht_ready"], 6)
            pe.wait_ge(S["pt_ready"], 1)
            columns(0)
            columns(1)
            level(0)
            columns(2)
            for l in (1, 2, 3):
                level(l)
            columns(3)
            for l in (4, 5):
                level(l)
            pe.wait_ge(S["lev_done"], NLEV)
            for b in range(NB):
                if b == 2:
                    pe.wait_ge(S["kdt_ready"], 1)
                for h in range(H):
                    t = tr(ps[0:ROWS[b], 1 + b % 2, h * KD:(h + 1) * KD],
                           h4(Kd)[:, h, b * P:b * P + ROWS[b]], ident)
                t.then_inc(S["kdt_mm"], 1)
            pe.wait_ge(full[4], 16)
            for b in range(NB):
                bank = free_bank(16 + b)
                row_block(hT, slot(4).rearrange("p (c n) -> p c n", c=DC), b, bank, range(DC), DC - 1
                          ).then_inc(S["proj_mm"], 1)

            pe.wait_ge(S["kdt_ready"], NB)
            pe.wait_ge(S["v_ready"], NB)
            pe.wait_ge(S["qd_ready"], 1)
            pe.wait_ge(S["aux_in"], 16 * 3)

            def update(i):
                b, j = divmod(i, 4)
                if i >= 2:
                    pe.wait_ge(S["st_ready"], i - 1)
                for h in range(H):
                    t = mm(ps[:, 1 + i % 2, h * KD:(h + 1) * KD],
                           KdT[j * CH:(j + 1) * CH, b, h * KD:(h + 1) * KD],
                           v[j * CH:(j + 1) * CH, b, h * KD:(h + 1) * KD], start=True, stop=True)
                t.then_inc(S["um_mm"], 1)

            O_BANK = (6, 7, 0)

            def outputs(i):
                b, j = divmod(i, 4)
                oo = ps[:, O_BANK[b], :]
                if i > 0:
                    if i < NCH - 1:
                        pe.wait_ge(S["st_ready"], i)
                    state = St[i % 2] if i < NCH - 1 else Ss
                    for h in range(H):
                        mm(oo[j * CH:(j + 1) * CH, h * KD:(h + 1) * KD], h4(Qd)[:, h, i * CH:(i + 1) * CH],
                           state[:, h * KD:(h + 1) * KD], start=(h == 0), stop=False,
                           tile_position=(0, j * CH), skip_group_check=True)
                for h in range(H):
                    pm = score[j * CH:(j + 1) * CH, b, h, :]
                    t = mm(oo[j * CH:(j + 1) * CH, h * KD:(h + 1) * KD], pm,
                           v[j * CH:(j + 1) * CH, b, h * KD:(h + 1) * KD],
                           start=(i == 0 and h == 0), stop=True,
                           tile_position=(j * CH, j * CH), skip_group_check=True)
                t.then_inc(S["o_mm"], 1)

            update(0)
            update(1)
            outputs(0)
            pe.wait_ge(full[5], 16)
            wg = slot(5).rearrange("p (c n) -> p c n", c=DC)
            for i in range(1, NCH):
                if i in (1, 3, 5):
                    b = i // 2
                    bank = free_bank(19 + b)
                    row_block(hT, wg, b, bank, range(DC), DC - 1).then_inc(S["proj_mm"], 1)
                if i + 1 < NCH:
                    update(i + 1)
                outputs(i)

            for b in range(NB):
                n = ROWS[b]
                pe.wait_ge(S["mixa_ready"], 1)
                for c in range(4):
                    t = tr(ps[:, O_BANK[b], c * n:(c + 1) * n], og[0:n, b, c * P:(c + 1) * P], cs(C_ID, n, n))
                t.then_inc(S["mixa_mm"], 1)
            pe.wait_ge(S["g_ready"], NB)
            pe.wait_ge(S["conv_ready"], 1)
            pe.wait_ge(S["conv_pool"], 1)
            for cc in range(H):
                t = mm(ps[:, 3, 0:T], ones, cacc[:, cc, 0:T], start=(cc == 0), stop=(cc == H - 1))
            t.then_inc(S["mean_mm"], 1)
            pe.wait_ge(S["st_ready"], NCH)
            for s_, lo in enumerate((PAD + SEQ - PAD, UP - PAD)):
                for cc in range(H):
                    t = tr(ps[0:PAD, 1 + s_, cc * P:(cc + 1) * P], U[:, cc, lo:lo + PAD], ident)
            t.then_inc(S["tail_mm"], 1)
            pe.wait_ge(S["mixa_copied"], NB)
            pe.wait_ge(S["tail_ready"], 2)
            pe.wait_ge(full[0], 32)
            pe.wait_ge(full[1], 32)
            wout = [slot(6 + n).rearrange("p (c n) -> p c n", c=DC) for n in range(2)]
            for b in range(NB):
                for n in range(2):
                    row_block(mixT, wout[n], b, X_BANK[b][n], range(4), DC - 1)
            pe.wait_ge(S["csq_ready"], 1)
            for cc in range(H):
                t = mm(ps[:, 4, 0:T], ones, csq[:, cc, :], start=(cc == 0), stop=(cc == H - 1))
            t.then_inc(S["var_mm"], 1)
            pe.wait_ge(S["mixc_ready"], H)
            for b in range(NB):
                for n in range(2):
                    row_block(mixT, wout[n], b, X_BANK[b][n], range(4, DC), DC - 1).then_inc(S["out_mm"], 1)

            TB = ((3, 4), (1, 2), (5, 6))
            for b in range(NB):
                n = ROWS[b]
                pe.wait_ge(S["x2_ready"], 2 * b + 2)
                for c in range(DC):
                    t = tr(ps[:, TB[b][c // 4], (c % 4) * n:(c % 4 + 1) * n],
                           X2[0:n, b, c * P:(c + 1) * P], cs(C_ID, n, n))
                    if c % 4 == 3:
                        t.then_inc(S["xt2_mm"], 1)
            pe.wait_ge(S["x2_lo"], 3)
            pe.wait_ge(S["x2_hi"], 3)
            pe.wait_ge(S["wr_ready"], 1)
            for b in range(NB):
                n = ROWS[b]
                for k in range(DC):
                    t = mm(ps[0:n, 7, b * E:(b + 1) * E], hT[:, k, b * P:b * P + n], wr[:, k * E:(k + 1) * E],
                           start=(k == 0), stop=(k == DC - 1))
            t.then_inc(S["lg_mm"], 1)
            pe.wait_ge(full[2], 32)
            wple = slot(8)[:, 0:2 * D].rearrange("p (c n) -> p c n", c=2)
            pTc = pT[:, :].rearrange("p (c t) -> p c t", c=2)
            for n in range(2):
                for b in range(NB):
                    row_block(pTc, wple[:, :, n * W:(n + 1) * W], b, (4, 5, 6, 0, 1, 2)[3 * n + b], range(2), 1
                              ).then_inc(S["pl_mm"], 1)
            pe.wait_ge(S["msk_ready"], 1)
            for b in range(NB):
                for b2 in range(b + 1):
                    mm(ps[:, 3, b * E:(b + 1) * E], tri if b2 == b else ones, msk[:, b2, :],
                       start=(b2 == 0), stop=(b2 == b))
            for b in range(NB):
                t = mm(ps[:, 3, NB * E:NB * E + E], ones, msk[:, b, :], start=(b == 0), stop=(b == NB - 1))
            t.then_inc(S["pos_mm"], 1)

            G, PP, QQ = 0, 4, 6

            def gather(j):
                pe.wait_ge(S["sel_ready"], j + 1)
                for n in range(2):
                    cols = slice(n * 512, (n + 1) * 512)
                    for b in range(2):
                        for k in range(3):
                            mm(ps[:, PP + n, :], selb[:, b, :], xsb[:, b, k, cols],
                               start=(b == 0 and k == 0), stop=False)
                    mm(ps[:, PP + n, :], selb[0:96, 2, :], xssb[0:96, cols],
                       start=False, stop=True).then_inc(S["gath_mm"], 1)

            def turn_tokens(j):
                for n in range(2):
                    pe.wait_ge(S["gath_ev"], j * 2 + (n + 1))
                    for c in range(4 * n, 4 * n + 4):
                        t = tr(ps[:, PP + n, (c % 4) * P:(c % 4 + 1) * P], gath[:, c * P:(c + 1) * P], ident)
                    t.then_inc(S["xt3_mm"], 1)

            pe.wait_ge(S["xs_l"], NB)
            pe.wait_ge(S["pl_ready"], 6)
            gather(0)
            turn_tokens(0)
            pe.wait_ge(S["gat_ready"], 1)
            for b in range(NB):
                t = tr(ps[0:E, 0, b * P:b * P + ROWS[b]], gat[0:ROWS[b], b, :], cs(C_ID, ROWS[b], ROWS[b]))
            t.then_inc(S["gT_mm"], 1)
            pe.wait_ge(S["gT_ready"], 1)
            for i in range(6):
                b, n = i // 2, i % 2
                if i >= 2:
                    pe.wait_ge(S["bd_added"], i - 1)
                mm(ps[0:ROWS[b], 1 + n, :], gatT[0:E, b * P:b * P + ROWS[b]],
                   bd[0:E, n * 512:(n + 1) * 512], start=True, stop=True).then_inc(S["bd_mm"], 1)
            pe.wait_ge(S["bd_added"], 6)
            pe.wait_ge(S["bias_ready"], 1)

            def combine(j):
                pe.wait_ge(S["gw_ev"], j + 1)
                pe.wait_ge(S["y_ev"], j * 2 + 2)
                for i in range(6):
                    b, n = i // 2, i % 2
                    if i >= 2:
                        pe.wait_ge(S["comb_add"], j * 6 + (i - 1))
                    mm(ps[0:ROWS[b], QQ + n, :], gw[:, b * P:b * P + ROWS[b]],
                       ybuf[:, n * 512:(n + 1) * 512], start=True, stop=True).then_inc(S["comb_mm"], 1)

            def step(j):
                pe.wait_ge(S["oneh_ready"], j + 1)
                pe.wait_ge(S["xt_ev"], j * 2 + 2)
                for n in range(4):
                    mm(ps[:, G + n, :], oneh[0:96, :], biasb[0:96, n * 512:(n + 1) * 512],
                       start=True, stop=False, skip_group_check=True)
                for k in range(8):
                    u = LEAD + k
                    pe.wait_ge(full[u % RING], j * (16 * PER // RING) + 16 * (u // RING + 1))
                    w = slot(u).rearrange("p (e n) -> p e n", e=2)
                    for n in range(4):
                        for e in range(2):
                            t = mm(ps[e * 64:e * 64 + 64, G + n, :], xT[:, k, e * 64:e * 64 + 64],
                                   w[:, e, n * 512:(n + 1) * 512], start=False, stop=(k == 7),
                                   tile_position=(0, e * 64), skip_group_check=True)
                    t.then_inc(S["unit_done"], 1)
                pe.wait_ge(S["y_ev"], j * 2 + 2)
                gather(j + 1)
                combine(j)
                turn_tokens(j + 1)
                pe.wait_ge(S["comb_add"], j * 6 + 6)
                for n in range(2):
                    pe.wait_ge(S["hid_ready"], j * 2 + (n + 1))
                    for c in range(4 * n, 4 * n + 4):
                        k, r = c // 2, c % 2
                        t = tr(ps[:, QQ + n, (c % 4) * P:(c % 4 + 1) * P],
                               ubuf[:, 256 * k + r:256 * k + r + 255:2], ident)
                    t.then_inc(S["hidt_mm"], 1)
                pe.wait_ge(S["xt_ev"], j * 2 + 4)
                pe.wait_ge(S["hidt_ev"], j * 2 + 2)
                for k in range(4):
                    u = LEAD + 8 + k
                    pe.wait_ge(full[u % RING], j * (16 * PER // RING) + 16 * (u // RING + 1))
                    w = slot(u).rearrange("p (e c n) -> p e c n", e=2, c=2)
                    for c in range(2):
                        for n in range(2):
                            for e in range(2):
                                t = mm(ps[e * 64:e * 64 + 64, PP + n, :], hidT[:, 2 * k + c, e * 64:e * 64 + 64],
                                       w[:, e, c, n * 512:(n + 1) * 512],
                                       start=(k == 0 and c == 0), stop=(k == 3 and c == 1),
                                       tile_position=(0, e * 64))
                    t.then_inc(S["unit_done"], 1)
                    if k == 1:
                        pe.wait_ge(S["selg_ready"], j + 1)
                        for b in range(NB):
                            t = tr(ps[:, QQ, b * P:b * P + ROWS[b]], selg[0:ROWS[b], b, :],
                                   cs(C_ID, ROWS[b], ROWS[b]))
                        t.then_inc(S["gw_mm"], 1)

            with pe.Fori(0, PAIRS) as j:
                step(j)
            pe.wait_ge(S["table_ready"], 1)
            n_more = pe.value_load(tbl[0:1, 0:1], min_val=0, max_val=MORE)
            with pe.If(n_more > 0):
                with pe.Fori(0, n_more) as i:
                    step(i + PAIRS)
            steps = n_more + PAIRS
            combine(steps)
            for b in range(NB):
                n = ROWS[b]
                if b < 2:
                    pe.wait_ge(S["comb_add"], steps * 6 + (2, 6)[b])
                for c in range(DC):
                    t = tr(ps[:, 2 * b + c // 4, (c % 4) * n:(c % 4 + 1) * n],
                           X2[0:n, b, c * P:(c + 1) * P], cs(C_ID, n, n))
                    if c % 4 == 3:
                        t.then_inc(S["x3t_mm"], 1)
            pe.wait_ge(S["h3_ready"], 6)
            pe.wait_ge(S["gate_in"], 16)
            token_rows(h3T, gate0, (5, 6, 7), S["pg_mm"])
            pe.wait_ge(full[LEAD % RING], steps * (16 * PER // RING) + 16 * (LEAD // RING + 1))
            token_rows(h3T, slot(LEAD).rearrange("p (c n) -> p c n", c=DC), (0, 1, 2), S["pg_mm"])

        @block.scalar
        def _(act):
            fn, copy = nc.scalar.activation, nc.scalar.copy
            act.dma_start(crow, a["cache_conv"][0, 0]).then_inc(S["aux_in"], 16)
            act.dma_start(Ss.rearrange("p (h v) -> p h v", h=H),
                          a["state_hgrn"][0, 0].rearrange("h k v -> k h v")).then_inc(S["aux_in"], 16)
            act.dma_start(brow, a["b_router"].broadcast_to([P, E])).then_inc(S["aux_in"], 16)
            for b in range(NB):
                src = a["p_prompt"][0, 0, b * P:(b + 1) * P, :] if b < 2 else a["p_sample"][0, 0]
                act.dma_start(pr[0:ROWS[b], b, :], src).then_inc(S["p_in"], 16)

            def squares(n, junk, ready, at):
                act.wait_ge(ready, at)
                for b in range(NB):
                    if b or n:
                        act.wait_ge(S["sq"], NB * n + b)
                    fn(junk, X2[:, b, :], ACT.Square, accum_out=ss[:, b:b + 1]).then_inc(S["sq"], 1)
                act.wait_ge(S["nvar"], n + 1)
                fn(rstd, rstd, ACT.Sqrt).then_inc(S["nsqrt"], 1)

            act.wait_ge(S["x_in"], 16 * NB)
            act.wait_ge(S["cst_in"], 16 * 10)
            squares(0, junk1, S["zero_ready"], 1)
            act.wait_ge(S["dve"], 3)
            fn(lb_e, lb_e, ACT.Exp).then_inc(S["act"], 1)
            act.wait_ge(S["pt_mm"], 1)
            copy(pT[:, 0:T], ps[:, 1, 0:T])
            copy(pT[:, T:2 * T], ps[:, 0, 192:192 + T])
            copy(U[:, :, PAD + SEQ:PAD + SEQ + PAD],
                 ps[:, 1, T:T + H * PAD].rearrange("p (c t) -> p c t", c=H)).then_inc(S["pt_ready"], 1)
            ROUND = (0, 3, 4, 5, 6, 7)

            def rows_out(write, bank, b, n=0):
                if b < 2:
                    return write(slice(0, P), slice(n * W, (n + 1) * W), ps[:, bank, :])
                for q in range(4):
                    ins = write(slice(0, DEC), slice(n * W + q * P, n * W + (q + 1) * P),
                                ps[q * DEC:(q + 1) * DEC, bank, 0:P])
                return ins

            for cc in range(H):
                act.wait_ge(S["proj_mm"], cc + 1)
                fn(h4(kf)[:, cc, :], ps[:, ROUND[cc % 6], 0:T], ACT.Sigmoid).then_inc(S["f_sig"], 1)
            act.wait_ge(S["f_ready"], 1)
            fn(lev, cf, ACT.Ln).then_inc(S["lnf_ready"], 1)
            act.wait_ge(S["c_ready"], 1)
            fn(Qd, cf, ACT.Exp).then_inc(S["ec_ready"], 1)
            act.wait_ge(S["ed_ready"], 1)
            fn(Kd, lev, ACT.Exp).then_inc(S["edx_ready"], 1)
            for cc in range(H):
                act.wait_ge(S["proj_mm"], 4 + cc + 1)
                copy(h4(qf)[:, cc, :], ps[:, ROUND[(4 + cc) % 6], 0:T]).then_inc(S["q_ready"], 1)

            def level(l):
                act.wait_ge(S["lev_neg"], l)
                fn(lev, lev, ACT.Exp).then_inc(S["lev_exp"], 1)

            def conv_gate(cc):
                act.wait_ge(S["proj_mm"], 8 + cc + 1)
                fn(h4(ubs)[:, cc, :], ps[:, ROUND[(8 + cc) % 6], 0:T], ACT.Sigmoid).then_inc(S["ubsig_ready"], 1)

            level(1)
            conv_gate(0)
            level(2)
            for cc in range(1, H):
                conv_gate(cc)
            for l in range(3, NLEV):
                level(l)
            for b in range(NB):
                act.wait_ge(S["kdt_mm"], b + 1)
                if b == 0:
                    act.wait_ge(S["u_ready"], H)
                copy(KdT[0:ROWS[b], b, :], ps[0:ROWS[b], 1 + b % 2, :]).then_inc(S["kdt_ready"], 1)
            for b in range(NB):
                act.wait_ge(S["proj_mm"], 16 + b + 1)
                rows_out(lambda rows, cols, x: copy(v[rows, b, cols], x), ROUND[(16 + b) % 6], b
                         ).then_inc(S["v_ready"], 1)
            for b in range(NB):
                act.wait_ge(S["proj_mm"], 19 + b + 1)
                rows_out(lambda rows, cols, x: fn(g[rows, b, cols], x, ACT.Sigmoid), ROUND[(19 + b) % 6], b
                         ).then_inc(S["gsig_ready"], 1)
            act.wait_ge(S["um_mm"], NCH)
            for b in range(NB):
                act.wait_ge(S["o_mm"], min(4 * b + 4, NCH))
                copy(og[0:ROWS[b], b, :], ps[0:ROWS[b], (6, 7, 0)[b], :]).then_inc(S["o_copied"], 1)
            act.wait_ge(S["st_ready"], NCH)
            act.dma_start(outs["sp"][0, 0].rearrange("h k v -> k h v"),
                          St[0].rearrange("p (h v) -> p h v", h=H)).then_inc(S["out_done"], 16)
            act.dma_start(outs["ss"][0, 0].rearrange("h k v -> k h v"),
                          So.rearrange("p (h v) -> p h v", h=H)).then_inc(S["out_done"], 16)
            act.wait_ge(S["hvar"], 1)
            fn(hrs, hrs, ACT.Sqrt).then_inc(S["hsqrt"], 1)
            act.wait_ge(S["tail_mm"], 1)
            for s_ in range(2):
                copy(tails[:, s_ * W:(s_ + 1) * W], ps[0:PAD, 1 + s_, :]).then_inc(S["tail_ready"], 1)
            act.wait_ge(S["tail_ready"], 2)
            act.dma_start(outs["cp"][0, 0], tails[:, 0:W]).then_inc(S["out_done"], 16)
            act.dma_start(outs["cs"][0, 0], tails[:, W:2 * W]).then_inc(S["out_done"], 16)
            act.wait_ge(S["cvar"], 1)
            fn(croot, croot, ACT.Sqrt).then_inc(S["csqrt"], 1)
            for cc in range(H):
                act.wait_ge(S["cn_ready"], cc + 1)
                fn(csq[:, cc, :], cacc[:, cc, 0:T], ACT.Sigmoid).then_inc(S["csig_ready"], 1)
            act.wait_ge(S["mixc_ready"], H)
            act.dma_start(wr.rearrange("p (c e) -> p c e", c=DC),
                          a["w_router"][0].rearrange("(c p) e -> p c e", p=P)).then_inc(S["bd_in"], 16)
            act.dma_start(bd, a["b_down"][0]).then_inc(S["bd_in"], 16)
            TB = ((3, 4), (1, 2), (5, 6))
            for b in range(NB):
                act.wait_ge(S["xt2_mm"], 2 * b + 2)
                n = ROWS[b]
                copy(hT[:, 4:8, b * P:b * P + n], ps[:, TB[b][1], 0:4 * n].rearrange("p (c t) -> p c t", c=4)
                     ).then_inc(S["x2_hi"], 1)
            squares(1, KdT_flat[:, 0:D], S["x2_ready"], 6)
            for b in range(NB):
                act.wait_ge(S["xn2_ready"], b + 1)
                if b < 2:
                    copy(xsb[:, b, 0, :], xn2[:, b, :]).then_inc(S["xs_h"], 1)
                else:
                    copy(xssb[0:DEC, :], xn2[0:DEC, b, :]).then_inc(S["xs_h"], 1)
            for b in range(NB):
                act.wait_ge(S["xs_r"], b + 1)
                if b < 2:
                    copy(xsb[:, b, 1, :], xn2[:, b, :]).then_inc(S["xs_m"], 1)
                else:
                    copy(mtmp, xn2[0:DEC, b, :]).then_inc(S["xs_m"], 1)
            act.wait_ge(S["xs_m"], NB)
            copy(xssb[DEC:2 * DEC, :], mtmp)
            for b in range(NB):
                act.wait_ge(S["xs_r"], NB + b + 1)
                if b < 2:
                    copy(xsb[:, b, 2, :], xn2[:, b, :]).then_inc(S["xs_l"], 1)
                else:
                    copy(xssb[2 * DEC:3 * DEC, :], xn2[0:DEC, b, :]).then_inc(S["xs_l"], 1)
            for i in range(6):
                n, b = divmod(i, NB)
                act.wait_ge(S["pl_mm"], i + 1)
                rows_out(lambda rows, cols, x: copy(ple3[rows, b, cols], x), (4, 5, 6, 0, 1, 2)[i], b, n
                         ).then_inc(S["pl_ready"], 1)
            act.wait_ge(S["top_ready"], 1)
            for b in range(NB):
                fn(wts[:, b, :], top[:, b, 0:TOPK], ACT.Exp, bias=ntop[:, b:b + 1],
                   accum_out=wsum[:, b:b + 1]).then_inc(S["wexp"], 1)

            def copy_gathered(j):
                for n in range(2):
                    act.wait_ge(S["gath_mm"], j * 2 + (n + 1))
                    copy(gath[:, n * 512:(n + 1) * 512], ps[:, 4 + n, :]).then_inc(S["gath_ev"], 1)

            copy_gathered(0)
            act.wait_ge(S["gT_mm"], 1)
            copy(gatT[0:E, :], ps[0:E, 0, 0:T]).then_inc(S["gT_ready"], 1)
            act.wait_ge(S["bd_added"], 6)
            act.wait_ge(S["lg_mm"], 1)
            act.dma_start(gate0, a["w_ple_gate"][0, :, 0:W].rearrange("(c p) n -> p c n", p=P)
                          ).then_inc(S["gate_in"], 16)
            act.dma_start(nfin, a["norm_final"].rearrange("(o n) -> o n", o=1).broadcast_to([P, D])
                          ).then_inc(S["nfin_in"], 16)

            def step(j):
                for n in range(2):
                    act.wait_ge(S["gate_ready"], j * 2 + (n + 1))
                    cols = slice(n * 512, (n + 1) * 512)
                    fn(sgm[:, cols], gbuf[:, cols], ACT.Sigmoid, scale=ALPHA).then_inc(S["sig_ready"], 1)
                copy_gathered(j + 1)
                for n in range(2):
                    act.wait_ge(S["hidt_mm"], j * 2 + (n + 1))
                    copy(hidT[:, 4 * n:4 * n + 4, :],
                         ps[:, 6 + n, :].rearrange("p (c s) -> p c s", c=4)).then_inc(S["hidt_ev"], 1)
                act.wait_ge(S["unit_done"], j * PER + PER)
                for n in range(2):
                    copy(ybuf[:, n * 512:(n + 1) * 512], ps[:, 4 + n, :]).then_inc(S["y_ev"], 1)

            with act.Fori(0, PAIRS) as j:
                step(j)
            act.wait_ge(S["table_ready"], 1)
            n_more = act.value_load(tbl[0:1, 0:1], min_val=0, max_val=MORE)
            with act.If(n_more > 0):
                with act.Fori(0, n_more) as i:
                    step(i + PAIRS)
            steps = n_more + PAIRS
            squares(2, junk3, S["comb_add"], steps * 6 + 6)
            act.wait_ge(S["rs4_ready"], 1)
            for i in range(6):
                n, b = divmod(i, NB)
                act.wait_ge(S["pg_mm"], i + 1)
                bank = (5, 6, 7, 0, 1, 2)[i]
                if b < 2:
                    fn(sg[:, b, n * W:(n + 1) * W], ps[:, bank, :], ACT.Sigmoid, scale=rstd[:, b:b + 1]
                       ).then_inc(S["pg_sig"], 1)
                    continue
                for q in range(4):
                    rows = slice(q * DEC, (q + 1) * DEC)
                    ins = fn(sg[0:DEC, b, n * W + q * P:n * W + (q + 1) * P], ps[rows, bank, 0:P], ACT.Sigmoid,
                             scale=rs4[rows, 0:1])
                ins.then_inc(S["pg_sig"], 1)
            squares(3, junk3, S["x4_ready"], 6)

        @block.gpsimd
        def _(pool):
            own = Own(pool, S["pool"])
            link = own.link
            for n in range(2 * D // W):
                cols = slice(n * W, (n + 1) * W)
                if n:
                    pool.wait_ge(S["pool"], own.count)
                for r in range(3):
                    pool.dma_start(braw[r * E:(r + 1) * E, :], a["b_gate_up"][0, :, cols]).then_inc(S["raw_in"], 16)
                pool.wait_ge(S["raw_in"], 48 * (n + 1))
                link(nc.gpsimd.tensor_copy(biasb[0:96, cols], braw))
                link(nc.gpsimd.tensor_tensor(bres, braw, biasb[0:96, cols], ALU.subtract))
                link(nc.gpsimd.tensor_copy(biasb[E:2 * E, cols], bres[E:2 * E, :]))
                link(nc.gpsimd.tensor_copy(biasb[2 * E:3 * E, cols], bres[2 * E:3 * E, :]))
                link(nc.gpsimd.tensor_tensor(bres[2 * E:3 * E, :], bres[2 * E:3 * E, :], biasb[2 * E:3 * E, cols],
                                             ALU.subtract))
                last = nc.gpsimd.tensor_copy(biasb[2 * E:3 * E, cols], bres[2 * E:3 * E, :])
                if n < 2 * D // W - 1:
                    link(last)
                else:
                    last.then_inc(S["bias_ready"], 1)
            for l in range(1, NLEV):
                pool.wait_ge(S["lev_exp"], l)
                if l == 1:
                    pool.wait_ge(S["bias_ready"], 1)
                else:
                    pool.wait_ge(S["lev_mm"], l)
                    pool.wait_ge(S["lev_k"], l - 1)
                nc.gpsimd.tensor_tensor(lk, kf, lev, ALU.mult).then_inc(S["lev_k"], 1)
            pool.wait_ge(S["lev_k"], NLEV - 1)
            pool.wait_ge(S["u_ready"], H)
            pool.wait_ge(S["pt_ready"], 1)
            G, cc = nc.gpsimd, H - 1
            for w in range(CW):
                tap = par[:, R_END + w * H + cc:R_END + w * H + cc + 1]
                if w == 0:
                    link(G.tensor_scalar(cacc[:, cc, :], U[:, cc, 0:CV], tap, pcol(R_CB + cc, 1),
                                         ALU.mult, ALU.add))
                    continue
                link(G.tensor_scalar(prod, U[:, cc, w:w + CV], tap, None, ALU.mult))
                if w < CW - 1:
                    link(G.tensor_tensor(cacc[:, cc, :], cacc[:, cc, :], prod, ALU.add))
                else:
                    G.tensor_tensor(cacc[:, cc, 0:SEQ], cacc[:, cc, 0:SEQ], prod[:, 0:SEQ], ALU.add)
                    G.tensor_tensor(cacc[:, cc, SEQ:T], cacc[:, cc, CV - DEC:CV], prod[:, CV - DEC:CV], ALU.add
                                    ).then_inc(S["conv_pool"], 1)

        @block.vector
        def _(dve):
            V = nc.vector
            own = Own(dve, S["dve"])
            link = own.link

            def zero_rest(x):
                V.memset(x[DEC:64], 0.0)
                return V.memset(x[64:P], 0.0)

            zero_rest(X2[:, 2, :]).then_inc(S["zero_ready"], 1)
            dve.wait_ge(S["par_mm"], 1)
            V.tensor_copy(par[:, 0:R_END], ps[:, 0, 0:R_END])
            link(V.tensor_copy(par[:, R_END:R_END + CW * H], ps[:, 0, 64:64 + CW * H]))
            link(V.tensor_tensor(lb_m, pcol(R_LB, H), pcol(R_LB + H, H), ALU.max))
            link(V.tensor_tensor(blocks(lb_e, 2), blocks(pcol(R_LB, 2 * H), 2),
                                 lb_m.unsqueeze(1).broadcast_to([P, 2, H]), ALU.subtract))

            def root_of_mean(n):
                dve.wait_ge(S["sq"], NB * (n + 1))
                V.tensor_scalar(rstd, ss, 1.0 / D, EPS, ALU.mult, ALU.add).then_inc(S["nvar"], 1)
                dve.wait_ge(S["nsqrt"], n + 1)
                link(V.reciprocal(rstd, rstd))

            root_of_mean(0)
            for b in range(NB):
                V.tensor_scalar(xn[:, b, :], X2[:, b, :], rstd[:, b:b + 1], None, ALU.mult
                                ).then_inc(S["xn_ready"], 1)
            dve.wait_ge(S["act"], 1)
            link(V.tensor_tensor(lb_m, lb_e[:, 0:H], lb_e[:, H:2 * H], ALU.add))
            link(V.reciprocal(lb_m, lb_m))
            link(V.tensor_tensor(lbt, lb_e[:, 0:H], lb_m, ALU.mult))
            V.tensor_scalar(oml, lbt, -1.0, 1.0, ALU.mult, ALU.add).then_inc(S["par_ready"], 1)

            def columns_with_gain(dst, done, ready, banks, gain):
                for b in range(NB):
                    for n in range(2):
                        t = ROWS[b]
                        dve.wait_ge(S[done], 2 * b + n + 1)
                        V.tensor_tensor(dst[:, 4 * n:4 * n + 4, b * P:b * P + t],
                                        ps[:, banks[2 * b + n], 0:4 * t].rearrange("p (c t) -> p c t", c=4),
                                        by_token(gain + 4 * n, 4, t), ALU.mult).then_inc(S[ready], 1)

            columns_with_gain(hT, "xt_mm", "ht_ready", (2, 3, 4, 5, 6, 7), R_MIX)
            V.memset(U[:, :, 0:PAD], 0.0)
            link(V.memset(reset, 1.0))
            link(V.memset(reset[:, 0:H * T:CH], 0.0))
            for cc in range(H):
                dve.wait_ge(S["f_sig"], cc + 1)
                ins = V.tensor_scalar(h4(kf)[:, cc, :], h4(kf)[:, cc, :], oml[:, cc:cc + 1], lbt[:, cc:cc + 1],
                                      ALU.mult, ALU.add)
            link(ins)
            V.tensor_scalar(cf, kf, TINY, None, ALU.max).then_inc(S["f_ready"], 1)
            V.tensor_scalar(kf, kf, -1.0, 1.0, ALU.mult, ALU.add)
            dve.wait_ge(S["lnf_ready"], 1)
            V.tensor_tensor_scan(cf, reset, lev, 0.0, ALU.mult, ALU.add).then_inc(S["c_ready"], 1)
            dve.wait_ge(S["c_ready"], 1)
            by_chunk = cf.rearrange("p (i t) -> p i t", t=CH)
            V.tensor_tensor(lev.rearrange("p (i t) -> p i t", t=CH),
                            by_chunk[:, :, CH - 1:CH].broadcast_to([P, H * NCH, CH]), by_chunk, ALU.subtract
                            ).then_inc(S["ed_ready"], 1)

            def exponents(l):
                m = HALVES[l - 1]
                if l == 1:
                    dve.wait_ge(S["edx_ready"], 1)
                else:
                    dve.wait_ge(S["lev_k"], l - 1)
                    dve.wait_ge(S["lev_q"], l - 1)
                c, e = (x.rearrange("p (i t) -> p i t", t=2 * m) for x in (cf, lev))
                middle = c[:, :, m - 1:m].broadcast_to([P, H * T // (2 * m), m])
                V.tensor_tensor(e[:, :, 0:m], middle, c[:, :, 0:m], ALU.subtract)
                V.tensor_tensor(e[:, :, m:2 * m], c[:, :, m:2 * m], middle, ALU.subtract
                                ).then_inc(S["lev_neg"], 1)

            def level_q(l):
                dve.wait_ge(S["lev_exp"], l)
                if l >= 2:
                    dve.wait_ge(S["lev_mm"], l)
                V.tensor_tensor(lq, qf, lev, ALU.mult).then_inc(S["lev_q"], 1)

            def masked(l):
                dve.wait_ge(S["lev_mm"], l + 1)
                if l:
                    dve.wait_ge(S["lev_done"], l)
                raw = ps[:, 1 + l % 2, 0:NB * H * CH].rearrange("p (b h t) -> p b h t", b=NB, h=H)
                mask = cs(C_MASK + l * CH, CH)
                for lo, n, rows in ((0, 2, P), (2, 1, DEC)):
                    dst = (score if l == 0 else stmp)[0:rows, lo:lo + n]
                    ins = V.tensor_tensor(dst, raw[0:rows, lo:lo + n],
                                          mask[0:rows].unsqueeze(1).unsqueeze(1).broadcast_to([rows, n, H, CH]),
                                          ALU.mult)
                if l == 0:
                    ins.then_inc(S["lev_done"], 1)
                    return
                link(ins)
                V.tensor_tensor(score[:, 0:2], score[:, 0:2], stmp[:, 0:2], ALU.add)
                V.tensor_tensor(score[0:DEC, 2], score[0:DEC, 2], stmp[0:DEC, 2], ALU.add
                                ).then_inc(S["lev_done"], 1)

            exponents(1)
            V.tensor_tensor(Kd, Kd, kf, ALU.mult).then_inc(S["kd_ready"], 1)
            link(V.tensor_copy(dec, h4(Qd)[:, :, CH - 1:T:CH]))
            dve.wait_ge(S["q_ready"], H)
            V.tensor_tensor(Qd, Qd, qf, ALU.mult).then_inc(S["qd_ready"], 1)
            level_q(1)
            masked(0)
            exponents(2)
            for l in (2, 3, 4):
                level_q(l)
                exponents(l + 1)
                masked(l - 1)

            for cc in range(H):
                bank = (0, 3, 4, 5, 6, 7)[(12 + cc) % 6]
                dve.wait_ge(S["ubsig_ready"], cc + 1)
                dve.wait_ge(S["proj_mm"], 12 + cc + 1)
                V.tensor_tensor(U[:, cc, PAD:PAD + SEQ], ps[:, bank, 0:SEQ], h4(ubs)[:, cc, 0:SEQ], ALU.mult)
                V.tensor_tensor(U[:, cc, UP - DEC:UP], ps[:, bank, SEQ:T], h4(ubs)[:, cc, SEQ:T], ALU.mult
                                ).then_inc(S["u_ready"], 1)
            level_q(5)
            masked(4)
            masked(5)

            dve.wait_ge(S["pt_ready"], 1)
            dve.wait_ge(S["u_ready"], H)
            taps_done = {}

            def taps(lo, hi):
                convolve(V, own, range(H - 1), range(lo, hi), U, cacc, par, taps_done)

            def state(i):
                last = i == NCH - 1
                old, new = (Ss, So) if last else (St[i % 2], St[(i + 1) % 2])
                up = ps[:, 1 + i % 2, :]
                dve.wait_ge(S["um_mm"], i + 1)
                if i == 0:
                    dve.wait_ge(S["bias_ready"], 1)
                    V.tensor_copy(new, up).then_inc(S["st_ready"], 1)
                    return
                if i >= 2:
                    dve.wait_ge(S["o_mm"], i)
                if last:
                    dve.wait_ge(S["conv_pool"], 1)
                dve.wait_ge(S["st_ready"], i)
                for h in range(H):
                    hs = slice(h * KD, (h + 1) * KD)
                    ins = V.scalar_tensor_tensor(out=new[:, hs], in0=old[:, hs], scalar=dec[:, h, i:i + 1],
                                                 in1=up[:, hs], op0=ALU.mult, op1=ALU.add)
                ins.then_inc(S["st_ready"], 1)

            def gate(b):
                bank = (0, 3, 4, 5, 6, 7)[(19 + b) % 6]
                dve.wait_ge(S["gsig_ready"], b + 1)
                if b < 2:
                    ins = V.tensor_tensor(g[:, b, :], ps[:, bank, :], g[:, b, :], ALU.mult)
                else:
                    for q in range(4):
                        x = g[0:DEC, b, q * P:(q + 1) * P]
                        ins = V.tensor_tensor(x, ps[q * DEC:(q + 1) * DEC, bank, 0:P], x, ALU.mult)
                ins.then_inc(S["g_ready"], 1)

            taps(0, 8)
            for i in range(NCH - 1):
                state(i)
                taps(8 + i, 9 + i)
                if i in (3, 5, 7):
                    gate(i // 2 - 1)
            taps(16, 22)
            state(NCH - 1)
            dve.wait_ge(S["o_copied"], NB)
            zero_rest(g[:, 2, :])
            link(zero_rest(og[:, 2, :]))
            link(V.tensor_tensor(osq, og, og, ALU.mult))
            heads = "p b (h n) -> p (b h) n"
            link(V.tensor_reduce(hss, osq.rearrange(heads, h=H), AX, ALU.add))
            V.tensor_scalar(hrs, hss, 1.0 / KD, EPS, ALU.mult, ALU.add).then_inc(S["hvar"], 1)
            taps(22, 24)
            dve.wait_ge(S["hsqrt"], 1)
            link(V.reciprocal(hrs, hrs))
            link(V.tensor_tensor(og.rearrange(heads, h=H), og.rearrange(heads, h=H),
                                 hrs.unsqueeze(2).broadcast_to([P, NB * H, KD]), ALU.mult))
            V.tensor_tensor(og, og, g, ALU.mult).then_inc(S["mixa_ready"], 1)
            taps(24, 26)
            for b in range(NB):
                n = ROWS[b]
                dve.wait_ge(S["mixa_mm"], b + 1)
                V.tensor_tensor(mixT[:, 0:4, b * P:b * P + n],
                                ps[:, (6, 7, 0)[b], 0:4 * n].rearrange("p (c t) -> p c t", c=4),
                                by_token(R_HN, H, n), ALU.mult).then_inc(S["mixa_copied"], 1)
            taps(26, CW)
            dve.wait_ge(S["dve"], own.count)
            V.memset(eps, 0.0).then_inc(S["conv_ready"], 1)

            cv = cacc[:, :, 0:T]
            dve.wait_ge(S["mean_mm"], 1)
            link(V.tensor_scalar(cmean, ps[:, 3, 0:T], 1.0 / W, None, ALU.mult))
            link(V.tensor_tensor(cv, cv, cmean.unsqueeze(1).broadcast_to([P, H, T]), ALU.subtract))
            dve.wait_ge(S["tail_mm"], 1)
            V.tensor_tensor(csq, cv, cv, ALU.mult).then_inc(S["csq_ready"], 1)
            dve.wait_ge(S["var_mm"], 1)
            V.tensor_scalar(croot, ps[:, 4, 0:T], 1.0 / W, EPS, ALU.mult, ALU.add).then_inc(S["cvar"], 1)
            dve.wait_ge(S["csqrt"], 1)
            link(V.reciprocal(croot, croot))
            link(V.tensor_tensor(cv, cv, croot.unsqueeze(1).broadcast_to([P, H, T]), ALU.mult))
            for cc in range(H):
                V.tensor_scalar(cv[:, cc, :], cv[:, cc, :], pcol(R_LG + cc, 1), pcol(R_LBI + cc, 1),
                                ALU.mult, ALU.add).then_inc(S["cn_ready"], 1)
            for cc in range(H):
                dve.wait_ge(S["csig_ready"], cc + 1)
                V.tensor_tensor(mixT[:, 4 + cc, :], cv[:, cc, :], csq[:, cc, :], ALU.mult
                                ).then_inc(S["mixc_ready"], 1)

            dve.wait_ge(S["bd_in"], 32)
            wrc = wr.rearrange("p (c e) -> p c e", c=DC)
            V.tensor_tensor(wrc, wrc, by_token(R_FFN, DC, E), ALU.mult).then_inc(S["wr_ready"], 1)
            for b in range(NB):
                for n in range(2):
                    bank = X_BANK[b][n]
                    dve.wait_ge(S["out_mm"], 2 * b + n + 1)
                    if b < 2:
                        x = X2[:, b, n * W:(n + 1) * W]
                        ins = V.tensor_tensor(x, ps[:, bank, :], x, ALU.add)
                    else:
                        for q in range(4):
                            x = X2[0:DEC, b, n * W + q * P:n * W + (q + 1) * P]
                            ins = V.tensor_tensor(x, ps[q * DEC:(q + 1) * DEC, bank, 0:P], x, ALU.add)
                    ins.then_inc(S["x2_ready"], 1)
            for b in range(NB):
                n = ROWS[b]
                dve.wait_ge(S["xt2_mm"], 2 * b + 1)
                V.tensor_copy(hT[:, 0:4, b * P:b * P + n],
                              ps[:, (3, 1, 5)[b], 0:4 * n].rearrange("p (c t) -> p c t", c=4)
                              ).then_inc(S["x2_lo"], 1)
            root_of_mean(1)
            for b in range(NB):
                V.tensor_scalar(xn2[:, b, :], X2[:, b, :], rstd[:, b:b + 1], None, ALU.mult
                                ).then_inc(S["xn2_ready"], 1)
            def remainders(k):
                for b in range(NB):
                    dve.wait_ge(S[("xs_h", "xs_m")[k]], b + 1)
                    if b < 2:
                        r, p_ = xn2[:, b, :], xsb[:, b, k, :]
                    else:
                        r, p_ = xn2[0:DEC, b, :], (xssb[0:DEC, :], mtmp)[k]
                    V.tensor_tensor(r, r, p_, ALU.subtract).then_inc(S["xs_r"], 1)

            remainders(0)
            zero_rest(lg[:, 2, :])
            dve.wait_ge(S["lg_mm"], 1)
            for b in range(NB):
                n = ROWS[b]
                ins = V.scalar_tensor_tensor(out=lg[0:n, b, :], in0=ps[0:n, 7, b * E:(b + 1) * E],
                                             scalar=rstd[0:n, b:b + 1], in1=brow[0:n, :],
                                             op0=ALU.mult, op1=ALU.add)
            link(ins)
            for b in range(NB):
                ins = V.max(top[:, b, :], lg[:, b, :])
            link(ins)
            V.tensor_scalar(ntop, top[:, :, 0], -1.0, None, ALU.mult).then_inc(S["top_ready"], 1)
            for b in range(NB):
                ins = V.max_index(topi[:, b, :], top[:, b, :], lg[:, b, :])
            link(ins)
            link(V.tensor_copy(topf, topi))
            chosen = selg.rearrange("p b (k e) -> p b k e", k=TOPK)
            link(V.tensor_tensor(chosen, cs(C_IOTA, E).unsqueeze(1).unsqueeze(1).broadcast_to([P, NB, TOPK, E]),
                                 topf[:, :, 0:TOPK].unsqueeze(3).broadcast_to([P, NB, TOPK, E]), ALU.is_equal))
            link(V.tensor_reduce(msk, chosen.rearrange("p b k e -> p b e k"), AX, ALU.add))
            zero_rest(msk[:, 2, :]).then_inc(S["msk_ready"], 1)
            remainders(1)
            dve.wait_ge(S["pos_mm"], 1)
            link(V.scalar_tensor_tensor(out=htmp, in0=ps[:, 3, 0:NB * E].rearrange("p (b e) -> p b e", b=NB),
                                        scalar=1.0, in1=msk, op0=ALU.add, op1=ALU.mult))
            link(V.tensor_scalar(posm[:, :, 0:E], htmp, -1.0, None, ALU.add))
            V.tensor_copy(posm[DEC:2 * DEC, 2, 0:E], posm[0:DEC, 2, 0:E])
            link(V.tensor_copy(posm[2 * DEC:3 * DEC, 2, 0:E], posm[0:DEC, 2, 0:E]))
            link(V.tensor_copy(cnt, ps[:, 3, NB * E:NB * E + E]))

            iota_s = cs(C_IOTA, SLOTS).unsqueeze(1).broadcast_to([P, NB * 2, SLOTS])

            def per_slot(x):
                return x.rearrange("p b e -> p (b e)").unsqueeze(2).broadcast_to([P, NB * 2, SLOTS])

            def columns_of(pair2, x):
                return x[:, :, bass.ds(pair2, 2)]

            def place(out, pair2, offset):
                if offset is None:
                    return V.tensor_copy(out, columns_of(pair2, posm))
                return V.tensor_scalar(out, columns_of(pair2, posm), offset, None, ALU.subtract)

            def select(j, pair2, offset):
                dve.wait_ge(S["gath_mm"], j * 2)
                place(cur, pair2, offset).then_inc(S["sel_cur"], 1)
                dve.wait_ge(S["sel_cur"], j + 1)
                V.tensor_tensor(selb.rearrange("p b (e s) -> p (b e) s", e=2), iota_s, per_slot(cur),
                                ALU.is_equal).then_inc(S["sel_ready"], 1)

            def select_bias(j, pair2):
                V.tensor_copy(oneh[0:96, :].rearrange("p (e s) -> p e s", e=2),
                              eye[0:96, bass.ds(pair2, 2)].unsqueeze(2).broadcast_to([96, 2, SLOTS])
                              ).then_inc(S["oneh_ready"], 1)

            def weigh(j, pair2, offset):
                place(curg, pair2, offset)
                V.tensor_copy(curw, columns_of(pair2, gat)).then_inc(S["selg_cur"], 1)
                dve.wait_ge(S["selg_cur"], j * 2 + 1)
                sel = selg.rearrange("p b (e s) -> p (b e) s", e=2)
                V.tensor_tensor(sel, iota_s, per_slot(curg), ALU.is_equal).then_inc(S["selg_cur"], 1)
                dve.wait_ge(S["selg_cur"], j * 2 + 2)
                V.tensor_tensor(sel, sel, per_slot(curw), ALU.mult).then_inc(S["selg_ready"], 1)

            def tokens_out(j):
                for n in range(2):
                    dve.wait_ge(S["xt3_mm"], j * 2 + (n + 1))
                    V.tensor_tensor(xT[:, 4 * n:4 * n + 4, :],
                                    ps[:, 4 + n, :].rearrange("p (c s) -> p c s", c=4),
                                    by_token(R_FFN + 4 * n, 4, P), ALU.mult).then_inc(S["xt_ev"], 1)

            dve.wait_ge(S["out_done"], 64)
            select(0, 0, None)
            select_bias(0, 0)
            dve.wait_ge(S["wexp"], NB)
            link(V.reciprocal(wsum, wsum))
            link(V.tensor_tensor(wts, wts, wsum.unsqueeze(2).broadcast_to([P, NB, TOPK]), ALU.mult))
            link(V.tensor_tensor(chosen, chosen, wts.unsqueeze(3).broadcast_to([P, NB, TOPK, E]), ALU.mult))
            link(V.tensor_reduce(gat, chosen.rearrange("p b k e -> p b e k"), AX, ALU.add))
            zero_rest(gat[:, 2, :]).then_inc(S["gat_ready"], 1)
            tokens_out(0)
            V.memset(gw, 0.0).then_inc(S["gw_ev"], 1)
            V.memset(ybuf[:, 0:512], 0.0).then_inc(S["y_ev"], 1)
            V.memset(ybuf[:, 512:D], 0.0).then_inc(S["y_ev"], 1)
            for i in range(6):
                b, n = i // 2, i % 2
                x = X2[0:ROWS[b], b, n * 512:(n + 1) * 512]
                dve.wait_ge(S["bd_mm"], i + 1)
                V.tensor_tensor(x, ps[0:ROWS[b], 1 + n, :], x, ALU.add).then_inc(S["bd_added"], 1)

            link(V.tensor_tensor(pmax, cnt[:, 0:E:2], cnt[:, 1:E:2], ALU.max))
            for b in range(OVER):
                ins = V.tensor_scalar(over[:, b * PAIRS:(b + 1) * PAIRS], pmax, float(SLOTS * (b + 1)), None,
                                      ALU.is_gt)
            link(ins)
            link(V.tensor_reduce(lst[:, 0:1], over, AX, ALU.add))
            V.tensor_copy(tbl[:, 0:1], lst[:, 0:1])
            link(V.tensor_tensor(over, over, cs(C_OVER, OVER * PAIRS), ALU.mult))
            for r in range(LIST // 8):
                link(V.max(lst[:, 8 * r:8 * r + 8], over))
                if r < LIST // 8 - 1:
                    link(V.match_replace(over, lst[:, 8 * r:8 * r + 8], over, 0.0))
            link(V.tensor_scalar(lcode, lst, -1.0, float(OVER * PAIRS), ALU.mult, ALU.add))
            link(V.tensor_scalar(lblk, lcode, float(PAIRS), None, ALU.is_ge))
            for q in range(2, OVER + 1):
                link(V.scalar_tensor_tensor(out=lblk, in0=lcode, scalar=float(PAIRS * q), in1=lblk,
                                            op0=ALU.is_ge, op1=ALU.add))
            link(V.scalar_tensor_tensor(out=lcode, in0=lblk, scalar=-float(PAIRS), in1=lcode,
                                        op0=ALU.mult, op1=ALU.add))
            link(V.tensor_scalar(lblk, lblk, float(SLOTS), float(SLOTS), ALU.mult, ALU.add))
            V.tensor_scalar(tbl[:, 1:1 + LIST], lcode, 2.0, None, ALU.mult).then_inc(S["table_ready"], 1)
            dve.wait_ge(S["table_ready"], 1)
            first = dve.value_load(tbl[0:1, 1:2], min_val=0, max_val=E - 2)
            place(posm[:, :, E:E + 2], first, lblk[:, 0:1])
            link(V.tensor_copy(eye[0:96, E:E + 2], eye[0:96, bass.ds(first, 2)]))

            def step(j, this, following):
                select(j + 1, *following)
                dve.wait_ge(S["unit_done"], j * PER + 1)
                select_bias(j + 1, following[0])
                weigh(j, *this)
                dve.wait_ge(S["unit_done"], j * PER + 8)
                for n in range(2):
                    cols = slice(n * 512, (n + 1) * 512)
                    V.tensor_scalar(gbuf[:, cols], ps[:, n, :], LIMIT, None, ALU.min).then_inc(S["gate_ready"], 1)
                for n in range(2):
                    cols = slice(n * 512, (n + 1) * 512)
                    V.tensor_scalar(ubuf[:, cols], ps[:, 2 + n, :], LIMIT, -LIMIT, ALU.min, ALU.max
                                    ).then_inc(S["up_ready"], 1)
                for n in range(2):
                    cols = slice(n * 512, (n + 1) * 512)
                    dve.wait_ge(S["sig_ready"], j * 2 + (n + 1))
                    V.tensor_tensor(gbuf[:, cols], gbuf[:, cols], sgm[:, cols], ALU.mult).then_inc(S["gs_ready"], 1)
                for n in range(2):
                    cols = slice(n * 512, (n + 1) * 512)
                    dve.wait_ge(S["gs_ready"], j * 2 + (n + 1))
                    dve.wait_ge(S["up_ready"], j * 2 + (n + 1))
                    V.scalar_tensor_tensor(out=ubuf[:, cols], in0=ubuf[:, cols], scalar=1.0, in1=gbuf[:, cols],
                                           op0=ALU.add, op1=ALU.mult).then_inc(S["hid_ready"], 1)
                add_outputs(j)
                tokens_out(j + 1)
                dve.wait_ge(S["gw_mm"], j + 1)
                V.tensor_copy(gw, ps[:, 6, 0:T]).then_inc(S["gw_ev"], 1)

            def add_outputs(j):
                for i in range(6):
                    b, n = i // 2, i % 2
                    x = X2[0:ROWS[b], b, n * 512:(n + 1) * 512]
                    dve.wait_ge(S["comb_mm"], j * 6 + (i + 1))
                    V.tensor_tensor(x, ps[0:ROWS[b], 6 + n, :], x, ALU.add).then_inc(S["comb_add"], 1)

            with dve.Fori(0, PAIRS) as j:
                step(j, (j * 2, None), (j * 2 + 2, None))
            n_more = dve.value_load(tbl[0:1, 0:1], min_val=0, max_val=MORE)
            with dve.If(n_more > 0):
                with dve.Fori(0, n_more) as i:
                    now = dve.value_load(tbl[0:1, bass.ds(i + 1, 1)], min_val=0, max_val=E - 2)
                    then = dve.value_load(tbl[0:1, bass.ds(i + 2, 1)], min_val=0, max_val=E - 2)
                    step(i + PAIRS, (now, lblk[:, bass.ds(i, 1)]), (then, lblk[:, bass.ds(i + 1, 1)]))
            steps = n_more + PAIRS
            add_outputs(steps)

            columns_with_gain(h3T, "x3t_mm", "h3_ready", (0, 1, 2, 3, 4, 5), R_PLE)
            root_of_mean(2)
            for q in range(4):
                ins = V.tensor_copy(rs4[q * DEC:(q + 1) * DEC, :], rstd[0:DEC, 2:3])
            ins.then_inc(S["rs4_ready"], 1)
            for i in range(6):
                n, b = divmod(i, NB)
                cols, rows = slice(n * 512, (n + 1) * 512), slice(0, ROWS[b])
                dve.wait_ge(S["pg_sig"], i + 1)
                link(V.tensor_tensor(sg[rows, b, cols], sg[rows, b, cols], ple3[rows, b, cols], ALU.mult))
                V.tensor_tensor(X2[rows, b, cols], X2[rows, b, cols], sg[rows, b, cols], ALU.add
                                ).then_inc(S["x4_ready"], 1)
            root_of_mean(3)
            dve.wait_ge(S["nfin_in"], 16)
            for b in range(NB):
                rows = slice(0, ROWS[b])
                V.scalar_tensor_tensor(out=sg[rows, b, :], in0=X2[rows, b, :], scalar=rstd[rows, b:b + 1],
                                       in1=nfin[rows, :], op0=ALU.mult, op1=ALU.mult).then_inc(S["y_ready"], 1)


INS = ["x_prompt", "x_sample", "state_hgrn", "cache_conv", "p_prompt", "p_sample", "norm_mix", "w_in",
       "hgrn_lb_logits", "hgrn_norm", "conv_w", "conv_b", "conv_ln_g", "conv_ln_b", "w_out", "norm_ffn",
       "w_router", "b_router", "w_gate_up", "b_gate_up", "w_down", "b_down", "w_ple", "norm_ple",
       "w_ple_gate", "norm_final"]
OUTS = [(1, SEQ, D), (1, DEC, D), (1, 1, H, KD, KD), (1, 1, PAD, W), (1, 1, H, KD, KD), (1, 1, PAD, W)]


def kernel(**inputs):
    import concourse.bacc as bacc
    from concourse.bass_utils import run_bass_kernel_spmd

    nc = bacc.Bacc("TRN2", target_bir_lowering=False, num_devices=1)
    arrays, aps, outs = {}, {}, []
    given = {n: np.ascontiguousarray(inputs[n]) for n in INS}
    given["consts"] = constants()
    for name, x in given.items():
        arrays[f"in_{name}"] = x
        aps[name] = nc.dram_tensor(f"in_{name}", x.shape, mybir.dt.from_np(x.dtype), kind="ExternalInput").ap()
    for i, shape in enumerate(OUTS):
        outs.append(nc.dram_tensor(f"out_{i}", shape, F32, kind="ExternalOutput").ap())
    program(nc, aps, outs)
    r = run_bass_kernel_spmd(nc, [arrays], core_ids=[0])
    return tuple(r.results[0][f"out_{i}"] for i in range(len(OUTS)))
```

```python
from contextlib import ExitStack

import numpy as np

import concourse.bass as bass
from concourse import mybir

ALU = mybir.AluOpType
ACT = mybir.ActivationFunctionType
F32 = mybir.dt.float32
BF16 = mybir.dt.bfloat16
I32 = mybir.dt.int32
U32 = mybir.dt.uint32
AX = mybir.AxisListType.X

P = 128
D = 1024
DC = D // P
NB = 3
SEQ, DEC = 256, 32
T = SEQ + DEC
ROWS = [P, P, DEC]
H, KD = 4, 128
W = H * KD
CW = 31
PAD = CW - 1
UP = PAD + SEQ + PAD + DEC
CV = UP - PAD
CH = 32
NCH = T // CH
HALVES = [16, 8, 4, 2, 1]
NLEV = len(HALVES) + 1
E = 32
TOPK = 4
SLOTS = 64
PAIRS = E // 2
OVER = 4
LIST = 24
MORE = SEQ * TOPK // SLOTS + DEC * TOPK // SLOTS
RING = 6
UNIT = 4096
LEAD = 9
PER = 12
APROD = 8
EARLY = 5
FREE = 5
SMALL = 1080
EPS = 1e-6
LIMIT, ALPHA = 7.0, 1.702
TINY = 2.0 ** -64

C_ID, C_TRI, C_ONE, C_IOTA, C_MASK, C_EYE, C_OVER = 0, 128, 256, 384, 448, 640, 674
C_END = C_OVER + OVER * PAIRS
R_MIX, R_FFN, R_PLE, R_LB, R_CB, R_LG, R_LBI, R_HN, R_END = 0, 8, 16, 24, 32, 36, 40, 44, 48


def constants():
    c = np.zeros((P, C_END), np.float32)
    c[:, C_ID:C_ID + P] = np.eye(P)
    c[:, C_TRI:C_TRI + P] = np.triu(np.ones((P, P)), 1)
    c[:, C_ONE:C_ONE + P] = 1.0
    c[:, C_IOTA:C_IOTA + SLOTS] = np.arange(SLOTS)
    s = np.arange(P)[:, None] % CH
    t = np.arange(CH)[None, :]
    masks = [(s == t)]
    for m in HALVES:
        masks.append((s // (2 * m) == t // (2 * m)) & (s % (2 * m) < m) & (t % (2 * m) >= m))
    c[:, C_MASK:C_MASK + NLEV * CH] = np.concatenate(masks, 1)
    c[:96, C_EYE:C_EYE + E] = np.arange(96)[:, None] % E == np.arange(E)[None, :]
    c[:, C_OVER:] = OVER * PAIRS - np.arange(OVER * PAIRS)
    return c


class Own:

    def __init__(self, engine, semaphore):
        self.engine, self.semaphore, self.count = engine, semaphore, 0

    def inc(self, ins):
        ins.then_inc(self.semaphore, 1)
        self.count += 1
        return self.count

    def link(self, ins):
        self.engine.wait_ge(self.semaphore, self.inc(ins))


def convolve(V, own, chunks, taps, U, out, par, done, ready):
    for w in taps:
        for cc in chunks:
            tap = par[:, R_END + w * H + cc:R_END + w * H + cc + 1]
            if w:
                own.engine.wait_ge(own.semaphore, done[cc])
            if w == 0:
                ins = V.tensor_scalar(out[:, cc, :], U[:, cc, 0:CV], tap, par[:, R_CB + cc:R_CB + cc + 1],
                                      ALU.mult, ALU.add)
            elif w < CW - 1:
                ins = V.scalar_tensor_tensor(out=out[:, cc, :], in0=U[:, cc, w:w + CV], scalar=tap,
                                             in1=out[:, cc, :], op0=ALU.mult, op1=ALU.add)
            else:
                V.scalar_tensor_tensor(out=out[:, cc, 0:SEQ], in0=U[:, cc, w:w + SEQ], scalar=tap,
                                       in1=out[:, cc, 0:SEQ], op0=ALU.mult, op1=ALU.add)
                ins = V.scalar_tensor_tensor(out=out[:, cc, SEQ:T], in0=U[:, cc, w + CV - DEC:w + CV],
                                             scalar=tap, in1=out[:, cc, CV - DEC:CV], op0=ALU.mult, op1=ALU.add)
            if w < CW - 1:
                done[cc] = own.inc(ins)
            else:
                ins.then_inc(ready, 1)


def program(nc, a, o):
    with ExitStack() as ctx:
        def sb(name, cols, dt=F32):
            return ctx.enter_context(nc.sbuf_tensor(name, [P, cols], dt))

        def sem(name):
            return ctx.enter_context(nc.semaphore(name))

        ps = ctx.enter_context(nc.psum_tensor("ps", [P, 8, 512], F32))

        ring = sb("ring", RING * UNIT)
        cst = sb("cst", C_END)
        par = sb("par", R_END + CW * H)
        acc = sb("acc", NB * D)
        ple = sb("ple", NB * D)
        xs = sb("xs", 2 * 3 * D // 2)
        xs_s = sb("xs_s", D // 2)
        bias = sb("bias", D)
        small = sb("small", SMALL)
        tbl = sb("tbl", 32, I32)
        pT = sb("pT", 2 * T)

        def cs(at, n, rows=P):
            return cst[0:rows, at:at + n]

        ident, tri, ones = cs(C_ID, P), cs(C_TRI, P), cs(C_ONE, P)
        used = [0]

        def sm(n):
            used[0] += n
            assert used[0] <= SMALL, used[0]
            return small[:, used[0] - n:used[0]]

        def blocks(x, b=NB):
            return x.rearrange("p (b n) -> p b n", b=b)

        lbt, oml, lb_m, lb_e = sm(H), sm(H), sm(H), sm(2 * H)
        dec = blocks(sm(H * NCH), H)
        ss, rstd, rs4, brow = sm(NB), sm(NB), sm(1), sm(E)
        hss, hrs = sm(NB * H), sm(NB * H)
        lg, top, topf = blocks(sm(NB * E)), blocks(sm(NB * 8)), blocks(sm(NB * 8))
        topi = blocks(sm(NB * 8).bitcast(U32))
        wts, wsum, ntop = blocks(sm(NB * TOPK)), sm(NB), sm(NB)
        msk4 = sm(4 * E)
        msk, gat, htmp = blocks(msk4[:, 0:NB * E]), blocks(sm(NB * E)), blocks(sm(NB * E))
        posm = blocks(sm(NB * (E + 2)))
        cnt, pmax, over = sm(E), sm(PAIRS), sm(OVER * PAIRS)
        lst, lblk, lcode = sm(LIST), sm(LIST), sm(LIST)
        cur, curg, curw = blocks(sm(NB * 2)), blocks(sm(NB * 2)), blocks(sm(NB * 2))

        ARENA = 15248
        arena = sb("arena", ARENA)
        at = [0]

        def ar(n):
            at[0] += n
            assert at[0] <= ARENA, at[0]
            return arena[:, at[0] - n:at[0]]

        hT = ar(DC * T).rearrange("p (c t) -> p c t", c=DC)
        mixT = hT
        qf, kf, cf = ar(H * T), ar(H * T), ar(H * T)
        U_flat = ar(H * UP)
        U = blocks(U_flat, H)
        cacc = blocks(ar(H * CV), H)
        Qd, Kd = ar(H * T), ar(H * T)
        KdT_flat = ar(NB * W)
        KdT = blocks(KdT_flat)
        St = [ar(W), ar(W)]
        So = ar(W)
        lev = ar(H * T)
        tails = Kd[0:PAD, 0:2 * W]
        par_rows = cacc[:, 0, 0:2 * P]
        crow = Kd[0:PAD, 0:W]
        A_Q = DC * T
        A_CONV = A_Q + 3 * H * T + H * UP
        A_QD = A_CONV + H * CV
        A_ST = A_QD + 2 * H * T + NB * W
        junk1 = arena[:, A_QD:A_QD + D]
        reset = KdT_flat[:, 0:H * T]
        csq = blocks(U_flat[:, 0:H * T], H)
        Ss = xs_s[:, 0:W]
        prod = lev[:, 0:CV]
        aprod = [lev[:, (i + 1) * CV:(i + 2) * CV] for i in range(2)] + \
                [xs[:, i * CV:(i + 1) * CV] for i in range(APROD - 2)]
        ubs = KdT_flat[:, 0:H * T]
        xn = blocks(ple[:, :])
        v, g = blocks(ple[:, 0:NB * W]), blocks(ple[:, NB * W:2 * NB * W])
        ple3, X2 = blocks(ple[:, :]), blocks(acc[:, :])
        lq, lk = xs[:, 0:H * T], xs[:, H * T:2 * H * T]
        og = blocks(arena[:, A_Q:A_Q + NB * W])
        osq = blocks(arena[:, A_Q + NB * W:A_Q + 2 * NB * W])
        pr = blocks(xs[:, 2 * H * T:2 * H * T + NB * 256])
        score = xs[:, 2 * H * T:2 * H * T + NB * H * CH].rearrange("p (b h t) -> p b h t", b=NB, h=H)
        stmp = xs[:, 2 * H * T + NB * H * CH:3072].rearrange("p (b h t) -> p b h t", b=NB, h=H)
        croot = xs[:, 2016:2016 + T]
        xn2 = blocks(arena[:, A_CONV + 2 * D:A_CONV + 5 * D])
        junk2 = arena[:, A_CONV + 5 * D:A_CONV + 6 * D]
        wr = arena[:, A_QD:A_QD + DC * E]
        braw = xs[0:96, 0:2 * D]
        bres = arena[0:96, A_ST:A_ST + D]
        mtmp = arena[0:DEC, A_CONV:A_CONV + D // 2].bitcast(BF16)

        def h4(x):
            return blocks(x, H)

        at2 = [A_CONV]

        def ex(n):
            at2[0] += n
            assert at2[0] <= ARENA, at2[0]
            return arena[:, at2[0] - n:at2[0]]

        gath = ex(D)
        xT = blocks(ex(D), DC)
        gbuf, sgm, ubuf = ex(D), ex(D), ex(D)
        hidT = blocks(ex(D), DC)
        ybuf = ex(D)
        gw = ex(T)
        selg = blocks(ex(NB * P))
        selb = blocks(ex(NB * P // 2).bitcast(BF16))
        oneh = ex(P // 2).bitcast(BF16)
        eye = cst[:, C_EYE:C_EYE + E + 2]
        gate0 = blocks(arena[:, 0:DC * W], DC)
        h3T = blocks(arena[:, A_CONV:A_CONV + DC * T], DC)
        sg = blocks(arena[:, A_CONV + DC * T:A_CONV + DC * T + NB * D])
        gate1 = blocks(arena[:, DC * W:DC * W + EARLY * W], EARLY)
        junk3, nfin = xs[:, 0:D], xs[:, D:2 * D]
        xsb = xs[:, :].bitcast(BF16).rearrange("p (b k n) -> p b k n", b=2, k=3)
        xssb = xs_s[:, :].bitcast(BF16)
        biasb = bias[:, :].bitcast(BF16)

        def pcol(at, n):
            return par[:, at:at + n]

        def by_token(at, n, t):
            return par[:, at:at + n].unsqueeze(2).broadcast_to([P, n, t])

        S = {n: sem(n) for n in (
            "cst_in", "x_in0", "x_in1", "x_in2", "par_in", "w_in_head", "aux_in", "p_in", "raw_in",
            "gate_in", "wr_in", "bd_in", "nfin_in",
            "dve", "pool", "act",
            "par_mm", "lb_sub", "sq", "nvar", "nsqrt", "xn_ready", "xt_mm", "ht_ready", "pt_mm", "pt_ready",
            "proj_mm", "ubsig_ready", "u_ready", "f_sig", "q_ready", "v_ready", "gsig_ready", "g_ready",
            "f_ready", "lnf_ready", "c_ready", "ec_ready", "ed_ready", "edx_ready", "qd_ready", "kd_ready",
            "lev_neg", "lev_exp", "lev_q", "lev_k", "lev_mm", "lev_done", "kdt_mm", "kdt_ready",
            "um_mm", "st_ready", "o_mm", "osq_ready", "gated", "hvar", "hsqrt", "mixa_ready", "mixa_mm", "mixa_copied",
            "conv_ready", "conv_pool", "prod_ready", "prod_used", "mean_mm", "csq_ready", "var_mm", "cvar",
            "csqrt", "cn_ready", "csig_ready", "mixc_ready", "tail_mm", "tail_ready",
            "out_mm", "x2_ready", "pl_mm", "xn2_ready", "xt2_mm", "lg_mm", "top_ready",
            "wexp", "msk_ready", "gat_ready", "pos_mm", "table_ready", "xs_h", "xs_rh", "xs_rh_s", "xs_m",
            "xs_rm", "xs_rm_s", "xs_l", "gT_mm", "wr_ready", "x2_lo", "x2_hi", "bias_ready", "zero_ready",
            "gw_zero",
            "unit_done", "oneh_ready", "sel_cur", "sel_ready", "selg_cur", "selg_ready", "half_done",
            "gath_mm", "gath_ev",
            "xt3_mm", "xt_ev", "gate_ready", "sig_ready", "up_ready", "gs_ready", "hid_ready", "hidt_mm",
            "hidt_ev", "y_ev", "gw_mm", "gw_ev", "comb_mm", "comb_add",
            "rs4_ready", "x3t_mm", "h3_ready", "pg_mm", "pg_sig", "x4_ready", "y_ready0", "y_ready1", "y_ready2",
            "y_scaled", "last_rstd", "out_done")}
        S["pl_ready"] = [sem(f"pl_ready{i}") for i in range(6)]
        full = [sem(f"ring_full{i}") for i in range(RING)]

        def slot(u):
            return ring[:, (u % RING) * UNIT:(u % RING + 1) * UNIT]

        block = ctx.enter_context(nc.Block())
        outs = {n: o[i] for i, n in enumerate(("yp", "ys", "sp", "cp", "ss", "cs"))}
        GROUPS = [1, 0, 5, 4, 2, 3]
        PROJ_DONE = [4, 8, 12, 16, 19, 22]
        O_BANK = (6, 7, 0)
        T3_BANK = (6, 7, 0, 1, 2, 3)
        PG_BANK = (4, 5, 6, 7, 0, 1)
        PL_BANK = (3, 4, 3, 4, 7, 6)
        X_BANK = ((1, 2), (5, 6), (7, 0))
        ROW_OF = [(a["x_prompt"], 0), (a["x_prompt"], P), (a["x_sample"], 0)]

        @block.sync
        def _(sp):
            for b in range(NB):
                src, r = ROW_OF[b]
                sp.dma_start(X2[0:ROWS[b], b, :], src[0, r:r + ROWS[b], :]).then_inc(S[f"x_in{b}"], 16)
            sp.dma_start(cst[:, :], a["consts"]).then_inc(S["cst_in"], 16)
            at_row = 0
            rows = par_rows[:, 0:P]
            for name, n in (("norm_mix", 8), ("norm_ffn", 8), ("norm_ple", 8), ("hgrn_lb_logits", 8),
                            ("conv_b", 4), ("conv_ln_g", 4), ("conv_ln_b", 4), ("hgrn_norm", 4)):
                sp.dma_start(rows[at_row:at_row + n, :],
                             a[name].rearrange("l (c p) -> (l c) p", p=P)).then_inc(S["par_in"], 16)
                at_row += n
            sp.dma_start(par_rows[0:CW * H, P:2 * P],
                         a["conv_w"].rearrange("l w (c p) -> (l w c) p", p=P)).then_inc(S["par_in"], 16)

            def w_in(u, lo, hi, done):
                sp.dma_start(slot(u).rearrange("p (c n) -> p c n", c=DC)[:, :, lo:hi],
                             a["w_in"][0, :, GROUPS[u] * W + lo:GROUPS[u] * W + hi].rearrange(
                                 "(c p) n -> p c n", p=P)).then_inc(done, 16)

            w_in(0, 0, W // 2, S["w_in_head"])
            for r in range(3):
                sp.dma_start(braw[r * E:(r + 1) * E, :], a["b_gate_up"][0]).then_inc(S["raw_in"], 16)
            w_in(0, W // 2, W, full[0])
            for u in range(1, 6):
                w_in(u, 0, W, full[u])
            for n in range(2):
                u = 6 + n
                sp.wait_ge(S["proj_mm"], PROJ_DONE[u - RING])
                sp.dma_start(slot(u).rearrange("p (c n) -> p c n", c=DC),
                             a["w_out"][0, :, n * W:(n + 1) * W].rearrange("(c p) n -> p c n", p=P)
                             ).then_inc(full[u % RING], 16)
            sp.wait_ge(S["proj_mm"], PROJ_DONE[2])
            sp.dma_start(slot(8)[:, 0:2 * D].rearrange("p (c n) -> p c n", c=2),
                         a["w_ple"][0].rearrange("(c p) n -> p c n", p=P)).then_inc(full[8 % RING], 16)

            def expert_unit(j, pair2, k):
                dst = slot(LEAD + k).rearrange("p (e n) -> p e n", e=2)
                if k < 8:
                    src = a["w_gate_up"][0, bass.ds(pair2, 2), k * P:(k + 1) * P, :].rearrange("e p n -> p e n")
                else:
                    r = (k - 8) * 2 * P
                    src = a["w_down"][0, bass.ds(pair2, 2), r:r + 2 * P, :].rearrange(
                        "e (p c) n -> p e (c n)", c=2)
                sp.dma_start(dst, src).then_inc(full[(LEAD + k) % RING], 16)

            before = {0: ("proj_mm", PROJ_DONE[3]), 1: ("proj_mm", PROJ_DONE[4]), 2: ("proj_mm", PROJ_DONE[5]),
                      3: ("out_mm", 6), 4: ("out_mm", 6), 5: ("pl_mm", 6)}
            for k in range(PER):
                if k in before:
                    sp.wait_ge(S[before[k][0]], before[k][1])
                else:
                    sp.wait_ge(S["unit_done"], k - RING + 1)
                expert_unit(0, 0, k)
            with sp.Fori(1, PAIRS) as j:
                for k in range(PER):
                    sp.wait_ge(S["unit_done"], j * PER + (k - RING + 1))
                    expert_unit(j, j * 2, k)
            sp.wait_ge(S["table_ready"], 1)
            n_more = sp.value_load(tbl[0:1, 0:1], min_val=0, max_val=MORE)
            with sp.If(n_more > 0):
                with sp.Fori(0, n_more) as i:
                    pair2 = sp.value_load(tbl[0:1, bass.ds(i + 1, 1)], min_val=0, max_val=E - 2)
                    for k in range(PER):
                        sp.wait_ge(S["unit_done"], i * PER + (PAIRS * PER + k - RING + 1))
                        expert_unit(i + PAIRS, pair2, k)
            steps = n_more + PAIRS
            sp.wait_ge(S["unit_done"], steps * PER + (1 - RING))
            sp.dma_start(slot(LEAD)[:, 0:(DC - EARLY) * W].rearrange("p (c n) -> p c n", n=W),
                         a["w_ple_gate"][0, EARLY * P:D, W:2 * W].rearrange("(c p) n -> p c n", p=P)
                         ).then_inc(full[LEAD % RING], 16)
            sp.wait_ge(S["gath_mm"], steps * 2 + 2)
            sp.dma_start(nfin, a["norm_final"].rearrange("(o n) -> o n", o=1).broadcast_to([P, D])
                         ).then_inc(S["nfin_in"], 16)
            for b in range(NB):
                sp.wait_ge(S[f"y_ready{b}"], 1)
                dst = outs["yp"][0, b * P:(b + 1) * P, :] if b < 2 else outs["ys"][0]
                sp.dma_start(dst, sg[0:ROWS[b], b, :]).then_inc(S["out_done"], 16)
            sp.wait_ge(S["out_done"], 16 * 7)

        @block.tensor
        def _(pe):
            mm, tr = nc.tensor.matmul, nc.tensor.transpose
            pe.wait_ge(S["cst_in"], 16)
            pe.wait_ge(S["par_in"], 16 * 9)
            tr(ps[:, 0, 0:R_END], par_rows[0:R_END, 0:P], cs(C_ID, R_END, R_END))
            tr(ps[:, 0, 64:64 + CW * H], par_rows[0:CW * H, P:2 * P],
               cs(C_ID, CW * H, CW * H)).then_inc(S["par_mm"], 1)

            for b in range(NB):
                n = ROWS[b]
                pe.wait_ge(S["xn_ready"], b + 1)
                for c in range(DC):
                    t = tr(ps[:, 2 + 2 * b + c // 4, (c % 4) * n:(c % 4 + 1) * n],
                           xn[0:n, b, c * P:(c + 1) * P], cs(C_ID, n, n))
                    if c % 4 == 3:
                        t.then_inc(S["xt_mm"], 1)
            def turn_frames():
                pe.wait_ge(S["p_in"], 16 * NB)
                for c in range(2):
                    for b in range(NB):
                        tr(ps[:, 1 + c, b * P:b * P + ROWS[b]], pr[0:ROWS[b], b, c * P:(c + 1) * P],
                           cs(C_ID, ROWS[b], ROWS[b]))
                pe.wait_ge(S["aux_in"], 16 * 3)
                for cc in range(H):
                    t = tr(ps[:, 2, T + cc * PAD:T + (cc + 1) * PAD], crow[:, cc * P:(cc + 1) * P],
                           cs(C_ID, PAD, PAD))
                t.then_inc(S["pt_mm"], 1)

            ROUND = (0, 3, 4, 5, 6, 7)
            reader = [(S["f_sig"], n + 1) for n in range(4)] + [(S["q_ready"], n + 1) for n in range(4)] + \
                     [(S["ubsig_ready"], n + 1) for n in range(4)] + [(S["u_ready"], n + 1) for n in range(4)]

            def free_bank(t):
                if t >= 6:
                    pe.wait_ge(*reader[t - 6])
                return ROUND[t % 6]

            def columns(u, part=range(4)):
                w = slot(u).rearrange("p (c n) -> p c n", c=DC)
                for cc in part:
                    if u == 0 and cc == 0:
                        pe.wait_ge(S["w_in_head"], 16)
                    elif cc == (2 if u == 0 else 0):
                        pe.wait_ge(full[u], 16)
                    bank = free_bank(4 * u + cc)
                    for k in range(DC):
                        t = mm(ps[:, bank, 0:T], w[:, k, cc * P:(cc + 1) * P], hT[:, k, :],
                               start=(k == 0), stop=(k == DC - 1))
                    t.then_inc(S["proj_mm"], 1)

            def row_block(src, w, b, bank, ks, last, w_from=0):
                for k in ks:
                    if b < 2:
                        t = mm(ps[:, bank, :], src[:, k, b * P:(b + 1) * P], w[:, k - w_from, :],
                               start=(k == 0), stop=(k == last), skip_group_check=True)
                    else:
                        for q in range(4):
                            t = mm(ps[q * DEC:(q + 1) * DEC, bank, 0:P], src[:, k, SEQ:T],
                                   w[:, k - w_from, q * P:(q + 1) * P], start=(k == 0), stop=(k == last),
                                   tile_position=(0, q * DEC), skip_group_check=True)
                return t

            def level(l):
                lqs, lks = (qf, kf) if l == 0 else (lq, lk)
                if l:
                    pe.wait_ge(S["lev_q"], l)
                    pe.wait_ge(S["lev_k"], l)
                else:
                    pe.wait_ge(S["kd_ready"], 1)
                    pe.wait_ge(S["q_ready"], 4)
                if l >= 2:
                    pe.wait_ge(S["lev_done"], l - 1)
                out = ps[:, 1 + l % 2, 0:NB * H * CH].rearrange("p (b h t) -> p b h t", b=NB, h=H)
                for i in range(NCH):
                    b, j = divmod(i, 4)
                    for h in range(H):
                        t = mm(out[j * CH:(j + 1) * CH, b, h, :], h4(lks)[:, h, i * CH:(i + 1) * CH],
                               h4(lqs)[:, h, i * CH:(i + 1) * CH], start=True, stop=True,
                               tile_position=(0, j * CH))
                t.then_inc(S["lev_mm"], 1)

            pe.wait_ge(S["ht_ready"], 6)
            columns(0)
            turn_frames()
            columns(1)
            pe.wait_ge(S["pt_ready"], 1)
            for l in range(NLEV):
                columns(2 + l // 4, [l % 4])
                level(l)
            columns(3, [2, 3])
            pe.wait_ge(S["lev_done"], NLEV)
            for b in range(NB):
                if b == 2:
                    pe.wait_ge(S["kdt_ready"], 1)
                for h in range(H):
                    t = tr(ps[0:ROWS[b], 1 + b % 2, h * KD:(h + 1) * KD],
                           h4(Kd)[:, h, b * P:b * P + ROWS[b]], ident)
                t.then_inc(S["kdt_mm"], 1)
            pe.wait_ge(full[4], 16)
            for b in range(NB):
                bank = free_bank(16 + b)
                row_block(hT, slot(4).rearrange("p (c n) -> p c n", c=DC), b, bank, range(DC), DC - 1
                          ).then_inc(S["proj_mm"], 1)

            pe.wait_ge(S["kdt_ready"], NB)
            pe.wait_ge(S["v_ready"], NB)
            pe.wait_ge(S["qd_ready"], 1)
            pe.wait_ge(S["aux_in"], 16 * 3)

            def update(i):
                b, j = divmod(i, 4)
                if i >= 2:
                    pe.wait_ge(S["st_ready"], i - 1)
                for h in range(H):
                    t = mm(ps[:, 1 + i % 2, h * KD:(h + 1) * KD],
                           KdT[j * CH:(j + 1) * CH, b, h * KD:(h + 1) * KD],
                           v[j * CH:(j + 1) * CH, b, h * KD:(h + 1) * KD], start=True, stop=True)
                t.then_inc(S["um_mm"], 1)

            def outputs(i):
                b, j = divmod(i, 4)
                oo = ps[:, O_BANK[b], :]
                if i > 0:
                    if i < NCH - 1:
                        pe.wait_ge(S["st_ready"], i)
                    state = St[i % 2] if i < NCH - 1 else Ss
                    for h in range(H):
                        mm(oo[j * CH:(j + 1) * CH, h * KD:(h + 1) * KD], h4(Qd)[:, h, i * CH:(i + 1) * CH],
                           state[:, h * KD:(h + 1) * KD], start=(h == 0), stop=False,
                           tile_position=(0, j * CH), skip_group_check=True)
                for h in range(H):
                    pm = score[j * CH:(j + 1) * CH, b, h, :]
                    t = mm(oo[j * CH:(j + 1) * CH, h * KD:(h + 1) * KD], pm,
                           v[j * CH:(j + 1) * CH, b, h * KD:(h + 1) * KD],
                           start=(i == 0 and h == 0), stop=True,
                           tile_position=(j * CH, j * CH), skip_group_check=True)
                t.then_inc(S["o_mm"], 1)

            update(0)
            update(1)
            outputs(0)
            pe.wait_ge(full[5], 16)
            wg = slot(5).rearrange("p (c n) -> p c n", c=DC)
            for i in range(1, NCH):
                if i in (1, 3, 5):
                    b = i // 2
                    bank = free_bank(19 + b)
                    row_block(hT, wg, b, bank, range(DC), DC - 1).then_inc(S["proj_mm"], 1)
                if i + 1 < NCH:
                    update(i + 1)
                outputs(i)

            def turn_outputs(b):
                n = ROWS[b]
                pe.wait_ge(S["mixa_ready"], b + 1)
                for c in range(4):
                    t = tr(ps[:, O_BANK[b], c * n:(c + 1) * n], og[0:n, b, c * P:(c + 1) * P], cs(C_ID, n, n))
                t.then_inc(S["mixa_mm"], 1)

            turn_outputs(0)
            turn_outputs(1)
            pe.wait_ge(S["g_ready"], NB)
            for s_, lo in enumerate((PAD + SEQ - PAD, UP - PAD)):
                for cc in range(H):
                    t = tr(ps[0:PAD, 3 + s_, cc * P:(cc + 1) * P], U[:, cc, lo:lo + PAD], ident)
            t.then_inc(S["tail_mm"], 1)
            pe.wait_ge(full[0], 32)
            pe.wait_ge(full[1], 32)
            wout = [slot(6 + n).rearrange("p (c n) -> p c n", c=DC) for n in range(2)]

            def out_first(b):
                if b == 0:
                    pe.wait_ge(S["st_ready"], NCH)
                pe.wait_ge(S["mixa_copied"], b + 1)
                for n in range(2):
                    row_block(mixT, wout[n], b, X_BANK[b][n], range(4), DC - 1)

            out_first(0)
            pe.wait_ge(S["tail_ready"], 2)
            pe.wait_ge(S["conv_ready"], H - 1)
            pe.wait_ge(S["conv_pool"], 1)
            for cc in range(H):
                t = mm(ps[:, 3, 0:T], ones, cacc[:, cc, 0:T], start=(cc == 0), stop=(cc == H - 1))
            t.then_inc(S["mean_mm"], 1)
            turn_outputs(2)
            out_first(1)
            pe.wait_ge(S["csq_ready"], 1)
            for cc in range(H):
                t = mm(ps[:, 4, 0:T], ones, csq[:, cc, :], start=(cc == 0), stop=(cc == H - 1))
            t.then_inc(S["var_mm"], 1)
            out_first(2)
            pe.wait_ge(full[2], 32)
            pe.wait_ge(S["cvar"], 1)
            wple = slot(8)[:, 0:2 * D].rearrange("p (c n) -> p c n", c=2)
            pTc = pT[:, :].rearrange("p (c t) -> p c t", c=2)

            def per_layer(i):
                n, b = divmod(i, NB)
                row_block(pTc, wple[:, :, n * W:(n + 1) * W], b, PL_BANK[i], range(2), 1).then_inc(S["pl_mm"], 1)

            for i in range(4):
                if i >= 2:
                    pe.wait_ge(S["pl_ready"][i - 2], 1)
                per_layer(i)

            TB = ((3, 4), (1, 2), (5, 6))

            def turn_rows(b):
                n = ROWS[b]
                pe.wait_ge(S["x2_ready"], 2 * b + 2)
                for c in range(DC):
                    t = tr(ps[:, TB[b][c // 4], (c % 4) * n:(c % 4 + 1) * n],
                           X2[0:n, b, c * P:(c + 1) * P], cs(C_ID, n, n))
                    if c % 4 == 3:
                        t.then_inc(S["xt2_mm"], 1)

            def router(b):
                n = ROWS[b]
                pe.wait_ge(S["x2_lo"], b + 1)
                pe.wait_ge(S["x2_hi"], b + 1)
                for k in range(DC):
                    t = mm(ps[0:n, 3, b * E:(b + 1) * E], hT[:, k, b * P:b * P + n], wr[:, k * E:(k + 1) * E],
                           start=(k == 0), stop=(k == DC - 1))
                t.then_inc(S["lg_mm"], 1)

            for b in range(NB):
                for n in range(2):
                    if b == 0 and n == 0:
                        for k in range(4, DC - 1):
                            pe.wait_ge(S["mixc_ready"], k - 3)
                            row_block(mixT, wout[n], b, X_BANK[b][n], [k], DC - 1)
                        pe.wait_ge(S["mixc_ready"], H)
                    ks = range(DC - 1 if b == 0 and n == 0 else 4, DC)
                    row_block(mixT, wout[n], b, X_BANK[b][n], ks, DC - 1).then_inc(S["out_mm"], 1)
                if b == 1:
                    for i in (2, 3):
                        pe.wait_ge(S["pl_ready"][i], 1)
                if b:
                    turn_rows(b - 1)
            pe.wait_ge(S["wr_ready"], 1)
            router(0)
            turn_rows(2)
            router(1)
            router(2)
            per_layer(4)
            pe.wait_ge(S["msk_ready"], 1)
            mm(ps[:, 0, 0:4 * E], tri, msk4, start=True, stop=False, skip_group_check=True)
            for b2 in range(NB):
                t = mm(ps[:, 0, (b2 + 1) * E:4 * E].rearrange("p (b e) -> p b e", e=E), ones,
                       msk[:, b2, :].unsqueeze(1).broadcast_to([P, NB - b2, E]),
                       start=False, stop=(b2 == NB - 1), skip_group_check=True)
            t.then_inc(S["pos_mm"], 1)
            per_layer(5)

            G, PP, QQ = 0, 4, 6

            def gather(j):
                pe.wait_ge(S["sel_ready"], j + 1)
                for n in range(2):
                    cols = slice(n * 512, (n + 1) * 512)
                    for b in range(2):
                        for k in range(3):
                            mm(ps[:, PP + n, :], selb[:, b, :], xsb[:, b, k, cols],
                               start=(b == 0 and k == 0), stop=False)
                    mm(ps[:, PP + n, :], selb[0:96, 2, :], xssb[0:96, cols],
                       start=False, stop=True).then_inc(S["gath_mm"], 1)

            def turn_tokens(j):
                for n in range(2):
                    pe.wait_ge(S["gath_ev"], j * 2 + (n + 1))
                    for c in range(4 * n, 4 * n + 4):
                        t = tr(ps[:, PP + n, (c % 4) * P:(c % 4 + 1) * P], gath[:, c * P:(c + 1) * P], ident)
                    t.then_inc(S["xt3_mm"], 1)

            pe.wait_ge(S["xs_l"], NB)
            gather(0)
            turn_tokens(0)
            pe.wait_ge(S["gat_ready"], 1)
            pe.wait_ge(S["pl_ready"][4], 1)
            pe.wait_ge(S["pl_ready"][5], 1)
            for b in range(NB):
                t = tr(ps[0:E, 6, b * P:b * P + ROWS[b]], gat[0:ROWS[b], b, :], cs(C_ID, ROWS[b], ROWS[b]))
            t.then_inc(S["gT_mm"], 1)
            pe.wait_ge(S["bd_in"], 16)
            pe.wait_ge(S["bias_ready"], 1)

            def combine(j, b):
                if b == 0:
                    pe.wait_ge(S["gw_ev"], j + 1)
                    pe.wait_ge(S["y_ev"], j * 2 + 2)
                for n in range(2):
                    if b:
                        pe.wait_ge(S["comb_add"], j * 6 + (2 * b + n - 1))
                    mm(ps[0:ROWS[b], QQ + n, :], gw[:, b * P:b * P + ROWS[b]],
                       ybuf[:, n * 512:(n + 1) * 512], start=True, stop=True).then_inc(S["comb_mm"], 1)

            def step(j):
                pe.wait_ge(S["oneh_ready"], j + 1)
                pe.wait_ge(S["xt_ev"], j * 2 + 2)
                for n in range(4):
                    mm(ps[:, G + n, :], oneh[0:96, :], biasb[0:96, n * 512:(n + 1) * 512],
                       start=True, stop=False, skip_group_check=True)
                for k in range(8):
                    u = LEAD + k
                    pe.wait_ge(full[u % RING], j * (16 * PER // RING) + 16 * (u // RING + 1))
                    w = slot(u).rearrange("p (e n) -> p e n", e=2)
                    for n in (0, 2, 1, 3):
                        for e in range(2):
                            t = mm(ps[e * 64:e * 64 + 64, G + n, :], xT[:, k, e * 64:e * 64 + 64],
                                   w[:, e, n * 512:(n + 1) * 512], start=False, stop=(k == 7),
                                   tile_position=(0, e * 64), skip_group_check=True)
                        if k == 7 and n == 2:
                            t.then_inc(S["half_done"], 1)
                    t.then_inc(S["unit_done"], 1)
                    if k == 1:
                        pe.wait_ge(S["y_ev"], j * 2 + 2)
                        gather(j + 1)
                    elif k == 3:
                        turn_tokens(j + 1)
                    elif k in (4, 5, 6):
                        combine(j, k - 4)
                pe.wait_ge(S["comb_add"], j * 6 + 6)
                for n in range(2):
                    pe.wait_ge(S["hid_ready"], j * 2 + (n + 1))
                    for c in range(4 * n, 4 * n + 4):
                        k, r = c // 2, c % 2
                        t = tr(ps[:, QQ + n, (c % 4) * P:(c % 4 + 1) * P],
                               ubuf[:, 256 * k + r:256 * k + r + 255:2], ident)
                    t.then_inc(S["hidt_mm"], 1)
                pe.wait_ge(S["xt_ev"], j * 2 + 4)
                pe.wait_ge(S["hidt_ev"], j * 2 + 2)
                for k in range(4):
                    u = LEAD + 8 + k
                    pe.wait_ge(full[u % RING], j * (16 * PER // RING) + 16 * (u // RING + 1))
                    w = slot(u).rearrange("p (e c n) -> p e c n", e=2, c=2)
                    for c in range(2):
                        for n in range(2):
                            for e in range(2):
                                t = mm(ps[e * 64:e * 64 + 64, PP + n, :], hidT[:, 2 * k + c, e * 64:e * 64 + 64],
                                       w[:, e, c, n * 512:(n + 1) * 512],
                                       start=(k == 0 and c == 0), stop=(k == 3 and c == 1),
                                       tile_position=(0, e * 64))
                    t.then_inc(S["unit_done"], 1)
                    if k == 1:
                        pe.wait_ge(S["selg_ready"], j + 1)
                        for b in range(NB):
                            t = tr(ps[:, QQ, b * P:b * P + ROWS[b]], selg[0:ROWS[b], b, :],
                                   cs(C_ID, ROWS[b], ROWS[b]))
                        t.then_inc(S["gw_mm"], 1)

            with pe.Fori(0, PAIRS) as j:
                step(j)
            pe.wait_ge(S["table_ready"], 1)
            n_more = pe.value_load(tbl[0:1, 0:1], min_val=0, max_val=MORE)
            with pe.If(n_more > 0):
                with pe.Fori(0, n_more) as i:
                    step(i + PAIRS)
            steps = n_more + PAIRS
            pe.wait_ge(S["gw_ev"], steps + 1)
            pe.wait_ge(S["y_ev"], steps * 2 + 2)
            for i in range(6):
                b, n = i // 2, i % 2
                if b < 2:
                    t = mm(ps[:, i, :], gw[:, b * P:(b + 1) * P], ybuf[:, n * W:(n + 1) * W], start=True, stop=True)
                else:
                    for q in range(4):
                        t = mm(ps[q * DEC:(q + 1) * DEC, i, 0:P], gw[:, SEQ:T],
                               ybuf[:, n * W + q * P:n * W + (q + 1) * P], start=True, stop=True,
                               tile_position=(0, q * DEC))
                t.then_inc(S["comb_mm"], 1)
            for b in range(NB):
                n = ROWS[b]
                if b < 2:
                    pe.wait_ge(S["comb_add"], steps * 6 + (2, 6)[b])
                for c in range(DC):
                    t = tr(ps[:, T3_BANK[2 * b + c // 4], (c % 4) * n:(c % 4 + 1) * n],
                           X2[0:n, b, c * P:(c + 1) * P], cs(C_ID, n, n))
                    if c % 4 == 3:
                        t.then_inc(S["x3t_mm"], 1)
            pe.wait_ge(S["gate_in"], 16 * 4)
            late = slot(LEAD)[:, 0:(DC - EARLY) * W].rearrange("p (c n) -> p c n", n=W)
            for b in range(NB):
                pe.wait_ge(S["h3_ready"], 2 * b + 2)
                row_block(h3T, gate0, b, PG_BANK[2 * b], range(DC), DC - 1).then_inc(S["pg_mm"], 1)
                row_block(h3T, gate1, b, PG_BANK[2 * b + 1], range(EARLY), DC - 1)
                if b == 0:
                    pe.wait_ge(full[LEAD % RING], steps * (16 * PER // RING) + 16 * (LEAD // RING + 1))
                row_block(h3T, late, b, PG_BANK[2 * b + 1], range(EARLY, DC), DC - 1, EARLY
                          ).then_inc(S["pg_mm"], 1)

        @block.scalar
        def _(act):
            fn, copy = nc.scalar.activation, nc.scalar.copy
            act.dma_start(crow, a["cache_conv"][0, 0]).then_inc(S["aux_in"], 16)
            act.dma_start(Ss.rearrange("p (h v) -> p h v", h=H),
                          a["state_hgrn"][0, 0].rearrange("h k v -> k h v")).then_inc(S["aux_in"], 16)
            act.dma_start(brow, a["b_router"].broadcast_to([P, E])).then_inc(S["aux_in"], 16)
            for b in range(NB):
                src = a["p_prompt"][0, 0, b * P:(b + 1) * P, :] if b < 2 else a["p_sample"][0, 0]
                act.dma_start(pr[0:ROWS[b], b, :], src).then_inc(S["p_in"], 16)

            def square(n, b, junk):
                if b or n:
                    act.wait_ge(S["sq"], NB * n + b)
                fn(junk, X2[:, b, :], ACT.Square, accum_out=ss[:, b:b + 1]).then_inc(S["sq"], 1)

            def root(n, b):
                act.wait_ge(S["nvar"], NB * n + b + 1)
                fn(rstd[:, b:b + 1], rstd[:, b:b + 1], ACT.Sqrt).then_inc(S["nsqrt"], 1)

            def gate_chunks(dst, lo, hi, col):
                act.dma_start(dst[:, lo:hi, :], a["w_ple_gate"][0, lo * P:hi * P, col:col + W].rearrange(
                    "(c p) n -> p c n", p=P)).then_inc(S["gate_in"], 16)

            for b in range(NB):
                act.wait_ge(S[f"x_in{b}"], 16)
                if b == 2:
                    act.wait_ge(S["zero_ready"], 1)
                square(0, b, junk1)
                if b:
                    root(0, b - 1)
            root(0, 2)
            act.wait_ge(S["lb_sub"], 1)
            fn(lb_e, lb_e, ACT.Exp).then_inc(S["act"], 1)
            ROUND = (0, 3, 4, 5, 6, 7)

            def rows_out(write, bank, b, n=0):
                if b < 2:
                    return write(slice(0, P), slice(n * W, (n + 1) * W), ps[:, bank, :])
                for q in range(4):
                    ins = write(slice(0, DEC), slice(n * W + q * P, n * W + (q + 1) * P),
                                ps[q * DEC:(q + 1) * DEC, bank, 0:P])
                return ins

            for cc in range(H):
                act.wait_ge(S["proj_mm"], cc + 1)
                fn(h4(kf)[:, cc, :], ps[:, ROUND[cc % 6], 0:T], ACT.Sigmoid).then_inc(S["f_sig"], 1)
            act.wait_ge(S["pt_mm"], 1)
            copy(pT[:, 0:T], ps[:, 1, 0:T])
            copy(pT[:, T:2 * T], ps[:, 2, 0:T])
            copy(U[:, :, PAD + SEQ:PAD + SEQ + PAD],
                 ps[:, 2, T:T + H * PAD].rearrange("p (c t) -> p c t", c=H)).then_inc(S["pt_ready"], 1)
            act.wait_ge(S["f_ready"], 1)
            fn(lev, cf, ACT.Ln).then_inc(S["lnf_ready"], 1)
            act.wait_ge(S["c_ready"], 1)
            fn(Qd, cf, ACT.Exp).then_inc(S["ec_ready"], 1)
            act.wait_ge(S["ed_ready"], 1)
            fn(Kd, lev, ACT.Exp).then_inc(S["edx_ready"], 1)

            def level(l):
                act.wait_ge(S["lev_neg"], l)
                fn(lev, lev, ACT.Exp).then_inc(S["lev_exp"], 1)

            def conv_gate(cc):
                act.wait_ge(S["proj_mm"], 8 + cc + 1)
                fn(h4(ubs)[:, cc, :], ps[:, ROUND[(8 + cc) % 6], 0:T], ACT.Sigmoid).then_inc(S["ubsig_ready"], 1)

            level(1)
            for cc in range(H):
                act.wait_ge(S["proj_mm"], 4 + cc + 1)
                copy(h4(qf)[:, cc, :], ps[:, ROUND[(4 + cc) % 6], 0:T]).then_inc(S["q_ready"], 1)
            for cc in range(H):
                conv_gate(cc)
                level(cc + 2)
            for b in range(NB):
                act.wait_ge(S["kdt_mm"], b + 1)
                if b == 0:
                    act.wait_ge(S["u_ready"], H)
                copy(KdT[0:ROWS[b], b, :], ps[0:ROWS[b], 1 + b % 2, :]).then_inc(S["kdt_ready"], 1)
            cc = H - 1

            def products(lo, hi):
                for i in range(lo, hi):
                    w = 2 * i + 1
                    if i >= APROD:
                        act.wait_ge(S["prod_used"], i - APROD + 1)
                    fn(aprod[i % APROD], U[:, cc, w:w + CV], ACT.Copy,
                       scale=par[:, R_END + w * H + cc:R_END + w * H + cc + 1]).then_inc(S["prod_ready"], 1)

            products(0, APROD)
            for b in range(NB):
                act.wait_ge(S["proj_mm"], 16 + b + 1)
                rows_out(lambda rows, cols, x: copy(v[rows, b, cols], x), ROUND[(16 + b) % 6], b
                         ).then_inc(S["v_ready"], 1)
            products(APROD, CW // 2)
            for b in range(NB):
                act.wait_ge(S["proj_mm"], 19 + b + 1)
                rows_out(lambda rows, cols, x: fn(g[rows, b, cols], x, ACT.Sigmoid), ROUND[(19 + b) % 6], b
                         ).then_inc(S["gsig_ready"], 1)
            for b in range(NB):
                act.wait_ge(S["o_mm"], min(4 * b + 4, NCH))
                n = ROWS[b]
                copy(og[0:n, b, :], ps[0:n, O_BANK[b], :])
                for h in range(H):
                    hs = slice(h * KD, (h + 1) * KD)
                    ins = fn(osq[0:n, b, hs], ps[0:n, O_BANK[b], hs], ACT.Square,
                             accum_out=hss[0:n, b * H + h:b * H + h + 1])
                ins.then_inc(S["osq_ready"], 1)
                act.wait_ge(S["hvar"], b + 1)
                fn(hrs[:, b * H:(b + 1) * H], hrs[:, b * H:(b + 1) * H], ACT.Sqrt).then_inc(S["hsqrt"], 1)
            act.wait_ge(S["tail_mm"], 1)
            for s_ in range(2):
                copy(tails[:, s_ * W:(s_ + 1) * W], ps[0:PAD, 3 + s_, :]).then_inc(S["tail_ready"], 1)
            act.dma_start(wr.rearrange("p (c e) -> p c e", c=DC),
                          a["w_router"][0].rearrange("(c p) e -> p c e", p=P)).then_inc(S["wr_in"], 16)
            act.wait_ge(S["st_ready"], NCH)
            act.dma_start(outs["sp"][0, 0].rearrange("h k v -> k h v"),
                          St[0].rearrange("p (h v) -> p h v", h=H)).then_inc(S["out_done"], 16)
            act.dma_start(outs["ss"][0, 0].rearrange("h k v -> k h v"),
                          So.rearrange("p (h v) -> p h v", h=H)).then_inc(S["out_done"], 16)
            act.wait_ge(S["tail_ready"], 2)
            act.dma_start(outs["cp"][0, 0], tails[:, 0:W]).then_inc(S["out_done"], 16)
            act.dma_start(outs["cs"][0, 0], tails[:, W:2 * W]).then_inc(S["out_done"], 16)
            act.wait_ge(S["mixa_mm"], NB)
            gate_chunks(gate0, FREE, DC, 0)
            gate_chunks(gate1, 0, 3, W)
            act.wait_ge(S["cvar"], 1)
            fn(croot, croot, ACT.Sqrt).then_inc(S["csqrt"], 1)
            act.wait_ge(S["gated"], NB)

            def per_layer(i):
                n, b = divmod(i, NB)
                act.wait_ge(S["pl_mm"], i + 1)
                rows_out(lambda rows, cols, x: copy(ple3[rows, b, cols], x), PL_BANK[i], b, n
                         ).then_inc(S["pl_ready"][i], 1)

            per_layer(0)
            per_layer(1)
            for cc in range(H):
                act.wait_ge(S["cn_ready"], cc + 1)
                fn(csq[:, cc, :], cacc[:, cc, 0:T], ACT.Sigmoid).then_inc(S["csig_ready"], 1)
            act.wait_ge(S["mixc_ready"], H)
            gate_chunks(gate1, 3, EARLY, W)
            act.wait_ge(S["out_done"], 64)
            act.dma_start(ybuf[0:E, :], a["b_down"][0]).then_inc(S["bd_in"], 16)

            def high(b):
                act.wait_ge(S["xn2_ready"], b + 1)
                if b < 2:
                    copy(xsb[:, b, 0, :], xn2[:, b, :]).then_inc(S["xs_h"], 1)
                else:
                    copy(xssb[0:DEC, :], xn2[0:DEC, b, :]).then_inc(S["xs_h"], 1)

            def middle(b):
                act.wait_ge(*((S["xs_rh"], b + 1) if b < 2 else (S["xs_rh_s"], 1)))
                if b < 2:
                    copy(xsb[:, b, 1, :], xn2[:, b, :]).then_inc(S["xs_m"], 1)
                else:
                    copy(mtmp, xn2[0:DEC, b, :]).then_inc(S["xs_m"], 1)

            def low(b):
                act.wait_ge(*((S["xs_rm"], b + 1) if b < 2 else (S["xs_rm_s"], 1)))
                if b < 2:
                    copy(xsb[:, b, 2, :], xn2[:, b, :]).then_inc(S["xs_l"], 1)
                else:
                    copy(xssb[2 * DEC:3 * DEC, :], xn2[0:DEC, b, :]).then_inc(S["xs_l"], 1)

            def tokens_hi(b):
                n = ROWS[b]
                act.wait_ge(S["xt2_mm"], 2 * b + 2)
                copy(hT[:, 4:8, b * P:b * P + n], ps[:, ((3, 4), (1, 2), (5, 6))[b][1], 0:4 * n].rearrange(
                    "p (c t) -> p c t", c=4)).then_inc(S["x2_hi"], 1)

            def square_of(b):
                act.wait_ge(S["x2_ready"], 2 * b + 2)
                square(1, b, junk2)

            square_of(0)
            root(1, 0)
            high(0)
            middle(0)
            tokens_hi(0)
            square_of(1)
            low(0)
            square_of(2)
            root(1, 1)
            tokens_hi(1)
            tokens_hi(2)
            root(1, 2)
            high(1)
            high(2)
            middle(1)
            middle(2)
            act.wait_ge(S["xs_m"], NB)
            copy(xssb[DEC:2 * DEC, :], mtmp)
            low(1)
            low(2)
            act.wait_ge(S["top_ready"], 1)
            for b in range(NB):
                fn(wts[:, b, :], top[:, b, 0:TOPK], ACT.Exp, bias=ntop[:, b:b + 1],
                   accum_out=wsum[:, b:b + 1]).then_inc(S["wexp"], 1)

            def copy_gathered(j):
                for n in range(2):
                    act.wait_ge(S["gath_mm"], j * 2 + (n + 1))
                    copy(gath[:, n * 512:(n + 1) * 512], ps[:, 4 + n, :]).then_inc(S["gath_ev"], 1)

            per_layer(4)
            per_layer(5)
            act.wait_ge(S["lg_mm"], NB)
            gate_chunks(gate0, 0, FREE, 0)
            copy_gathered(0)
            act.wait_ge(S["gT_mm"], 1)
            act.wait_ge(S["gw_zero"], 1)
            copy(gw[0:E, :], ps[0:E, 6, 0:T]).then_inc(S["gw_ev"], 1)

            def step(j):
                copy_gathered(j + 1)
                for n in range(2):
                    act.wait_ge(S["gate_ready"], j * 2 + (n + 1))
                    cols = slice(n * 512, (n + 1) * 512)
                    fn(sgm[:, cols], gbuf[:, cols], ACT.Sigmoid, scale=ALPHA).then_inc(S["sig_ready"], 1)
                for n in range(2):
                    act.wait_ge(S["hidt_mm"], j * 2 + (n + 1))
                    copy(hidT[:, 4 * n:4 * n + 4, :],
                         ps[:, 6 + n, :].rearrange("p (c s) -> p c s", c=4)).then_inc(S["hidt_ev"], 1)
                act.wait_ge(S["unit_done"], j * PER + PER)
                for n in range(2):
                    copy(ybuf[:, n * 512:(n + 1) * 512], ps[:, 4 + n, :]).then_inc(S["y_ev"], 1)

            with act.Fori(0, PAIRS) as j:
                step(j)
            act.wait_ge(S["table_ready"], 1)
            n_more = act.value_load(tbl[0:1, 0:1], min_val=0, max_val=MORE)
            with act.If(n_more > 0):
                with act.Fori(0, n_more) as i:
                    step(i + PAIRS)
            steps = n_more + PAIRS
            for b in range(NB):
                act.wait_ge(S["comb_add"], steps * 6 + (2 * b + 2))
                square(2, b, junk3)
            for b in range(NB):
                root(2, b)

            def gate_rows(b):
                for n in range(2):
                    act.wait_ge(S["pg_mm"], 2 * b + n + 1)
                    bank = PG_BANK[2 * b + n]
                    if b < 2:
                        ins = fn(sg[:, b, n * W:(n + 1) * W], ps[:, bank, :], ACT.Sigmoid, scale=rstd[:, b:b + 1])
                    else:
                        for q in range(4):
                            rows = slice(q * DEC, (q + 1) * DEC)
                            ins = fn(sg[0:DEC, b, n * W + q * P:n * W + (q + 1) * P], ps[rows, bank, 0:P],
                                     ACT.Sigmoid, scale=rs4[rows, 0:1])
                    ins.then_inc(S["pg_sig"], 1)

            def square_last(b):
                act.wait_ge(S["x4_ready"], 2 * b + 2)
                square(3, b, junk3)

            act.wait_ge(S["rs4_ready"], 1)
            gate_rows(0)
            square_last(0)
            root(3, 0)
            gate_rows(1)
            square_last(1)
            gate_rows(2)
            square_last(2)
            root(3, 1)
            root(3, 2)
            act.wait_ge(S["last_rstd"], 1)
            act.wait_ge(S["y_scaled"], 2)
            fn(sg[:, 1, :], sg[:, 1, :], ACT.Copy, scale=rstd[:, 1:2]).then_inc(S["y_ready1"], 1)

        @block.gpsimd
        def _(pool):
            own = Own(pool, S["pool"])
            link = own.link
            pool.wait_ge(S["raw_in"], 48)
            for n in range(2):
                cols = slice(n * D, (n + 1) * D)
                raw = braw[:, cols]
                link(nc.gpsimd.tensor_copy(biasb[0:96, cols], raw))
                link(nc.gpsimd.tensor_tensor(bres, raw, biasb[0:96, cols], ALU.subtract))
                link(nc.gpsimd.tensor_copy(biasb[E:2 * E, cols], bres[E:2 * E, :]))
                link(nc.gpsimd.tensor_copy(biasb[2 * E:3 * E, cols], bres[2 * E:3 * E, :]))
                link(nc.gpsimd.tensor_tensor(bres[2 * E:3 * E, :], bres[2 * E:3 * E, :], biasb[2 * E:3 * E, cols],
                                             ALU.subtract))
                last = nc.gpsimd.tensor_copy(biasb[2 * E:3 * E, cols], bres[2 * E:3 * E, :])
                if n == 0:
                    link(last)
                else:
                    last.then_inc(S["bias_ready"], 1)
            for l in range(1, NLEV):
                pool.wait_ge(S["lev_exp"], l)
                if l == 1:
                    pool.wait_ge(S["bias_ready"], 1)
                else:
                    pool.wait_ge(S["lev_mm"], l)
                    pool.wait_ge(S["lev_k"], l - 1)
                nc.gpsimd.tensor_tensor(lk, kf, lev, ALU.mult).then_inc(S["lev_k"], 1)
            pool.wait_ge(S["lev_k"], NLEV - 1)
            pool.wait_ge(S["u_ready"], H)
            pool.wait_ge(S["pt_ready"], 1)
            G, cc = nc.gpsimd, H - 1
            for w in range(CW):
                tap = par[:, R_END + w * H + cc:R_END + w * H + cc + 1]
                if w == 0:
                    link(G.tensor_scalar(cacc[:, cc, :], U[:, cc, 0:CV], tap, pcol(R_CB + cc, 1),
                                         ALU.mult, ALU.add))
                    continue
                if w % 2:
                    i = w // 2
                    pool.wait_ge(S["prod_ready"], i + 1)
                    G.tensor_tensor(cacc[:, cc, :], cacc[:, cc, :], aprod[i % APROD], ALU.add
                                    ).then_inc(S["prod_used"], 1)
                    pool.wait_ge(S["prod_used"], i + 1)
                    continue
                link(G.tensor_scalar(prod, U[:, cc, w:w + CV], tap, None, ALU.mult))
                if w < CW - 1:
                    link(G.tensor_tensor(cacc[:, cc, :], cacc[:, cc, :], prod, ALU.add))
                else:
                    G.tensor_tensor(cacc[:, cc, 0:SEQ], cacc[:, cc, 0:SEQ], prod[:, 0:SEQ], ALU.add)
                    G.tensor_tensor(cacc[:, cc, SEQ:T], cacc[:, cc, CV - DEC:CV], prod[:, CV - DEC:CV], ALU.add
                                    ).then_inc(S["conv_pool"], 1)
            pool.wait_ge(S["conv_pool"], 1)
            rest = xn2[0:DEC, 2, :]
            pool.wait_ge(S["xs_h"], NB)
            G.tensor_tensor(rest, rest, xssb[0:DEC, :], ALU.subtract).then_inc(S["xs_rh_s"], 1)
            pool.wait_ge(S["xs_rh_s"], 1)
            pool.wait_ge(S["xs_m"], NB)
            G.tensor_tensor(rest, rest, mtmp, ALU.subtract).then_inc(S["xs_rm_s"], 1)

        @block.vector
        def _(dve):
            V = nc.vector
            own = Own(dve, S["dve"])
            link = own.link

            def zero_rest(x):
                V.memset(x[DEC:64], 0.0)
                return V.memset(x[64:P], 0.0)

            zero_rest(X2[:, 2, :]).then_inc(S["zero_ready"], 1)
            V.memset(hss, 0.0)
            V.memset(msk4[:, NB * E:4 * E], 0.0)

            def mean(n, b):
                dve.wait_ge(S["sq"], NB * n + b + 1)
                V.tensor_scalar(rstd[:, b:b + 1], ss[:, b:b + 1], 1.0 / D, EPS, ALU.mult, ALU.add
                                ).then_inc(S["nvar"], 1)

            def invert(n, b):
                dve.wait_ge(S["nsqrt"], NB * n + b + 1)
                link(V.reciprocal(rstd[:, b:b + 1], rstd[:, b:b + 1]))

            for b in range(NB):
                mean(0, b)
                if b:
                    invert(0, b - 1)
                    V.tensor_scalar(xn[:, b - 1, :], X2[:, b - 1, :], rstd[:, b - 1:b], None, ALU.mult
                                    ).then_inc(S["xn_ready"], 1)
            invert(0, 2)
            V.tensor_scalar(xn[:, 2, :], X2[:, 2, :], rstd[:, 2:3], None, ALU.mult).then_inc(S["xn_ready"], 1)
            dve.wait_ge(S["par_mm"], 1)
            V.tensor_copy(par[:, 0:R_END], ps[:, 0, 0:R_END])
            link(V.tensor_copy(par[:, R_END:R_END + CW * H], ps[:, 0, 64:64 + CW * H]))
            link(V.tensor_tensor(lb_m, pcol(R_LB, H), pcol(R_LB + H, H), ALU.max))
            V.tensor_tensor(blocks(lb_e, 2), blocks(pcol(R_LB, 2 * H), 2),
                            lb_m.unsqueeze(1).broadcast_to([P, 2, H]), ALU.subtract).then_inc(S["lb_sub"], 1)

            def columns_with_gain(dst, b, done, ready, banks, gain):
                for n in range(2):
                    t = ROWS[b]
                    dve.wait_ge(S[done], 2 * b + n + 1)
                    V.tensor_tensor(dst[:, 4 * n:4 * n + 4, b * P:b * P + t],
                                    ps[:, banks[2 * b + n], 0:4 * t].rearrange("p (c t) -> p c t", c=4),
                                    by_token(gain + 4 * n, 4, t), ALU.mult).then_inc(S[ready], 1)

            for b in range(NB):
                columns_with_gain(hT, b, "xt_mm", "ht_ready", (2, 3, 4, 5, 6, 7), R_MIX)
            dve.wait_ge(S["act"], 1)
            link(V.tensor_tensor(lb_m, lb_e[:, 0:H], lb_e[:, H:2 * H], ALU.add))
            link(V.reciprocal(lb_m, lb_m))
            link(V.tensor_tensor(lbt, lb_e[:, 0:H], lb_m, ALU.mult))
            link(V.tensor_scalar(oml, lbt, -1.0, 1.0, ALU.mult, ALU.add))
            V.memset(U[:, :, 0:PAD], 0.0)
            link(V.memset(reset, 1.0))
            link(V.memset(reset[:, 0:H * T:CH], 0.0))
            for cc in range(H):
                dve.wait_ge(S["f_sig"], cc + 1)
                ins = V.tensor_scalar(h4(kf)[:, cc, :], h4(kf)[:, cc, :], oml[:, cc:cc + 1], lbt[:, cc:cc + 1],
                                      ALU.mult, ALU.add)
            link(ins)
            V.tensor_scalar(cf, kf, TINY, None, ALU.max).then_inc(S["f_ready"], 1)
            V.tensor_scalar(kf, kf, -1.0, 1.0, ALU.mult, ALU.add)
            dve.wait_ge(S["lnf_ready"], 1)
            V.tensor_tensor_scan(cf, reset, lev, 0.0, ALU.mult, ALU.add).then_inc(S["c_ready"], 1)
            dve.wait_ge(S["c_ready"], 1)
            by_chunk = cf.rearrange("p (i t) -> p i t", t=CH)
            V.tensor_tensor(lev.rearrange("p (i t) -> p i t", t=CH),
                            by_chunk[:, :, CH - 1:CH].broadcast_to([P, H * NCH, CH]), by_chunk, ALU.subtract
                            ).then_inc(S["ed_ready"], 1)

            def exponents(l):
                m = HALVES[l - 1]
                if l == 1:
                    dve.wait_ge(S["edx_ready"], 1)
                else:
                    dve.wait_ge(S["lev_k"], l - 1)
                    dve.wait_ge(S["lev_q"], l - 1)
                c, e = (x.rearrange("p (i t) -> p i t", t=2 * m) for x in (cf, lev))
                middle = c[:, :, m - 1:m].broadcast_to([P, H * T // (2 * m), m])
                V.tensor_tensor(e[:, :, 0:m], middle, c[:, :, 0:m], ALU.subtract)
                V.tensor_tensor(e[:, :, m:2 * m], c[:, :, m:2 * m], middle, ALU.subtract
                                ).then_inc(S["lev_neg"], 1)

            def level_q(l):
                dve.wait_ge(S["lev_exp"], l)
                if l >= 2:
                    dve.wait_ge(S["lev_mm"], l)
                else:
                    dve.wait_ge(S["bias_ready"], 1)
                V.tensor_tensor(lq, qf, lev, ALU.mult).then_inc(S["lev_q"], 1)

            def masked(l):
                dve.wait_ge(S["lev_mm"], l + 1)
                if l:
                    dve.wait_ge(S["lev_done"], l)
                raw = ps[:, 1 + l % 2, 0:NB * H * CH].rearrange("p (b h t) -> p b h t", b=NB, h=H)
                mask = cs(C_MASK + l * CH, CH)
                for lo, n, rows in ((0, 2, P), (2, 1, DEC)):
                    dst = (score if l == 0 else stmp)[0:rows, lo:lo + n]
                    ins = V.tensor_tensor(dst, raw[0:rows, lo:lo + n],
                                          mask[0:rows].unsqueeze(1).unsqueeze(1).broadcast_to([rows, n, H, CH]),
                                          ALU.mult)
                if l == 0:
                    ins.then_inc(S["lev_done"], 1)
                    return
                link(ins)
                V.tensor_tensor(score[:, 0:2], score[:, 0:2], stmp[:, 0:2], ALU.add)
                V.tensor_tensor(score[0:DEC, 2], score[0:DEC, 2], stmp[0:DEC, 2], ALU.add
                                ).then_inc(S["lev_done"], 1)

            exponents(1)
            V.tensor_tensor(Kd, Kd, kf, ALU.mult).then_inc(S["kd_ready"], 1)
            link(V.tensor_copy(dec, h4(Qd)[:, :, CH - 1:T:CH]))
            dve.wait_ge(S["q_ready"], H)
            V.tensor_tensor(Qd, Qd, qf, ALU.mult).then_inc(S["qd_ready"], 1)
            level_q(1)
            masked(0)
            exponents(2)
            for l in (2, 3, 4):
                level_q(l)
                exponents(l + 1)
                masked(l - 1)

            level_q(5)
            masked(4)
            masked(5)

            for cc in range(H):
                bank = (0, 3, 4, 5, 6, 7)[(12 + cc) % 6]
                dve.wait_ge(S["ubsig_ready"], cc + 1)
                dve.wait_ge(S["proj_mm"], 12 + cc + 1)
                V.tensor_tensor(U[:, cc, PAD:PAD + SEQ], ps[:, bank, 0:SEQ], h4(ubs)[:, cc, 0:SEQ], ALU.mult)
                V.tensor_tensor(U[:, cc, UP - DEC:UP], ps[:, bank, SEQ:T], h4(ubs)[:, cc, SEQ:T], ALU.mult
                                ).then_inc(S["u_ready"], 1)
            dve.wait_ge(S["pt_ready"], 1)
            dve.wait_ge(S["u_ready"], H)
            taps_done = {}

            def taps(lo, hi):
                convolve(V, own, range(H - 1), range(lo, hi), U, cacc, par, taps_done, S["conv_ready"])

            def state(i):
                last = i == NCH - 1
                old, new = (Ss, So) if last else (St[i % 2], St[(i + 1) % 2])
                up = ps[:, 1 + i % 2, :]
                dve.wait_ge(S["um_mm"], i + 1)
                if i == 0:
                    dve.wait_ge(S["bias_ready"], 1)
                    V.tensor_copy(new, up).then_inc(S["st_ready"], 1)
                    return
                if i >= 2:
                    dve.wait_ge(S["o_mm"], i)
                dve.wait_ge(S["st_ready"], i)
                for h in range(H):
                    hs = slice(h * KD, (h + 1) * KD)
                    ins = V.scalar_tensor_tensor(out=new[:, hs], in0=old[:, hs], scalar=dec[:, h, i:i + 1],
                                                 in1=up[:, hs], op0=ALU.mult, op1=ALU.add)
                ins.then_inc(S["st_ready"], 1)

            def gate(b):
                bank = (0, 3, 4, 5, 6, 7)[(19 + b) % 6]
                dve.wait_ge(S["gsig_ready"], b + 1)
                if b < 2:
                    ins = V.tensor_tensor(g[:, b, :], ps[:, bank, :], g[:, b, :], ALU.mult)
                else:
                    for q in range(4):
                        x = g[0:DEC, b, q * P:(q + 1) * P]
                        ins = V.tensor_tensor(x, ps[q * DEC:(q + 1) * DEC, bank, 0:P], x, ALU.mult)
                ins.then_inc(S["g_ready"], 1)

            def gated(b):
                n = ROWS[b]
                mine = hrs[:, b * H:(b + 1) * H]
                dve.wait_ge(S["osq_ready"], b + 1)
                V.tensor_scalar(mine, hss[:, b * H:(b + 1) * H], 1.0 / KD, EPS, ALU.mult, ALU.add
                                ).then_inc(S["hvar"], 1)
                V.tensor_tensor(og[0:n, b, :], og[0:n, b, :], g[0:n, b, :], ALU.mult).then_inc(S["gated"], 1)

            def over_root(b):
                n = ROWS[b]
                mine = hrs[:, b * H:(b + 1) * H]
                dve.wait_ge(S["hsqrt"], b + 1)
                link(V.reciprocal(mine, mine))
                dve.wait_ge(S["gated"], b + 1)
                x = og[0:n, b, :].rearrange("p (h n) -> p h n", h=H)
                V.tensor_tensor(x, x, mine[0:n].unsqueeze(2).broadcast_to([n, H, KD]), ALU.mult
                                ).then_inc(S["mixa_ready"], 1)

            def outputs_gain(b):
                n = ROWS[b]
                dve.wait_ge(S["mixa_mm"], b + 1)
                V.tensor_tensor(mixT[:, 0:4, b * P:b * P + n],
                                ps[:, O_BANK[b], 0:4 * n].rearrange("p (c t) -> p c t", c=4),
                                by_token(R_HN, H, n), ALU.mult).then_inc(S["mixa_copied"], 1)

            at_tap = 14
            taps(0, at_tap)
            for i in range(NCH - 1):
                state(i)
                more = (2, 4, 1, 3, 1, 2, 1, 1)[i]
                taps(at_tap, at_tap + more)
                at_tap += more
                if i in (3, 5, 7):
                    gate(i // 2 - 1)
            gated(0)
            state(NCH - 1)
            gated(1)
            over_root(0)
            over_root(1)
            taps(at_tap, CW - 1)
            outputs_gain(0)
            outputs_gain(1)
            gated(2)
            taps(CW - 1, CW)
            over_root(2)
            dve.wait_ge(S["wr_in"], 16)
            wrc = wr.rearrange("p (c e) -> p c e", c=DC)
            V.tensor_tensor(wrc, wrc, by_token(R_FFN, DC, E), ALU.mult).then_inc(S["wr_ready"], 1)
            dve.wait_ge(S["out_done"], 64)
            dve.wait_ge(S["conv_pool"], 1)
            V.memset(gw[E:2 * E, :], 0.0)
            V.memset(gw[2 * E:P, :], 0.0).then_inc(S["gw_zero"], 1)
            V.memset(ybuf[E:2 * E, :], 0.0).then_inc(S["y_ev"], 1)
            V.memset(ybuf[2 * E:P, :], 0.0).then_inc(S["y_ev"], 1)
            cv = cacc[:, :, 0:T]
            dve.wait_ge(S["conv_ready"], H - 1)
            dve.wait_ge(S["mean_mm"], 1)
            link(V.scalar_tensor_tensor(out=cv, in0=ps[:, 3, 0:T].unsqueeze(1).broadcast_to([P, H, T]),
                                        scalar=-1.0 / W, in1=cv, op0=ALU.mult, op1=ALU.add))
            dve.wait_ge(S["tail_mm"], 1)
            V.tensor_tensor(csq, cv, cv, ALU.mult).then_inc(S["csq_ready"], 1)
            outputs_gain(2)
            dve.wait_ge(S["var_mm"], 1)
            V.tensor_scalar(croot, ps[:, 4, 0:T], 1.0 / W, EPS, ALU.mult, ALU.add).then_inc(S["cvar"], 1)
            dve.wait_ge(S["csqrt"], 1)
            link(V.reciprocal(croot, croot))
            link(V.tensor_tensor(cv, cv, croot.unsqueeze(1).broadcast_to([P, H, T]), ALU.mult))
            for cc in range(H):
                V.tensor_scalar(cv[:, cc, :], cv[:, cc, :], pcol(R_LG + cc, 1), pcol(R_LBI + cc, 1),
                                ALU.mult, ALU.add).then_inc(S["cn_ready"], 1)
            dve.wait_ge(S["gated"], NB)
            dve.wait_ge(S["pl_mm"], 3)
            for q in range(4):
                ins = V.tensor_copy(ple3[0:DEC, 2, q * P:(q + 1) * P], ps[q * DEC:(q + 1) * DEC, 3, 0:P])
            ins.then_inc(S["pl_ready"][2], 1)
            dve.wait_ge(S["pl_mm"], 4)
            V.tensor_copy(ple3[:, 0, W:2 * W], ps[:, 4, :]).then_inc(S["pl_ready"][3], 1)
            for cc in range(H):
                dve.wait_ge(S["csig_ready"], cc + 1)
                V.tensor_tensor(mixT[:, 4 + cc, :], cv[:, cc, :], csq[:, cc, :], ALU.mult
                                ).then_inc(S["mixc_ready"], 1)

            def residual(b):
                for n in range(2):
                    bank = X_BANK[b][n]
                    dve.wait_ge(S["out_mm"], 2 * b + n + 1)
                    if b < 2:
                        x = X2[:, b, n * W:(n + 1) * W]
                        ins = V.tensor_tensor(x, ps[:, bank, :], x, ALU.add)
                    else:
                        for q in range(4):
                            x = X2[0:DEC, b, n * W + q * P:n * W + (q + 1) * P]
                            ins = V.tensor_tensor(x, ps[q * DEC:(q + 1) * DEC, bank, 0:P], x, ALU.add)
                    ins.then_inc(S["x2_ready"], 1)

            def normalise(b):
                invert(1, b)
                V.tensor_scalar(xn2[:, b, :], X2[:, b, :], rstd[:, b:b + 1], None, ALU.mult
                                ).then_inc(S["xn2_ready"], 1)

            def tokens_lo(b):
                n = ROWS[b]
                dve.wait_ge(S["xt2_mm"], 2 * b + 1)
                V.tensor_copy(hT[:, 0:4, b * P:b * P + n],
                              ps[:, (3, 1, 5)[b], 0:4 * n].rearrange("p (c t) -> p c t", c=4)
                              ).then_inc(S["x2_lo"], 1)

            def remainder(b, k):
                dve.wait_ge(S[("xs_h", "xs_m")[k]], b + 1)
                V.tensor_tensor(xn2[:, b, :], xn2[:, b, :], xsb[:, b, k, :], ALU.subtract
                                ).then_inc(S[("xs_rh", "xs_rm")[k]], 1)

            residual(0)
            mean(1, 0)
            normalise(0)
            remainder(0, 0)
            residual(1)
            tokens_lo(0)
            remainder(0, 1)
            residual(2)
            mean(1, 1)
            mean(1, 2)
            tokens_lo(1)
            tokens_lo(2)
            normalise(1)
            normalise(2)
            remainder(1, 0)
            zero_rest(lg[:, 2, :])
            dve.wait_ge(S["lg_mm"], NB)
            for b in range(NB):
                n = ROWS[b]
                ins = V.scalar_tensor_tensor(out=lg[0:n, b, :], in0=ps[0:n, 3, b * E:(b + 1) * E],
                                             scalar=rstd[0:n, b:b + 1], in1=brow[0:n, :],
                                             op0=ALU.mult, op1=ALU.add)
            link(ins)
            for b in range(NB):
                ins = V.max(top[:, b, :], lg[:, b, :])
            link(ins)
            V.tensor_scalar(ntop, top[:, :, 0], -1.0, None, ALU.mult).then_inc(S["top_ready"], 1)
            for b in range(NB):
                ins = V.max_index(topi[:, b, :], top[:, b, :], lg[:, b, :])
            link(ins)
            link(V.tensor_copy(topf, topi))
            chosen = selg.rearrange("p b (k e) -> p b k e", k=TOPK)
            link(V.tensor_tensor(chosen, cs(C_IOTA, E).unsqueeze(1).unsqueeze(1).broadcast_to([P, NB, TOPK, E]),
                                 topf[:, :, 0:TOPK].unsqueeze(3).broadcast_to([P, NB, TOPK, E]), ALU.is_equal))
            link(V.tensor_reduce(msk, chosen.rearrange("p b k e -> p b e k"), AX, ALU.add))
            zero_rest(msk[:, 2, :]).then_inc(S["msk_ready"], 1)
            remainder(1, 1)
            dve.wait_ge(S["pos_mm"], 1)
            link(V.scalar_tensor_tensor(out=htmp, in0=ps[:, 0, 0:NB * E].rearrange("p (b e) -> p b e", b=NB),
                                        scalar=1.0, in1=msk, op0=ALU.add, op1=ALU.mult))
            link(V.tensor_scalar(posm[:, :, 0:E], htmp, -1.0, None, ALU.add))
            V.tensor_copy(posm[DEC:2 * DEC, 2, 0:E], posm[0:DEC, 2, 0:E])
            link(V.tensor_copy(posm[2 * DEC:3 * DEC, 2, 0:E], posm[0:DEC, 2, 0:E]))
            link(V.tensor_copy(cnt, ps[:, 0, NB * E:NB * E + E]))

            iota_s = cs(C_IOTA, SLOTS).unsqueeze(1).broadcast_to([P, NB * 2, SLOTS])

            def per_slot(x):
                return x.rearrange("p b e -> p (b e)").unsqueeze(2).broadcast_to([P, NB * 2, SLOTS])

            def columns_of(pair2, x):
                return x[:, :, bass.ds(pair2, 2)]

            def place(out, pair2, offset):
                if offset is None:
                    return V.tensor_copy(out, columns_of(pair2, posm))
                return V.tensor_scalar(out, columns_of(pair2, posm), offset, None, ALU.subtract)

            FIRST = 0

            def select(j, pair2, offset):
                if pair2 is not FIRST:
                    dve.wait_ge(S["gath_mm"], j * 2)
                place(cur, pair2, offset).then_inc(S["sel_cur"], 1)
                dve.wait_ge(S["sel_cur"], j + 1)
                V.tensor_tensor(selb.rearrange("p b (e s) -> p (b e) s", e=2), iota_s, per_slot(cur),
                                ALU.is_equal).then_inc(S["sel_ready"], 1)

            def select_bias(j, pair2):
                V.tensor_copy(oneh[0:96, :].rearrange("p (e s) -> p e s", e=2),
                              eye[0:96, bass.ds(pair2, 2)].unsqueeze(2).broadcast_to([96, 2, SLOTS])
                              ).then_inc(S["oneh_ready"], 1)

            def weigh(j, pair2, offset):
                place(curg, pair2, offset)
                V.tensor_copy(curw, columns_of(pair2, gat)).then_inc(S["selg_cur"], 1)
                dve.wait_ge(S["selg_cur"], j * 2 + 1)
                sel = selg.rearrange("p b (e s) -> p (b e) s", e=2)
                V.tensor_tensor(sel, iota_s, per_slot(curg), ALU.is_equal).then_inc(S["selg_cur"], 1)
                dve.wait_ge(S["selg_cur"], j * 2 + 2)
                V.tensor_tensor(sel, sel, per_slot(curw), ALU.mult).then_inc(S["selg_ready"], 1)

            def tokens_out(j):
                for n in range(2):
                    dve.wait_ge(S["xt3_mm"], j * 2 + (n + 1))
                    V.tensor_tensor(xT[:, 4 * n:4 * n + 4, :],
                                    ps[:, 4 + n, :].rearrange("p (c s) -> p c s", c=4),
                                    by_token(R_FFN + 4 * n, 4, P), ALU.mult).then_inc(S["xt_ev"], 1)

            select(0, FIRST, None)
            select_bias(0, 0)
            dve.wait_ge(S["wexp"], NB)
            link(V.reciprocal(wsum, wsum))
            link(V.tensor_tensor(wts, wts, wsum.unsqueeze(2).broadcast_to([P, NB, TOPK]), ALU.mult))
            link(V.tensor_tensor(chosen, chosen, wts.unsqueeze(3).broadcast_to([P, NB, TOPK, E]), ALU.mult))
            link(V.tensor_reduce(gat, chosen.rearrange("p b k e -> p b e k"), AX, ALU.add))
            zero_rest(gat[:, 2, :]).then_inc(S["gat_ready"], 1)
            tokens_out(0)
            link(V.tensor_tensor(pmax, cnt[:, 0:E:2], cnt[:, 1:E:2], ALU.max))
            for b in range(OVER):
                ins = V.tensor_scalar(over[:, b * PAIRS:(b + 1) * PAIRS], pmax, float(SLOTS * (b + 1)), None,
                                      ALU.is_gt)
            link(ins)
            link(V.tensor_reduce(lst[:, 0:1], over, AX, ALU.add))
            V.tensor_copy(tbl[:, 0:1], lst[:, 0:1])
            link(V.tensor_tensor(over, over, cs(C_OVER, OVER * PAIRS), ALU.mult))
            for r in range(LIST // 8):
                link(V.max(lst[:, 8 * r:8 * r + 8], over))
                if r < LIST // 8 - 1:
                    link(V.match_replace(over, lst[:, 8 * r:8 * r + 8], over, 0.0))
            link(V.tensor_scalar(lcode, lst, -1.0, float(OVER * PAIRS), ALU.mult, ALU.add))
            link(V.tensor_scalar(lblk, lcode, float(PAIRS), None, ALU.is_ge))
            for q in range(2, OVER + 1):
                link(V.scalar_tensor_tensor(out=lblk, in0=lcode, scalar=float(PAIRS * q), in1=lblk,
                                            op0=ALU.is_ge, op1=ALU.add))
            link(V.scalar_tensor_tensor(out=lcode, in0=lblk, scalar=-float(PAIRS), in1=lcode,
                                        op0=ALU.mult, op1=ALU.add))
            link(V.tensor_scalar(lblk, lblk, float(SLOTS), float(SLOTS), ALU.mult, ALU.add))
            V.tensor_scalar(tbl[:, 1:1 + LIST], lcode, 2.0, None, ALU.mult).then_inc(S["table_ready"], 1)
            dve.wait_ge(S["table_ready"], 1)
            first = dve.value_load(tbl[0:1, 1:2], min_val=0, max_val=E - 2)
            place(posm[:, :, E:E + 2], first, lblk[:, 0:1])
            link(V.tensor_copy(eye[0:96, E:E + 2], eye[0:96, bass.ds(first, 2)]))

            def step(j, this, following):
                select(j + 1, *following)
                dve.wait_ge(S["unit_done"], j * PER + 1)
                select_bias(j + 1, following[0])
                weigh(j, *this)
                add_outputs(j)
                halves = [slice(n * 512, (n + 1) * 512) for n in range(2)]

                def clamp(n):
                    cols = halves[n]
                    if n == 0:
                        dve.wait_ge(S["half_done"], j + 1)
                    else:
                        dve.wait_ge(S["unit_done"], j * PER + 8)
                    V.tensor_scalar(gbuf[:, cols], ps[:, n, :], LIMIT, None, ALU.min).then_inc(S["gate_ready"], 1)
                    V.tensor_scalar(ubuf[:, cols], ps[:, 2 + n, :], LIMIT, -LIMIT, ALU.min, ALU.max
                                    ).then_inc(S["up_ready"], 1)

                def swish(n):
                    cols = halves[n]
                    dve.wait_ge(S["sig_ready"], j * 2 + (n + 1))
                    V.tensor_tensor(gbuf[:, cols], gbuf[:, cols], sgm[:, cols], ALU.mult).then_inc(S["gs_ready"], 1)

                def hidden(n):
                    cols = halves[n]
                    dve.wait_ge(S["gs_ready"], j * 2 + (n + 1))
                    dve.wait_ge(S["up_ready"], j * 2 + (n + 1))
                    V.scalar_tensor_tensor(out=ubuf[:, cols], in0=ubuf[:, cols], scalar=1.0, in1=gbuf[:, cols],
                                           op0=ALU.add, op1=ALU.mult).then_inc(S["hid_ready"], 1)

                clamp(0)
                swish(0)
                clamp(1)
                hidden(0)
                swish(1)
                hidden(1)
                tokens_out(j + 1)
                dve.wait_ge(S["gw_mm"], j + 1)
                V.tensor_copy(gw, ps[:, 6, 0:T]).then_inc(S["gw_ev"], 1)

            def add_outputs(j):
                for i in range(6):
                    b, n = i // 2, i % 2
                    x = X2[0:ROWS[b], b, n * 512:(n + 1) * 512]
                    dve.wait_ge(S["comb_mm"], j * 6 + (i + 1))
                    V.tensor_tensor(x, ps[0:ROWS[b], 6 + n, :], x, ALU.add).then_inc(S["comb_add"], 1)

            with dve.Fori(0, PAIRS) as j:
                step(j, (j * 2, None), (j * 2 + 2, None))
            n_more = dve.value_load(tbl[0:1, 0:1], min_val=0, max_val=MORE)
            with dve.If(n_more > 0):
                with dve.Fori(0, n_more) as i:
                    now = dve.value_load(tbl[0:1, bass.ds(i + 1, 1)], min_val=0, max_val=E - 2)
                    then = dve.value_load(tbl[0:1, bass.ds(i + 2, 1)], min_val=0, max_val=E - 2)
                    step(i + PAIRS, (now, lblk[:, bass.ds(i, 1)]), (then, lblk[:, bass.ds(i + 1, 1)]))
            steps = n_more + PAIRS
            for i in range(6):
                b, n = i // 2, i % 2
                x = X2[0:ROWS[b], b, n * 512:(n + 1) * 512]
                dve.wait_ge(S["comb_mm"], steps * 6 + (i + 1))
                if b < 2:
                    ins = V.tensor_tensor(x, ps[:, i, :], x, ALU.add)
                else:
                    for q in range(4):
                        y = x[:, q * P:(q + 1) * P]
                        ins = V.tensor_tensor(y, ps[q * DEC:(q + 1) * DEC, i, 0:P], y, ALU.add)
                ins.then_inc(S["comb_add"], 1)

            for b in range(NB):
                columns_with_gain(h3T, b, "x3t_mm", "h3_ready", T3_BANK, R_PLE)
                mean(2, b)
            for b in range(NB):
                invert(2, b)
            for q in range(4):
                ins = V.tensor_copy(rs4[q * DEC:(q + 1) * DEC, :], rstd[0:DEC, 2:3])
            ins.then_inc(S["rs4_ready"], 1)
            for b in range(NB):
                rows = slice(0, ROWS[b])
                for n in range(2):
                    cols = slice(n * 512, (n + 1) * 512)
                    dve.wait_ge(S["pg_sig"], 2 * b + n + 1)
                    link(V.tensor_tensor(sg[rows, b, cols], sg[rows, b, cols], ple3[rows, b, cols], ALU.mult))
                    V.tensor_tensor(X2[rows, b, cols], X2[rows, b, cols], sg[rows, b, cols], ALU.add
                                    ).then_inc(S["x4_ready"], 1)
                if b == 0:
                    dve.wait_ge(S["nfin_in"], 16)
                dve.wait_ge(S["x4_ready"], 2 * b + 2)
                V.tensor_tensor(sg[rows, b, :], X2[rows, b, :], nfin[rows, :], ALU.mult
                                ).then_inc(S["y_scaled"], 1)
                mean(3, b)
                if b == 0:
                    invert(3, 0)
                    dve.wait_ge(S["y_scaled"], 1)
                    V.tensor_scalar(sg[:, 0, :], sg[:, 0, :], rstd[:, 0:1], None, ALU.mult
                                    ).then_inc(S["y_ready0"], 1)
            for b in (1, 2):
                dve.wait_ge(S["nsqrt"], NB * 3 + b + 1)
                V.reciprocal(rstd[:, b:b + 1], rstd[:, b:b + 1]).then_inc(S["last_rstd"], 1)
            dve.wait_ge(S["last_rstd"], 2)
            dve.wait_ge(S["y_scaled"], 3)
            V.tensor_scalar(sg[0:DEC, 2, :], sg[0:DEC, 2, :], rstd[0:DEC, 2:3], None, ALU.mult
                            ).then_inc(S["y_ready2"], 1)


INS = ["x_prompt", "x_sample", "state_hgrn", "cache_conv", "p_prompt", "p_sample", "norm_mix", "w_in",
       "hgrn_lb_logits", "hgrn_norm", "conv_w", "conv_b", "conv_ln_g", "conv_ln_b", "w_out", "norm_ffn",
       "w_router", "b_router", "w_gate_up", "b_gate_up", "w_down", "b_down", "w_ple", "norm_ple",
       "w_ple_gate", "norm_final"]
OUTS = [(1, SEQ, D), (1, DEC, D), (1, 1, H, KD, KD), (1, 1, PAD, W), (1, 1, H, KD, KD), (1, 1, PAD, W)]


def kernel(**inputs):
    import concourse.bacc as bacc
    from concourse.bass_utils import run_bass_kernel_spmd

    nc = bacc.Bacc("TRN2", target_bir_lowering=False, num_devices=1)
    arrays, aps, outs = {}, {}, []
    given = {n: np.ascontiguousarray(inputs[n]) for n in INS}
    given["consts"] = constants()
    for name, x in given.items():
        arrays[f"in_{name}"] = x
        aps[name] = nc.dram_tensor(f"in_{name}", x.shape, mybir.dt.from_np(x.dtype), kind="ExternalInput").ap()
    for i, shape in enumerate(OUTS):
        outs.append(nc.dram_tensor(f"out_{i}", shape, F32, kind="ExternalOutput").ap())
    program(nc, aps, outs)
    r = run_bass_kernel_spmd(nc, [arrays], core_ids=[0])
    return tuple(r.results[0][f"out_{i}"] for i in range(len(OUTS)))
```
